# Optimizing a Trainium2 kernel written in Bass

```python
import math
import jax, jax.numpy as jnp
from jax import lax
import numpy as np

D_MODEL = 1024
BATCH = 1
SEQ = 256
DEPTH = 2

HEAD_DIM = 128
QBLOCK = 128
A_HEADS = 4
A_KV_RANK = 256
IDX_HEADS = 4
IDX_DIM = 64
DSA_TOPK = 256
B_HEADS = 4
CMP_LEN = 32
CMP_STRIDE = 16
SEL_BLOCK = 64
N_SEL = 8
WINDOW = 512
C_HEADS = 8
NUM_BUCKETS = 32
MAX_DISTANCE = 128
D_FF = 2816
N_EXPERTS = 8
TOP_K = 2
EXPERT_FF = 3584
RMS_EPS = 1e-6
NEG_BIG = -1e30

N_EVEN = (DEPTH + 1) // 2
N_ODD = DEPTH // 2
EVEN_SPLITS = (A_HEADS * HEAD_DIM, A_KV_RANK, IDX_HEADS * IDX_DIM, IDX_DIM, IDX_HEADS,
               B_HEADS * HEAD_DIM, 6 * HEAD_DIM, 3 * B_HEADS)
EVEN_IN = sum(EVEN_SPLITS)
MIX_EVEN = (A_HEADS + B_HEADS) * HEAD_DIM
MIX_ODD = C_HEADS * HEAD_DIM

kernel_name = 'hybrid_dsa_nsa_stickbreak_moe'

def rmsnorm(x, g):
    xf = x.astype(jnp.float32)
    y = xf * lax.rsqrt(jnp.mean(xf * xf, axis=-1, keepdims=True) + RMS_EPS)
    return (y * g.astype(jnp.float32)).astype(x.dtype)

def rel_bucket(dist):
    n = jnp.maximum(dist, 0)
    max_exact = NUM_BUCKETS // 2
    large = max_exact + (jnp.log(jnp.maximum(n, 1).astype(jnp.float32) / max_exact)
                         / math.log(MAX_DISTANCE / max_exact)
                         * (NUM_BUCKETS - max_exact)).astype(jnp.int32)
    large = jnp.minimum(large, NUM_BUCKETS - 1)
    return jnp.where(n < max_exact, n, large)

def masked_softmax(logits, mask):
    lf = jnp.where(mask, logits.astype(jnp.float32), NEG_BIG)
    return jnp.where(mask, jax.nn.softmax(lf, axis=-1), 0.0)

def to_blocks(a, nb):
    return jnp.moveaxis(a.reshape((a.shape[0], nb, QBLOCK) + a.shape[2:]), 1, 0)

def from_blocks(a):
    nb, b, qb = a.shape[:3]
    return jnp.moveaxis(a, 0, 1).reshape((b, nb * qb) + a.shape[3:])

def gather_rows(table, idx):
    return jax.vmap(lambda tb, ii: tb[ii])(table, idx)

def swiglu(h, wg, wu, wd):
    return (jax.nn.silu(h @ wg) * (h @ wu)) @ wd

def even_mixer(h, w_in, kv_norm, w_uk, w_uv, cmp_pos, cmp_w1, cmp_w2, w_out, rel_bias):
    b, s, _ = h.shape
    nb = s // QBLOCK
    offs = [int(o) for o in np.cumsum(EVEN_SPLITS)[:-1]]
    a_q, a_lat, i_q, i_k, i_w, b_q, b_kv, b_g = jnp.split(h @ w_in, offs, axis=-1)
    a_q = a_q.reshape(b, s, A_HEADS, HEAD_DIM)
    c_kv = rmsnorm(a_lat, kv_norm)
    a_k = c_kv @ w_uk
    a_v = c_kv @ w_uv
    i_q = i_q.reshape(b, s, IDX_HEADS, IDX_DIM)
    i_w = i_w * (IDX_HEADS ** -0.5)
    b_q = b_q.reshape(b, s, B_HEADS, HEAD_DIM)
    b_kv = b_kv.reshape(b, s, 6, HEAD_DIM)
    ck_raw, cv_raw, sk, sv, wk, wv = [b_kv[:, :, j] for j in range(6)]
    b_g = jax.nn.sigmoid(b_g.reshape(b, s, 3, B_HEADS))

    n_cmp = (s - CMP_LEN) // CMP_STRIDE + 1
    cmp_start = jnp.arange(n_cmp, dtype=jnp.int32) * CMP_STRIDE
    cmp_tok = cmp_start[:, None] + jnp.arange(CMP_LEN, dtype=jnp.int32)[None, :]
    cmp_end = cmp_start + CMP_LEN - 1

    def compress(kv, j):
        blk = kv[:, cmp_tok] + cmp_pos[j]
        hid = jax.nn.gelu(blk.reshape(b, n_cmp, CMP_LEN * HEAD_DIM) @ cmp_w1[j])
        return hid @ cmp_w2[j]

    ck = compress(ck_raw, 0)
    cv = compress(cv_raw, 1)

    n_sb = s // SEL_BLOCK
    n_sel = min(N_SEL, n_sb)
    sb_start = jnp.arange(n_sb, dtype=jnp.int32) * SEL_BLOCK
    overlap = ((cmp_start[:, None] < sb_start[None, :] + SEL_BLOCK)
               & (cmp_start[:, None] + CMP_LEN > sb_start[None, :])).astype(jnp.float32)
    sk_blocks = sk.reshape(b, n_sb, SEL_BLOCK, HEAD_DIM)
    sv_blocks = sv.reshape(b, n_sb, SEL_BLOCK, HEAD_DIM)
    blk_ids = jnp.arange(n_sb, dtype=jnp.int32)
    sel_off = jnp.arange(SEL_BLOCK, dtype=jnp.int32)

    pad = jnp.zeros((b, WINDOW, HEAD_DIM), wk.dtype)
    wk_pad = jnp.concatenate([pad, wk], axis=1)
    wv_pad = jnp.concatenate([pad, wv], axis=1)
    win_off = jnp.arange(WINDOW + QBLOCK, dtype=jnp.int32)

    k_dsa = min(DSA_TOPK, s // 4)
    key_pos = jnp.arange(s, dtype=jnp.int32)
    bias_a = rel_bias[:, :A_HEADS]
    bias_b = rel_bias[:, A_HEADS:]
    scale = HEAD_DIM ** -0.5
    idx_scale = IDX_DIM ** -0.5

    def block_fn(args):
        qi, qa, iq, iw, qb, g = args
        t = qi * QBLOCK + jnp.arange(QBLOCK, dtype=jnp.int32)
        isc = jax.nn.relu(jnp.einsum('bqhd,bsd->bqhs', iq, i_k) * idx_scale)
        isc = jnp.einsum('bqhs,bqh->bqs', isc, iw).astype(jnp.float32)
        isc = jnp.where(key_pos[None, None, :] <= t[None, :, None], isc, -jnp.inf)
        _, sel_a = lax.top_k(isc, k_dsa)
        ka = gather_rows(a_k, sel_a)
        va = gather_rows(a_v, sel_a)
        la = (jnp.einsum('bqhd,bqkd->bhqk', qa, ka) * scale
              + jnp.moveaxis(bias_a[rel_bucket(t[None, :, None] - sel_a)], -1, 1))
        pa = masked_softmax(la, (sel_a <= t[None, :, None])[:, None])
        oa = jnp.einsum('bhqk,bqkd->bqhd', pa, va)
        lc = (jnp.einsum('bqhd,bnd->bhqn', qb, ck) * scale
              + jnp.moveaxis(bias_b[rel_bucket(t[:, None] - cmp_end[None, :])], -1, 0))
        pc = masked_softmax(lc, (cmp_end[None, :] <= t[:, None])[None, None])
        oc = jnp.einsum('bhqn,bnd->bqhd', pc, cv)
        imp = jnp.einsum('bhqn,nm->bqm', pc, overlap)
        cur = t // SEL_BLOCK
        forced = ((blk_ids[None, :] == 0) | (blk_ids[None, :] == cur[:, None])
                  | (blk_ids[None, :] == cur[:, None] - 1))
        imp = jnp.where(forced[None], jnp.inf,
                        jnp.where(blk_ids[None, None, :] > cur[None, :, None], -jnp.inf, imp))
        _, sel_b = lax.top_k(imp, n_sel)
        ks = gather_rows(sk_blocks, sel_b).reshape(b, QBLOCK, n_sel * SEL_BLOCK, HEAD_DIM)
        vs = gather_rows(sv_blocks, sel_b).reshape(b, QBLOCK, n_sel * SEL_BLOCK, HEAD_DIM)
        tok = (sel_b[..., None] * SEL_BLOCK + sel_off).reshape(b, QBLOCK, n_sel * SEL_BLOCK)
        ls = (jnp.einsum('bqhd,bqkd->bhqk', qb, ks) * scale
              + jnp.moveaxis(bias_b[rel_bucket(t[None, :, None] - tok)], -1, 1))
        ps = masked_softmax(ls, (tok <= t[None, :, None])[:, None])
        osel = jnp.einsum('bhqk,bqkd->bqhd', ps, vs)
        kw = lax.dynamic_slice_in_dim(wk_pad, qi * QBLOCK, WINDOW + QBLOCK, axis=1)
        vw = lax.dynamic_slice_in_dim(wv_pad, qi * QBLOCK, WINDOW + QBLOCK, axis=1)
        wpos = qi * QBLOCK - WINDOW + win_off
        dist = t[:, None] - wpos[None, :]
        lw = (jnp.einsum('bqhd,bkd->bhqk', qb, kw) * scale
              + jnp.moveaxis(bias_b[rel_bucket(dist)], -1, 0))
        pw = masked_softmax(lw, ((wpos[None, :] >= 0) & (dist >= 0) & (dist < WINDOW))[None, None])
        ow = jnp.einsum('bhqk,bkd->bqhd', pw, vw)
        ob = (g[:, :, 0, :, None] * oc + g[:, :, 1, :, None] * osel
              + g[:, :, 2, :, None] * ow)
        o = jnp.concatenate([oa, ob], axis=2).reshape(b, QBLOCK, MIX_EVEN)
        return o.astype(h.dtype)

    xs = (jnp.arange(nb, dtype=jnp.int32), to_blocks(a_q, nb), to_blocks(i_q, nb),
          to_blocks(i_w, nb), to_blocks(b_q, nb), to_blocks(b_g, nb))
    o = from_blocks(lax.map(block_fn, xs))
    return o @ w_out

def odd_mixer(h, w_qkv, w_out):
    b, s, _ = h.shape
    nb = s // QBLOCK
    q, k, v = jnp.split(h @ w_qkv, 3, axis=-1)
    q = q.reshape(b, s, C_HEADS, HEAD_DIM)
    k = k.reshape(b, s, C_HEADS, HEAD_DIM)
    v = v.reshape(b, s, C_HEADS, HEAD_DIM)
    key_pos = jnp.arange(s, dtype=jnp.int32)
    scale = HEAD_DIM ** -0.5

    def block_fn(args):
        qi, qb = args
        t = qi * QBLOCK + jnp.arange(QBLOCK, dtype=jnp.int32)
        z = jnp.einsum('bqhd,bshd->bhqs', qb, k).astype(jnp.float32) * scale
        strict = key_pos[None, :] < t[:, None]
        log_1m = jnp.where(strict, jax.nn.log_sigmoid(-z), 0.0)
        after = lax.cumsum(log_1m, axis=3, reverse=True) - log_1m
        a = jnp.where(strict, jnp.exp(jax.nn.log_sigmoid(z) + after), 0.0)
        o = jnp.einsum('bhqs,bshd->bqhd', a, v)
        return o.reshape(b, QBLOCK, MIX_ODD).astype(h.dtype)

    o = from_blocks(lax.map(block_fn, (jnp.arange(nb, dtype=jnp.int32), to_blocks(q, nb))))
    return o @ w_out

def moe_swiglu(h, w_router, w_gate, w_up, w_down):
    logits = (h @ w_router).astype(jnp.float32)
    top_v, top_i = lax.top_k(logits, TOP_K)
    top_w = jax.nn.softmax(top_v, axis=-1)
    gates = jnp.sum(jax.nn.one_hot(top_i, N_EXPERTS, dtype=jnp.float32) * top_w[..., None], axis=-2)
    gates = gates.astype(h.dtype)
    y = jnp.zeros_like(h)
    for e in range(N_EXPERTS):
        y = y + gates[..., e:e + 1] * swiglu(h, w_gate[e], w_up[e], w_down[e])
    return y

def setup_inputs(seed: int = 0) -> dict:
    key = jax.random.key(seed)
    ks = jax.random.split(key, 32)
    f32 = jnp.float32

    def nrm(k, shape, scale):
        return jax.random.normal(k, shape, f32) * scale

    def gain(k, shape):
        return 1.0 + 0.02 * jax.random.normal(k, shape, f32)

    hd = HEAD_DIM
    return {
        'x': nrm(ks[0], (BATCH, SEQ, D_MODEL), 1.0),
        'rel_bias': nrm(ks[1], (NUM_BUCKETS, A_HEADS + B_HEADS), 0.2),
        'ev_norm_mix': gain(ks[2], (N_EVEN, D_MODEL)),
        'ev_w_in': nrm(ks[3], (N_EVEN, D_MODEL, EVEN_IN), D_MODEL ** -0.5),
        'ev_kv_norm': gain(ks[4], (N_EVEN, A_KV_RANK)),
        'ev_w_uk': nrm(ks[5], (N_EVEN, A_KV_RANK, hd), A_KV_RANK ** -0.5),
        'ev_w_uv': nrm(ks[6], (N_EVEN, A_KV_RANK, hd), A_KV_RANK ** -0.5),
        'ev_cmp_pos': nrm(ks[7], (N_EVEN, 2, CMP_LEN, hd), 0.02),
        'ev_cmp_w1': nrm(ks[8], (N_EVEN, 2, CMP_LEN * hd, hd), (CMP_LEN * hd) ** -0.5),
        'ev_cmp_w2': nrm(ks[9], (N_EVEN, 2, hd, hd), hd ** -0.5),
        'ev_w_out': nrm(ks[10], (N_EVEN, MIX_EVEN, D_MODEL), MIX_EVEN ** -0.5),
        'ev_norm_ffn': gain(ks[11], (N_EVEN, D_MODEL)),
        'ev_w_gate': nrm(ks[12], (N_EVEN, D_MODEL, D_FF), D_MODEL ** -0.5),
        'ev_w_up': nrm(ks[13], (N_EVEN, D_MODEL, D_FF), D_MODEL ** -0.5),
        'ev_w_down': nrm(ks[14], (N_EVEN, D_FF, D_MODEL), D_FF ** -0.5),
        'od_norm_mix': gain(ks[15], (N_ODD, D_MODEL)),
        'od_w_qkv': nrm(ks[16], (N_ODD, D_MODEL, 3 * MIX_ODD), D_MODEL ** -0.5),
        'od_w_out': nrm(ks[17], (N_ODD, MIX_ODD, D_MODEL), MIX_ODD ** -0.5),
        'od_norm_ffn': gain(ks[18], (N_ODD, D_MODEL)),
        'od_w_router': nrm(ks[19], (N_ODD, D_MODEL, N_EXPERTS), D_MODEL ** -0.5),
        'od_w_gate': nrm(ks[20], (N_ODD, N_EXPERTS, D_MODEL, EXPERT_FF), D_MODEL ** -0.5),
        'od_w_up': nrm(ks[21], (N_ODD, N_EXPERTS, D_MODEL, EXPERT_FF), D_MODEL ** -0.5),
        'od_w_down': nrm(ks[22], (N_ODD, N_EXPERTS, EXPERT_FF, D_MODEL), EXPERT_FF ** -0.5),
        'final_norm': gain(ks[23], (D_MODEL,)),
    }

def reference(x, rel_bias, ev_norm_mix, ev_w_in, ev_kv_norm, ev_w_uk, ev_w_uv, ev_cmp_pos,
              ev_cmp_w1, ev_cmp_w2, ev_w_out, ev_norm_ffn, ev_w_gate, ev_w_up, ev_w_down,
              od_norm_mix, od_w_qkv, od_w_out, od_norm_ffn, od_w_router, od_w_gate, od_w_up,
              od_w_down, final_norm):
    for layer in range(DEPTH):
        i = layer // 2
        if layer % 2 == 0:
            x = x + even_mixer(rmsnorm(x, ev_norm_mix[i]), ev_w_in[i], ev_kv_norm[i], ev_w_uk[i],
                               ev_w_uv[i], ev_cmp_pos[i], ev_cmp_w1[i], ev_cmp_w2[i], ev_w_out[i],
                               rel_bias)
            x = x + swiglu(rmsnorm(x, ev_norm_ffn[i]), ev_w_gate[i], ev_w_up[i], ev_w_down[i])
        else:
            x = x + odd_mixer(rmsnorm(x, od_norm_mix[i]), od_w_qkv[i], od_w_out[i])
            x = x + moe_swiglu(rmsnorm(x, od_norm_ffn[i]), od_w_router[i], od_w_gate[i],
                               od_w_up[i], od_w_down[i])
    return rmsnorm(x, final_norm)


_drawn_inputs = setup_inputs


def setup_inputs(seed=0):
    import zlib

    import numpy as np

    out = dict(_drawn_inputs(seed))
    spreads = {}
    factors = {'ev_kv_norm': 8.0,
     'ev_cmp_pos': 4.459,
     'od_norm_ffn': 2.718,
     'final_norm': 8.401,
     'od_norm_mix': 3.641}
    for name, (base, spread) in spreads.items():
        noise = np.random.default_rng([zlib.crc32(name.encode()), seed]).standard_normal(out[name].shape)
        drawn = base * np.exp(spread * noise) if base else spread * noise
        out[name] = __import__('jax').numpy.asarray(drawn.astype(out[name].dtype))
    for name, factor in factors.items():
        out[name] = (out[name] * factor).astype(out[name].dtype)
    return out
```

```python
from contextlib import ExitStack

import numpy as np

import concourse.bass as bass
from concourse import mybir

F32 = mybir.dt.float32
F32R = mybir.dt.float32r
ALU = mybir.AluOpType
ACT = mybir.ActivationFunctionType
AX = mybir.AxisListType

P = 128
SEQ = 256
D = 1024
KD = D // P
T = SEQ // P
HD = 128
AH = BH = 4
CH = 8
RANK = 256
IDX_DIM = 64
NB = 32
MAX_DIST = 128
CMP_LEN, CMP_STRIDE = 32, 16
NCMP = (SEQ - CMP_LEN) // CMP_STRIDE + 1
NCP = NCMP + 1
TOPK = min(256, SEQ // 4)
FF = 2816
EFF = 3584
NE = 8
EPS = 1e-6
NEG = -1e30
UNSEEN = -1e38
TAKEN = -3e38
SCALE = HD ** -0.5
W = 512

O_AQ = 0
O_LAT = O_AQ + AH * HD
O_IQ = O_LAT + RANK
O_IK = O_IQ + 4 * IDX_DIM
O_IW = O_IK + IDX_DIM
O_BQ = O_IW + 4
O_KV = O_BQ + BH * HD
O_BG = O_KV + 6 * HD

UNIT = 2048
R = 6
H = 3

FFN_CHUNKS = [(f, min(W, FF - f)) for f in range(0, FF, W)]
MOE_CHUNKS = [(f, min(W, EFF - f)) for f in range(0, EFF, W)]


def bucket_rows():
    dist = np.arange(SEQ)
    half = NB // 2
    large = half + (np.log(np.maximum(dist, 1).astype(np.float32) / half)
                    / np.float32(np.log(MAX_DIST / half)) * (NB - half)).astype(np.int32)
    bucket = np.where(dist < half, dist, np.minimum(large, NB - 1))
    rows = np.zeros((NB, SEQ + P), np.float32)
    rows[bucket[::-1], np.arange(SEQ)] = 1.0
    return rows


def chunk_units(chunks):
    return [(2, 2) if w == W else (1, 1) for _, w in chunks]


def ffn_order(chunks):
    order = []
    cu = chunk_units(chunks)
    for c in range(len(chunks) + 1):
        if c < len(chunks):
            order += [("gate", c, q) for q in range(cu[c][0])] + [("up", c, q) for q in range(cu[c][0])]
        if c:
            order += [("down", c - 1, q) for q in range(cu[c - 1][1])]
    return order


def bounds(chunks):
    cu, n, out = chunk_units(chunks), 0, []
    for c in range(len(chunks)):
        g = n + cu[c][0]
        u = g + cu[c][0]
        n = u + (cu[c - 1][1] if c else 0)
        out.append((g, u, n))
    return out


def at(const, e=None, per=0):
    return const if e is None else e * per + const


def build(nc, x_d, rel_bias, ev_norm_mix, ev_w_in, ev_kv_norm, ev_w_uk, ev_w_uv, ev_cmp_pos, ev_cmp_w1,
          ev_cmp_w2, ev_w_out, ev_norm_ffn, ev_w_gate, ev_w_up, ev_w_down, od_norm_mix, od_w_qkv, od_w_out,
          od_norm_ffn, od_w_router, od_w_gate, od_w_up, od_w_down, final_norm, out_d):
    win = ev_w_in[0].rearrange("(p k) n -> p k n", k=KD)

    def k_units(view, parts, width):
        return [([(view[:, 4 * q:4 * q + 4, s:s + n], d, n) for s, d, n in parts], 4, width) for q in range(2)]

    units = []
    units += k_units(win, [(O_IQ, 0, 320), (O_IK, 320, 64), (O_IW, 384, 4), (O_BG, 388, 12)], 400)
    units += k_units(win, [(O_AQ, 0, W)], W)
    units += k_units(win, [(O_LAT, 0, RANK), (O_KV + 3 * HD, 256, HD), (O_KV + 5 * HD, 384, HD)], W)
    units += k_units(win, [(O_BQ, 0, W)], W)
    units += k_units(win, [(O_KV, 0, 3 * HD), (O_KV + 4 * HD, 3 * HD, HD)], W)
    U_CMP = len(units)
    for j in range(2):
        w1 = ev_cmp_w1[0, j].rearrange("(l p) n -> p l n", p=P)
        units += [([(w1[:, 16 * q:16 * q + 16], 0, HD)], 16, HD) for q in range(2)]
    U_WO = [0, 0]
    U_WO[0] = len(units)

    def out_units(w):
        v = w.rearrange("(h p) n -> p h n", p=P)
        return [u for n in range(2) for u in k_units(v, [(W * n, 0, W)], W)]

    units += out_units(ev_w_out[0])
    U_FFN = len(units)
    gate_v, up_v = (w[0].rearrange("(p k) f -> p k f", k=KD) for w in (ev_w_gate, ev_w_up))
    for kind, c, q in ffn_order(FFN_CHUNKS):
        f, w = FFN_CHUNKS[c]
        if kind == "down":
            v = ev_w_down[0, f:f + w].rearrange("(p j) n -> p j n", j=w // P)
            units.append(([(v[:, 2 * q:2 * q + 2], 0, D)], 2, D))
        else:
            v = gate_v if kind == "gate" else up_v
            ks = slice(4 * q, 4 * q + 4) if w == W else slice(0, KD)
            units.append(([(v[:, ks, f:f + w], 0, w)], UNIT // w, w))
    U_QKV = len(units)
    qkv_v = od_w_qkv[0].rearrange("(p k) n -> p k n", k=KD)
    for g in range(3 * D // W):
        units += k_units(qkv_v, [(W * g, 0, W)], W)
    U_WO[1] = len(units)
    units += out_units(od_w_out[0])
    U_MOE = len(units)
    moe_order = ffn_order(MOE_CHUNKS)
    PER = len(moe_order)
    assert PER % R == 0 and PER % H == 0
    moe_gate, moe_up = (w.rearrange("o e (p k) f -> (o e) p k f", k=KD) for w in (od_w_gate, od_w_up))
    moe_down = od_w_down.rearrange("o e (c p j) n -> (o e) c p j n", p=P, j=W // P)

    landed_at = []
    slot_total = [0] * R
    for n, (pieces, _, _) in enumerate(units):
        slot_total[n % R] += 16 * len(pieces)
        landed_at.append(slot_total[n % R])

    def landed(n):
        if n < U_MOE:
            return landed_at[n]
        return slot_total[n % R] + 16 * len([m for m in range(U_MOE, n + 1) if m % R == n % R])

    def shape_of(n):
        if n < U_MOE:
            return units[n][1:]
        return (2, D) if moe_order[(n - U_MOE) % PER][0] == "down" else (4, W)

    buckets_d = nc.inline_tensor(bucket_rows(), "bucket_rows").ap()
    diag_d = nc.dram_tensor("bias_by_distance", [CH, SEQ + P], F32).ap()

    with ExitStack() as ctx:
        def sb(name, shape, dt=F32):
            return ctx.enter_context(nc.sbuf_tensor(name, shape, dt))

        def sem(name):
            return ctx.enter_context(nc.semaphore(name))

        raw = sb("raw", [P, R, UNIT])
        hi = sb("hi", [P, H, UNIT], F32R)
        lo = sb("lo", [P, H, UNIT], F32R)
        x = sb("x", [P, T, D])
        work = sb("work", [P, 4, D])
        probT = sb("probT", [P, T, 4, P])
        xT_hi = sb("xT_hi", [P, KD, SEQ], F32R)
        xT_lo = sb("xT_lo", [P, KD, SEQ], F32R)
        gain = sb("gain", [P, 2, D])
        qT = sb("qT", [P, 8, SEQ])
        bias_kT = sb("bias_kT", [P, 8, SEQ])
        kv = sb("kv", [P, 9 * SEQ])
        tok = sb("tok", [P, T, W])
        latT = sb("latT", [P, T, SEQ])
        hT_hi = sb("hT_hi", [P, 4, SEQ], F32R)
        hT_lo = sb("hT_lo", [P, 4, SEQ], F32R)
        iscore = sb("iscore", [P, T, SEQ])
        ident = sb("ident", [P, P])
        flip = sb("flip", [P, P])
        bucket_sb = sb("bucket_sb", [NB, SEQ + P])
        rel_sb = sb("rel_sb", [NB, CH])
        diag_sb = sb("diag_sb", [CH, SEQ + P])
        wuk = sb("wuk", [P, 2, HD])
        wuv = sb("wuv", [P, 2, HD])
        w2 = sb("w2", [P, 2, HD])
        pos_sb = sb("pos_sb", [CMP_LEN, 2, HD])
        posT = sb("posT", [P, 2, CMP_LEN])
        kv_gain = sb("kv_gain", [P, RANK])
        wr = sb("wr", [P, KD, NE])
        wr_hi = sb("wr_hi", [P, KD, NE], F32R)
        wr_lo = sb("wr_lo", [P, KD, NE], F32R)
        small = sb("small", [P, T, 16])
        gates = sb("gates", [P, T, 12])
        stat = sb("stat", [P, 8])
        hid = sb("hid", [P, 2, NCP])
        hid2 = sb("hid2", [P, 2, NCP])
        hid3 = sb("hid3", [P, 2, NCP])
        ckT = sb("ckT", [P, NCP])
        cv = sb("cv", [NCP, HD])
        negmax = sb("negmax", [P, 2, 4])
        expsum = sb("expsum", [P, 2, 4])
        inv = sb("inv", [P, 2, 4])
        top8 = sb("top8", [P, 8])
        rlog = sb("rlog", [P, T, 16])
        rsel = sb("rsel", [P, T, 16])
        rexp = sb("rexp", [P, T, NE])
        rtop = sb("rtop", [P, T, 8])
        rneg = sb("rneg", [P, T])
        rsum = sb("rsum", [P, T])
        rgate = sb("rgate", [P, T, NE])
        ones = sb("ones", [P, SEQ])
        ps = ctx.enter_context(nc.psum_tensor("ps", [P, 8, W], F32))

        iqT = kv[:, 0:2 * SEQ].rearrange("p (b s) -> p b s", b=2)
        ikT = kv[:, 2 * SEQ:3 * SEQ]
        akT = kv[:, 3 * SEQ:4 * SEQ]
        skT = kv[:, 4 * SEQ:5 * SEQ]
        wkT = kv[:, 5 * SEQ:6 * SEQ]
        av = kv[:, 6 * SEQ:7 * SEQ].rearrange("p (t d) -> p t d", t=T)
        rawT = kv[:, 7 * SEQ:9 * SEQ].rearrange("p (j s) -> p j s", j=2)
        v1 = kv[:, 0:T * D].rearrange("p (t d) -> p t d", t=T)
        blk_hi, blk_lo = (h[:].rearrange("p j s -> p (j s)").rearrange("p (j l n) -> p j l n", j=2, n=NCP)
                          for h in (hT_hi, hT_lo))
        topw = work[:, 3, 0:SEQ]
        hankel = work[:, 2:4, :].rearrange("p a (b s) -> p (a b) s", s=SEQ)

        raw_landed = [sem(f"raw_landed{i}") for i in range(R)]
        hi_ready = sem("hi_ready")
        lo_ready = sem("lo_ready")
        units_used = sem("units_used")
        x_loaded = sem("x_loaded")
        gain_loaded = [sem(f"gain_loaded{i}") for i in range(5)]
        small_loaded = sem("small_loaded")
        ident_ready = sem("ident_ready")
        flip_ready = sem("flip_ready")
        var_ready = sem("var_ready")
        std_ready = sem("std_ready")
        xs_ready = sem("xs_ready")
        xT_done = sem("xT_done")
        xT_hi_ready = sem("xT_hi_ready")
        xT_ready = sem("xT_ready")
        diag_done = sem("diag_done")
        diag_copied = sem("diag_copied")
        diag_stored = sem("diag_stored")
        hankel_loaded = sem("hankel_loaded")
        bias_flipped = sem("bias_flipped")
        bias_copied = sem("bias_copied")
        bias_masked = sem("bias_masked")
        proj_copied = sem("proj_copied")
        small_copied = sem("small_copied")
        gates_ready = sem("gates_ready")
        gates_masked = sem("gates_masked")
        lat_ready = sem("lat_ready")
        latT_done = sem("latT_done")
        latT_copied = sem("latT_copied")
        akv_done = sem("akv_done")
        akv_copied = sem("akv_copied")
        idx_done = sem("idx_done")
        idx_relu = sem("idx_relu")
        idx_summed = sem("idx_summed")
        idx_masked = sem("idx_masked")
        pos_done = sem("pos_done")
        blk_made = sem("blk_made")
        blk_hi_ready = sem("blk_hi_ready")
        blk_ready = sem("blk_ready")
        gelu_arg = sem("gelu_arg")
        gelu_exp = sem("gelu_exp")
        hid_ready = sem("hid_ready")
        ckv_done = sem("ckv_done")
        ckv_copied = sem("ckv_copied")
        scores_done = sem("scores_done")
        logits_ready = sem("logits_ready")
        exps_done = sem("exps_done")
        probs_ready = sem("probs_ready")
        probT_done = sem("probT_done")
        probT_copied = sem("probT_copied")
        pv_done = sem("pv_done")
        oT_hi_ready = sem("oT_hi_ready")
        oT_ready = sem("oT_ready")
        x_added = sem("x_added")
        silu_done = sem("silu_done")
        h_done = sem("h_done")
        hT_done = sem("hT_done")
        hT_hi_ready = sem("hT_hi_ready")
        hT_ready = sem("hT_ready")
        z_done = sem("z_done")
        log_done = sem("log_done")
        soft_done = sem("soft_done")
        soft_masked = sem("soft_masked")
        stick_arg = sem("stick_arg")
        stick_exp = sem("stick_exp")
        stick_masked = sem("stick_masked")
        wr_hi_ready = sem("wr_hi_ready")
        wr_ready = sem("wr_ready")
        logit_done = sem("logit_done")
        router_max = sem("router_max")
        router_exp = sem("router_exp")
        y_added = sem("y_added")
        dve_chain = sem("dve_chain")
        act_chain = sem("act_chain")
        out_ready = sem("out_ready")
        out_stored = sem("out_stored")

        block = ctx.enter_context(nc.Block())

        BATCH = [("dsa", 0), ("dsa", 1), ("sel", 0), ("win", 0), ("cmp", 0), ("sel", 1), ("win", 1), ("cmp", 1)]
        GROUP = [0, 1, 2, 2, 2, 3, 3, 3]
        NBATCH = len(BATCH)

        def keys(b):
            kind, t = BATCH[b]
            return P * (t + 1) if kind != "cmp" else (NCMP - CMP_STRIDE // 2 if t == 0 else NCMP)

        def key_bias(b):
            kind, t = BATCH[b]
            heads = slice(0, AH) if kind == "dsa" else slice(AH, AH + BH)
            if kind == "cmp":
                first = P * (1 - t) + CMP_LEN - 1
                return bias_kT[:, heads, first:first + CMP_STRIDE * (keys(b) - 1) + 1:CMP_STRIDE]
            return bias_kT[:, heads, P * (1 - t):P * (1 - t) + keys(b)]

        def logit_tile(b, n):
            return work[:, b % 2, :].rearrange("p (h s) -> p h s", h=4)[:, :, 0:n]

        def prob_tile(b, n):
            return work[:, 2 + b % 2, :].rearrange("p (h s) -> p h s", h=4)[:, :, 0:n]

        def score_psum(first, n):
            return ps[:, first:first + 2, :].rearrange("p a (h s) -> p (a h) s", s=SEQ)[:, :, 0:n]

        STICK = [(1, 0), (1, 1), (0, 0), (0, 1)]
        NSTICK = len(STICK)

        def unit(ring, n):
            a, b = shape_of(n)
            return ring[:, n % (R if ring is raw else H), 0:a * b]

        def unit3(ring, n):
            a, b = shape_of(n)
            return unit(ring, n).rearrange("p (a b) -> p a b", a=a)

        @block.sync
        def _(sp):
            for n, (pieces, a, b) in enumerate(units):
                if n >= R:
                    sp.wait_ge(lo_ready, n - R + 1)
                for src, d, cnt in pieces:
                    sp.dma_start(unit3(raw, n)[:, :, d:d + cnt], src).then_inc(raw_landed[n % R], 16)
            with sp.Fori(0, NE) as e:
                for i, (kind, c, q) in enumerate(moe_order):
                    n = U_MOE + i
                    sp.wait_ge(lo_ready, at(n - R + 1, e, PER))
                    if kind == "down":
                        src = moe_down[bass.ds(e, 1), c, :, 2 * q:2 * q + 2, :].rearrange("e p j n -> (e p) j n")
                    else:
                        view = moe_gate if kind == "gate" else moe_up
                        src = view[bass.ds(e, 1), :, 4 * q:4 * q + 4, W * c:W * c + W].rearrange(
                            "e p k f -> (e p) k f")
                    sp.dma_start(unit3(raw, n), src).then_inc(raw_landed[n % R], 16)
            sp.wait_ge(out_ready, T)
            sp.dma_start(out_d[0].rearrange("(t p) d -> p t d", p=P), work[:, 0:T, :]).then_inc(out_stored, 16)
            sp.wait_ge(out_stored, 16)

        gains = [ev_norm_mix[0], ev_norm_ffn[0], od_norm_mix[0], od_norm_ffn[0], final_norm]

        def row_to_all(row):
            return bass.AP(tensor=row.tensor, offset=row.offset, ap=[[0, P], [1, row.shape[0]]])

        @block.gpsimd
        def _(pool):
            pool.memset(ident[:], 0.0).then_inc(ident_ready, 1)
            pool.memset(flip[:], 0.0).then_inc(flip_ready, 1)
            pool.wait_ge(ident_ready, 1)
            pool.affine_select(out=ident[:], in_=ident[:], compare_op=ALU.not_equal, fill=1.0, base=0,
                               pattern=[[-1, P]], channel_multiplier=1).then_inc(ident_ready, 1)
            pool.wait_ge(flip_ready, 1)
            pool.affine_select(out=flip[:], in_=flip[:], compare_op=ALU.not_equal, fill=1.0, base=-(P - 1),
                               pattern=[[1, P]], channel_multiplier=1).then_inc(flip_ready, 1)
            pool.wait_ge(diag_copied, 1)
            pool.dma_start(diag_d, diag_sb[:]).then_inc(diag_stored, 16)
            pool.wait_ge(diag_stored, 16)
            pool.dma_start(hankel, bass.AP(tensor=diag_d.tensor, offset=diag_d.offset,
                                           ap=[[1, P], [SEQ + P, CH], [1, SEQ]])).then_inc(hankel_loaded, 16)
            pool.wait_ge(bias_copied, 4)
            pool.affine_select(out=bias_kT[:], in_=bias_kT[:], compare_op=ALU.is_ge, fill=NEG, base=P,
                               pattern=[[0, 8], [-1, SEQ]], channel_multiplier=1).then_inc(bias_masked, 1)
            pool.wait_ge(gates_ready, 1)
            pool.affine_select(out=gates[:, 0, 0:BH], in_=gates[:, 0, 0:BH], compare_op=ALU.is_ge, fill=0.0,
                               base=-(CMP_LEN - 1), pattern=[[0, BH]], channel_multiplier=1)\
                .then_inc(gates_masked, 1)
            for i, t in enumerate((1, 0)):
                pool.wait_ge(idx_summed, i + 1)
                n = P * (t + 1)
                pool.affine_select(out=iscore[:, t, 0:n], in_=iscore[:, t, 0:n], compare_op=ALU.is_ge, fill=UNSEEN,
                                   base=P * t, pattern=[[-1, n]], channel_multiplier=1).then_inc(idx_masked, 1)
            pool.wait_ge(xs_ready, 2)
            pool.dma_start(gain[:, 0, :], row_to_all(gains[2])).then_inc(gain_loaded[2], 16)
            pool.wait_ge(xs_ready, 4)
            pool.dma_start(gain[:, 1, :], row_to_all(gains[3])).then_inc(gain_loaded[3], 16)
            pool.wait_ge(xs_ready, 6)
            pool.dma_start(gain[:, 0, :], row_to_all(gains[4])).then_inc(gain_loaded[4], 16)
            for b in range(NSTICK + 1):
                if b < NSTICK:
                    t, _ = STICK[b]
                    n = P * (t + 1)
                    pool.wait_ge(soft_done, b + 1)
                    lt = logit_tile(b, n)
                    pool.affine_select(out=lt, in_=lt, compare_op=ALU.is_gt, fill=0.0, base=P * t,
                                       pattern=[[0, 4], [-1, n]], channel_multiplier=1).then_inc(soft_masked, 1)
                if b:
                    t, _ = STICK[b - 1]
                    n = P * (t + 1)
                    pool.wait_ge(stick_exp, b)
                    pt = prob_tile(b - 1, n)
                    pool.affine_select(out=pt, in_=pt, compare_op=ALU.is_gt, fill=0.0, base=P * t,
                                       pattern=[[0, 4], [-1, n]], channel_multiplier=1).then_inc(stick_masked, 1)

        @block.scalar
        def _(act):
            chain = [0]

            def link(ins):
                chain[0] += 1
                ins.then_inc(act_chain, 1)
                act.wait_ge(act_chain, chain[0])

            act.dma_start(x[:], x_d[0].rearrange("(t p) d -> p t d", p=P)).then_inc(x_loaded, 16)
            act.dma_start(rel_sb[:], rel_bias).then_inc(small_loaded, 16)
            act.dma_start(bucket_sb[:], buckets_d).then_inc(small_loaded, 16)
            act.dma_start(pos_sb[:], ev_cmp_pos[0].rearrange("j l d -> l j d")).then_inc(small_loaded, 16)
            act.dma_start(wuk[:], ev_w_uk[0].rearrange("(p k) d -> p k d", k=2)).then_inc(small_loaded, 16)
            act.dma_start(wuv[:], ev_w_uv[0].rearrange("(p k) d -> p k d", k=2)).then_inc(small_loaded, 16)
            act.dma_start(w2[:], ev_cmp_w2[0].rearrange("j p d -> p j d")).then_inc(small_loaded, 16)
            act.dma_start(kv_gain[:], row_to_all(ev_kv_norm[0])).then_inc(small_loaded, 16)
            act.dma_start(wr[:], od_w_router[0].rearrange("(p k) e -> p k e", k=KD)).then_inc(small_loaded, 16)
            act.dma_start(gain[:, 0, :], row_to_all(gains[0])).then_inc(gain_loaded[0], 16)
            act.dma_start(gain[:, 1, :], row_to_all(gains[1])).then_inc(gain_loaded[1], 16)

            done = [0]

            def split(n, e=None):
                act.wait_ge(raw_landed[n % R], at(landed(n), e, 16 * PER // R))
                if n >= H:
                    act.wait_ge(units_used, at(n - H + 1, e, PER))
                act.activation(unit(hi, n), unit(raw, n), ACT.Copy).then_inc(hi_ready, 1)

            def splits_to(n):
                while done[0] < n:
                    split(done[0])
                    done[0] += 1

            def norm(i):
                act.wait_ge(var_ready, i + 1)
                act.activation(stat[:, 2:4], stat[:, 0:2], ACT.Sqrt).then_inc(std_ready, 1)
                if i < 4:
                    for b in range(4):
                        act.wait_ge(xT_done, 4 * i + b + 1)
                        act.activation(xT_hi[:, 2 * b:2 * b + 2, :],
                                       ps[:, b, :].rearrange("p (k s) -> p k s", k=2), ACT.Copy)\
                            .then_inc(xT_hi_ready, 1)

            act.wait_ge(diag_done, 1)
            act.activation(diag_sb[:], ps[0:CH, 7, 0:SEQ + P], ACT.Copy).then_inc(diag_copied, 1)
            splits_to(H)
            norm(0)

            def projected(g, n):
                splits_to(n + 2)
                act.wait_ge(units_used, n)

            projected(0, 2)
            act.activation(iqT, score_psum(0, SEQ)[:, 0:2, :], ACT.Copy).then_inc(proj_copied, 1)
            act.activation(ikT, ps[:, 1, 0:SEQ], ACT.Copy).then_inc(proj_copied, 1)
            projected(1, 4)
            act.activation(qT[:, 0:4, :], score_psum(2, SEQ), ACT.Copy).then_inc(proj_copied, 1)
            for a in range(4):
                act.wait_ge(bias_flipped, a + 1)
                act.activation(bias_kT[:, 2 * a:2 * a + 2, :], ps[:, 4 + a, :].rearrange("p (h s) -> p h s", h=2),
                               ACT.Copy).then_inc(bias_copied, 1)
            projected(2, 6)
            act.activation(tok[:], ps[:, 4:6, :], ACT.Copy).then_inc(proj_copied, 1)
            for i, t in enumerate((1, 0)):
                n = P * (t + 1)
                act.wait_ge(idx_done, i + 1)
                if i:
                    act.wait_ge(idx_summed, i)
                act.activation(logit_tile(0, n), score_psum(6, n), ACT.Relu, scale=IDX_DIM ** -0.5)\
                    .then_inc(idx_relu, 1)
            act.wait_ge(small_copied, 1)
            act.activation(gates[:], small[:, :, 4:16], ACT.Sigmoid).then_inc(gates_ready, 1)
            act.wait_ge(var_ready, 2)
            act.activation(stat[:, 6:8], stat[:, 4:6], ACT.Sqrt).then_inc(std_ready, 1)
            projected(3, 8)
            act.activation(qT[:, 4:8, :], score_psum(2, SEQ), ACT.Copy).then_inc(proj_copied, 1)
            act.wait_ge(latT_done, 1)
            act.activation(latT[:], ps[:, 4, :].rearrange("p (k s) -> p k s", k=2), ACT.Copy)\
                .then_inc(latT_copied, 1)
            projected(4, 10)
            act.activation(rawT, score_psum(0, SEQ)[:, 0:2, :], ACT.Copy).then_inc(proj_copied, 1)
            act.activation(kv[:, 4 * SEQ:6 * SEQ].rearrange("p (b s) -> p b s", b=2),
                           score_psum(0, SEQ)[:, 2:4, :], ACT.Copy).then_inc(proj_copied, 1)
            act.wait_ge(akv_done, 1)
            act.activation(akT, ps[:, 5, 0:SEQ], ACT.Copy).then_inc(akv_copied, 1)
            act.activation(av, ps[:, 5, SEQ:W].rearrange("p (t d) -> p t d", t=T), ACT.Copy).then_inc(akv_copied, 1)
            for j in range(2):
                act.wait_ge(blk_made, j + 1)
                act.activation(blk_hi[:, j], work[:, 1, W * j:W * j + W].rearrange("p (l n) -> p l n", n=NCP),
                               ACT.Copy).then_inc(blk_hi_ready, 1)
            splits_to(U_WO[0])
            act.wait_ge(gelu_arg, 1)
            act.activation(hid3[:], hid2[:], ACT.Exp, scale=-2.0 * (2.0 / np.pi) ** 0.5).then_inc(gelu_exp, 1)
            act.wait_ge(ckv_done, 1)
            act.activation(ckT[:, 0:NCMP], ps[:, 4, 0:NCMP], ACT.Copy).then_inc(ckv_copied, 1)
            act.activation(cv[0:NCMP, :], ps[0:NCMP, 5, 0:HD], ACT.Copy).then_inc(ckv_copied, 1)
            splits_to(U_WO[0] + H)

            def exps(b):
                act.wait_ge(logits_ready, b + 1)
                n = keys(b)
                for h in range(4):
                    ins = act.activation(prob_tile(b, n)[:, h, :], logit_tile(b, n)[:, h, :], ACT.Exp,
                                         bias=negmax[:, b % 2, h:h + 1], accum_out=expsum[:, b % 2, h:h + 1])
                ins.then_inc(exps_done, 1)

            def copy_probT(b, n, bank):
                act.wait_ge(probT_done, b + 1)
                if n < P:
                    act.activation(probT[0:n, 0], ps[0:n, bank, :].rearrange("p (h q) -> p h q", h=4),
                                   ACT.Copy).then_inc(probT_copied, 1)
                else:
                    act.activation(probT[:, 0:n // P], ps[:, bank:bank + n // P, :].rearrange("p t (h q) -> p t h q", h=4),
                                   ACT.Copy).then_inc(probT_copied, 1)

            def heads_hi(g, heads, t, bank):
                act.activation(xT_hi[:, heads, P * t:P * t + P], ps[:, bank, :].rearrange("p (h q) -> p h q", h=4),
                               ACT.Copy).then_inc(oT_hi_ready, 1)

            exps(0)
            for b in range(NBATCH):
                if b + 1 < NBATCH:
                    exps(b + 1)
                copy_probT(b, keys(b), 4)
                g = GROUP[b]
                if b + 1 == NBATCH or GROUP[b + 1] != g:
                    act.wait_ge(pv_done, b + 1)
                    heads_hi(g, slice(4 * (g // 2), 4 * (g // 2) + 4), g % 2, 6 + g % 2)
            splits_to(U_FFN + H - 1)
            norm_base = 1

            def ffn(chunks, first, e=None, cbase=0):
                pos, ends = [0], bounds(chunks)
                total = len(ffn_order(chunks))
                per_c = T * len(chunks)

                def to(n):
                    n = min(n, total)
                    if e is None:
                        splits_to(first + n)
                        return
                    while pos[0] < n:
                        split(first + pos[0], e)
                        pos[0] += 1

                def hT_high(c, t):
                    w = chunks[c][1]
                    act.wait_ge(hT_done, at(T * (cbase + c) + t + 1, e, per_c))
                    act.activation(hT_hi[:, 0:w // P, P * t:P * t + P],
                                   ps[:, 7, 0:w].rearrange("p (j q) -> p j q", q=P), ACT.Copy)\
                        .then_inc(hT_hi_ready, 1)

                for c, (g_end, u_end, d_end) in enumerate(ends):
                    w = chunks[c][1]
                    to(g_end + 2)
                    act.wait_ge(units_used, at(first + g_end, e, PER))
                    for t in range(T):
                        i = T * (cbase + c) + t
                        if i >= T or e is not None:
                            act.wait_ge(h_done, at(i - T + 1, e, per_c))
                        act.activation(work[:, 0, W * t:W * t + w], ps[:, 4 + (4 * c + t) % 3, 0:w], ACT.Silu)\
                            .then_inc(silu_done, 1)
                    if c:
                        hT_high(c - 1, 1)
                    to(d_end + 2)
                    hT_high(c, 0)
                hT_high(len(chunks) - 1, 1)
                to(total)

            act.wait_ge(var_ready, 3)
            act.activation(stat[:, 2:4], stat[:, 0:2], ACT.Sqrt).then_inc(std_ready, 1)

            def xT_high(i):
                for b in range(4):
                    act.wait_ge(xT_done, 4 * i + b + 1)
                    act.activation(xT_hi[:, 2 * b:2 * b + 2, :],
                                   ps[:, b, :].rearrange("p (k s) -> p k s", k=2), ACT.Copy)\
                        .then_inc(xT_hi_ready, 1)

            xT_high(1)
            ffn(FFN_CHUNKS, U_FFN)

            splits_to(U_QKV + H)
            act.wait_ge(var_ready, 4)
            act.activation(stat[:, 2:4], stat[:, 0:2], ACT.Sqrt).then_inc(std_ready, 1)
            xT_high(2)
            for g in range(6):
                splits_to(U_QKV + 2 * g + 4)
                act.wait_ge(units_used, U_QKV + 2 * g + 2)
                if g < 2:
                    act.activation(qT[:, 4 * g:4 * g + 4, :], score_psum(2 * g, SEQ), ACT.Copy, scale=SCALE)\
                        .then_inc(proj_copied, 1)
                elif g < 4:
                    act.activation(bias_kT[:, 4 * g - 8:4 * g - 4, :], score_psum(2 * g, SEQ), ACT.Copy)\
                        .then_inc(proj_copied, 1)
                else:
                    act.activation(v1[:, :, W * (g - 4):W * (g - 4) + W], ps[:, 2 * g - 8:2 * g - 6, :], ACT.Copy)\
                        .then_inc(proj_copied, 1)
            splits_to(U_WO[1] + H)

            def stick_logs(b):
                n = P * (STICK[b][0] + 1)
                act.wait_ge(z_done, b + 1)
                if b >= 2:
                    act.wait_ge(stick_arg, b - 1)
                zt, lt = score_psum(4 + 2 * (b % 2), n), logit_tile(b, n)
                link(act.activation(lt, zt, ACT.Abs))
                link(act.activation(lt, lt, ACT.Exp, scale=-1.0))
                act.activation(lt, lt, ACT.Ln, bias=1.0).then_inc(log_done, 1)

            def stick_exps(b):
                n = P * (STICK[b][0] + 1)
                act.wait_ge(stick_arg, b + 1)
                act.activation(prob_tile(b, n), prob_tile(b, n), ACT.Exp).then_inc(stick_exp, 1)

            for b in range(NSTICK + 1):
                if b < NSTICK:
                    stick_logs(b)
                if b:
                    t, g = STICK[b - 1]
                    stick_exps(b - 1)
                    copy_probT(NBATCH + b - 1, P * (t + 1), 0)
                    act.wait_ge(pv_done, NBATCH + b)
                    heads_hi(4 + b - 1, slice(4 * g, 4 * g + 4), t, 2 + (b - 1) % 2)
            splits_to(U_MOE)
            act.wait_ge(var_ready, 5)
            act.activation(stat[:, 2:4], stat[:, 0:2], ACT.Sqrt).then_inc(std_ready, 1)
            act.activation(wr_hi[:], wr[:], ACT.Copy).then_inc(wr_hi_ready, 1)
            xT_high(3)
            for t in range(T):
                act.wait_ge(router_max, t + 1)
                act.activation(rexp[:, t], rlog[:, t, 0:NE], ACT.Exp, bias=rneg[:, t:t + 1]).then_inc(router_exp, 1)
            with act.Fori(0, NE) as e:
                ffn(MOE_CHUNKS, U_MOE, e, len(FFN_CHUNKS))
            act.wait_ge(var_ready, 6)
            act.activation(stat[:, 2:4], stat[:, 0:2], ACT.Sqrt).then_inc(std_ready, 1)

        @block.vector
        def _(dve):
            chain = [0]

            def link(ins):
                chain[0] += 1
                ins.then_inc(dve_chain, 1)
                dve.wait_ge(dve_chain, chain[0])

            done = [0]

            def split(n, e=None):
                dve.wait_ge(hi_ready, at(n + 1, e, PER))
                dve.tensor_tensor(unit(lo, n), unit(raw, n), unit(hi, n).bitcast(F32), ALU.subtract)\
                    .then_inc(lo_ready, 1)

            def splits_to(n):
                while done[0] < n:
                    split(done[0])
                    done[0] += 1

            def rms(i, src, width, col, vcount):
                for t in range(T):
                    junk = work[:, t, 0:width]
                    link(dve.tensor_tensor_reduce(junk, src(t), src(t), 1.0, 0.0, ALU.mult, ALU.add,
                                                  stat[:, col + t:col + t + 1]))
                dve.tensor_scalar(stat[:, col:col + 2], stat[:, col:col + 2], 1.0 / width, EPS, ALU.mult, ALU.add)\
                    .then_inc(var_ready, 1)
                dve.wait_ge(std_ready, vcount)
                link(dve.reciprocal(stat[:, col + 2:col + 4], stat[:, col + 2:col + 4]))

            def norm(i, vcount):
                rms(i, lambda t: x[:, t, :], D, 0, vcount)
                dve.wait_ge(gain_loaded[i], 16)
                for t in range(T):
                    dve.scalar_tensor_tensor(out=work[:, t, :], in0=x[:, t, :], scalar=stat[:, 2 + t:3 + t],
                                             in1=gain[:, i % 2, :], op0=ALU.mult, op1=ALU.mult)\
                        .then_inc(xs_ready if i < 4 else out_ready, 1)

            def xT_low(i):
                for b in range(4):
                    dve.wait_ge(xT_hi_ready, 4 * i + b + 1)
                    dst = xT_lo[:, 2 * b:2 * b + 2, :]
                    dve.tensor_tensor(dst, ps[:, b, :].rearrange("p (k s) -> p k s", k=2),
                                      xT_hi[:, 2 * b:2 * b + 2, :].bitcast(F32), ALU.subtract).then_inc(xT_ready, 1)

            dve.memset(ones[:], 1.0)
            dve.wait_ge(x_loaded, 16)
            norm(0, 1)
            splits_to(2)
            xT_low(0)
            splits_to(4)
            dve.wait_ge(proj_copied, 2)
            link(dve.tensor_copy(small[:], ps[:, 1, SEQ:SEQ + 32].rearrange("p (t n) -> p t n", t=T)))
            dve.tensor_scalar(small[:, :, 0:4], small[:, :, 0:4], 0.5, None, ALU.mult).then_inc(small_copied, 1)
            splits_to(8)
            dve.wait_ge(proj_copied, 4)
            dve.wait_ge(xT_done, 4)
            for t in range(T):
                link(dve.tensor_tensor_reduce(work[:, 1, RANK * t:RANK * t + RANK], tok[:, t, 0:RANK],
                                              tok[:, t, 0:RANK], 1.0, 0.0, ALU.mult, ALU.add, stat[:, 4 + t:5 + t]))
            dve.tensor_scalar(stat[:, 4:6], stat[:, 4:6], 1.0 / RANK, EPS, ALU.mult, ALU.add).then_inc(var_ready, 1)

            def index_sum(i, t):
                n = P * (t + 1)
                dve.wait_ge(idx_relu, i + 1)
                dve.wait_ge(small_copied, 1)
                sc, dst = logit_tile(0, n), iscore[:, t, 0:n]
                link(dve.tensor_scalar(dst, sc[:, 0, :], small[:, t, 0:1], None, ALU.mult))
                for h in range(1, 4):
                    ins = dve.scalar_tensor_tensor(out=dst, in0=sc[:, 2 * (h % 2) + h // 2, :],
                                                   scalar=small[:, t, h:h + 1], in1=dst, op0=ALU.mult, op1=ALU.add)
                    if h < 3:
                        link(ins)
                ins.then_inc(idx_summed, 1)

            def top_keys(i, t):
                n = P * (t + 1)
                dve.wait_ge(idx_masked, i + 1)
                src = iscore[:, t, 0:n]
                for r in range(TOPK // 8):
                    link(dve.max(top8[:], src))
                    link(dve.match_replace(topw[:, 0:n], top8[:], src, TAKEN))
                    src = topw[:, 0:n]
                link(dve.tensor_tensor(iscore[:, t, 0:n], topw[:, 0:n], iscore[:, t, 0:n], ALU.is_equal))

            index_sum(0, 1)
            index_sum(1, 0)
            dve.wait_ge(std_ready, 2)
            link(dve.reciprocal(stat[:, 6:8], stat[:, 6:8]))
            dve.wait_ge(small_loaded, 16 * 8)
            for t in range(T):
                dve.scalar_tensor_tensor(out=tok[:, t, 0:RANK], in0=tok[:, t, 0:RANK], scalar=stat[:, 6 + t:7 + t],
                                         in1=kv_gain[:], op0=ALU.mult, op1=ALU.mult).then_inc(lat_ready, 1)
            splits_to(10)
            dve.wait_ge(bias_flipped, 4)
            top_keys(0, 1)
            splits_to(12)
            top_keys(1, 0)
            dve.wait_ge(pos_done, 1)
            link(dve.tensor_copy(posT[:], ps[:, 7, 0:2 * CMP_LEN].rearrange("p (j l) -> p j l", j=2)))
            dve.wait_ge(proj_copied, 7)
            half = CMP_STRIDE
            for j in range(2):
                blk = work[:, 1, W * j:W * j + W].rearrange("p (l n) -> p l n", n=NCP)
                src = rawT[:, j, :].rearrange("p (n l) -> p l n", l=half)
                dve.memset(blk[:, :, NCMP:NCP], 0.0)
                for a in range(2):
                    ins = dve.tensor_tensor(blk[:, half * a:half * a + half, 0:NCMP], src[:, :, a:a + NCMP],
                                            posT[:, j, half * a:half * a + half].unsqueeze(2)
                                            .broadcast_to([P, half, NCMP]), ALU.add)
                ins.then_inc(blk_made, 1)
            for j in range(2):
                dve.wait_ge(blk_hi_ready, j + 1)
                dve.tensor_tensor(blk_lo[:, j], work[:, 1, W * j:W * j + W].rearrange("p (l n) -> p l n", n=NCP),
                                  blk_hi[:, j].bitcast(F32), ALU.subtract).then_inc(blk_ready, 1)
            splits_to(U_WO[0])
            dve.wait_ge(units_used, U_WO[0])
            link(dve.tensor_copy(hid[:], ps[:, 7, 64:64 + 2 * NCP].rearrange("p (j n) -> p j n", j=2)))
            link(dve.tensor_tensor(hid2[:], hid[:], hid[:], ALU.mult))
            link(dve.tensor_scalar(hid2[:], hid2[:], 0.044715, 1.0, ALU.mult, ALU.add))
            dve.tensor_tensor(hid2[:], hid2[:], hid[:], ALU.mult).then_inc(gelu_arg, 1)
            dve.wait_ge(gelu_exp, 1)
            link(dve.tensor_scalar(hid3[:], hid3[:], 1.0, None, ALU.add))
            link(dve.reciprocal(hid3[:], hid3[:]))
            dve.tensor_tensor(hid[:], hid[:], hid3[:], ALU.mult).then_inc(hid_ready, 1)
            splits_to(U_WO[0] + H)

            def logits(b):
                kind, t = BATCH[b]
                n = keys(b)
                dve.wait_ge(scores_done, b + 1)
                lt = logit_tile(b, n)
                link(dve.scalar_tensor_tensor(out=lt, in0=score_psum(2 * (b % 2), n), scalar=SCALE, in1=key_bias(b),
                                              op0=ALU.mult, op1=ALU.add))
                if kind == "dsa":
                    out_of = iscore[:, t, 0:n].unsqueeze(1).broadcast_to([P, 4, n])
                    link(dve.scalar_tensor_tensor(out=lt, in0=out_of, scalar=NEG, in1=lt, op0=ALU.mult, op1=ALU.add))
                dve.tensor_reduce(negmax[:, b % 2, :], lt, AX.X, ALU.max, negate=True).then_inc(logits_ready, 1)

            def normalise(b):
                kind, t = BATCH[b]
                n = keys(b)
                dve.wait_ge(exps_done, b + 1)
                iv = inv[:, b % 2, :]
                link(dve.reciprocal(iv, expsum[:, b % 2, :]))
                if kind != "dsa":
                    br = ("cmp", "sel", "win").index(kind)
                    link(dve.tensor_tensor(iv, iv, gates[:, t, 4 * br:4 * br + 4], ALU.mult))
                pt = prob_tile(b, n)
                dve.tensor_tensor(pt, pt, iv.unsqueeze(2).broadcast_to([P, 4, n]), ALU.mult)\
                    .then_inc(probs_ready, 1)

            def heads_lo(i, heads, t, bank):
                dve.wait_ge(oT_hi_ready, i + 1)
                dve.tensor_tensor(xT_lo[:, heads, P * t:P * t + P], ps[:, bank, :].rearrange("p (h q) -> p h q", h=4),
                                  xT_hi[:, heads, P * t:P * t + P].bitcast(F32), ALU.subtract).then_inc(oT_ready, 1)

            dve.wait_ge(bias_masked, 1)
            dve.wait_ge(gates_masked, 1)
            logits(0)
            for b in range(NBATCH):
                if b + 1 < NBATCH:
                    logits(b + 1)
                normalise(b)
                g = GROUP[b]
                if b + 1 == NBATCH or GROUP[b + 1] != g:
                    heads_lo(g, slice(4 * (g // 2), 4 * (g // 2) + 4), g % 2, 6 + g % 2)

            def add_out(layer):
                for n in range(2):
                    splits_to(min(U_WO[layer] + 2 * n + 4, U_MOE))
                    dve.wait_ge(units_used, U_WO[layer] + 2 * n + 2)
                    for t in range(T):
                        xs = x[:, t, W * n:W * n + W]
                        link(dve.tensor_tensor(xs, xs, ps[:, 2 * n + t, :], ALU.add))

            add_out(0)
            splits_to(U_FFN + H - 1)
            norm(1, 3)
            xT_low(1)

            def ffn(chunks, first, e=None, cbase=0):
                pos, ends = [0], bounds(chunks)
                total = len(ffn_order(chunks))
                per_c = T * len(chunks)

                def to(n):
                    n = min(n, total)
                    if e is None:
                        splits_to(first + n)
                        return
                    while pos[0] < n:
                        split(first + pos[0], e)
                        pos[0] += 1

                def hT_low(c, t):
                    w = chunks[c][1]
                    dve.wait_ge(hT_hi_ready, at(T * (cbase + c) + t + 1, e, per_c))
                    dve.tensor_tensor(hT_lo[:, 0:w // P, P * t:P * t + P],
                                      ps[:, 7, 0:w].rearrange("p (j q) -> p j q", q=P),
                                      hT_hi[:, 0:w // P, P * t:P * t + P].bitcast(F32), ALU.subtract)\
                        .then_inc(hT_ready, 1)

                for c, (g_end, u_end, d_end) in enumerate(ends):
                    w = chunks[c][1]
                    to(g_end + 2)
                    if c:
                        hT_low(c - 1, 1)
                    to(u_end + 1)
                    dve.wait_ge(units_used, at(first + u_end, e, PER))
                    for t in range(T):
                        i = T * (cbase + c) + t
                        dve.wait_ge(silu_done, at(i + 1, e, per_c))
                        if i >= T or e is not None:
                            dve.wait_ge(hT_done, at(i - T + 1, e, per_c))
                        dve.tensor_tensor(work[:, 1, W * t:W * t + w], work[:, 0, W * t:W * t + w],
                                          ps[:, 4 + (4 * c + 2 + t) % 3, 0:w], ALU.mult).then_inc(h_done, 1)
                    to(d_end + 2)
                    hT_low(c, 0)
                hT_low(len(chunks) - 1, 1)
                to(total)
                dve.wait_ge(units_used, at(first + total, e, PER))
                if e is not None:
                    dve.wait_ge(y_added, at(1, e, 1))
                for t in range(T):
                    for n in range(2):
                        xs = x[:, t, W * n:W * n + W]
                        if e is None:
                            ins = dve.tensor_tensor(xs, xs, ps[:, 2 * t + n, :], ALU.add)
                        else:
                            ins = dve.scalar_tensor_tensor(out=xs, in0=ps[:, 2 * t + n, :],
                                                           scalar=rgate[:, t, bass.ds(e, 1)], in1=xs,
                                                           op0=ALU.mult, op1=ALU.add)
                ins.then_inc(y_added, 1)

            ffn(FFN_CHUNKS, U_FFN)
            dve.wait_ge(y_added, 1)

            splits_to(U_QKV + H - 1)
            norm(2, 4)
            xT_low(2)
            splits_to(U_WO[1] + H)

            def softplus(b):
                t, g = STICK[b]
                n = P * (t + 1)
                dve.wait_ge(log_done, b + 1)
                lt, zt = logit_tile(b, n), score_psum(4 + 2 * (b % 2), n)
                dve.scalar_tensor_tensor(out=lt, in0=zt, scalar=0.0, in1=lt, op0=ALU.max, op1=ALU.add)\
                    .then_inc(soft_done, 1)

            def stick(b):
                t, g = STICK[b]
                n = P * (t + 1)
                dve.wait_ge(soft_masked, b + 1)
                if b >= 2:
                    dve.wait_ge(probT_done, NBATCH + b - 1)
                lt, pt, zt = logit_tile(b, n), prob_tile(b, n), score_psum(4 + 2 * (b % 2), n)
                for h in range(4):
                    ins = dve.tensor_tensor_scan(pt[:, h, ::-1], ones[:, 0:n], lt[:, h, ::-1], 0.0,
                                                 ALU.mult, ALU.add)
                link(ins)
                dve.tensor_tensor(pt, zt, pt, ALU.subtract).then_inc(stick_arg, 1)

            for b in range(NSTICK):
                softplus(b)
                stick(b)
                if b:
                    t, g = STICK[b - 1]
                    heads_lo(4 + b - 1, slice(4 * g, 4 * g + 4), t, 2 + (b - 1) % 2)
            t, g = STICK[-1]
            heads_lo(4 + NSTICK - 1, slice(4 * g, 4 * g + 4), t, 2 + (NSTICK - 1) % 2)
            add_out(1)
            norm(3, 5)
            dve.wait_ge(wr_hi_ready, 1)
            dve.tensor_tensor(wr_lo[:], wr[:], wr_hi[:].bitcast(F32), ALU.subtract).then_inc(wr_ready, 1)
            xT_low(3)
            link(dve.memset(rlog[:], TAKEN))
            link(dve.memset(rtop[:], TAKEN))
            dve.wait_ge(logit_done, 1)
            for t in range(T):
                link(dve.tensor_copy(rlog[:, t, 0:NE], ps[:, 4, NE * t:NE * t + NE]))
                link(dve.max(top8[:], rlog[:, t]))
                link(dve.tensor_copy(rtop[:, t, 0:2], top8[:, 0:2]))
                dve.tensor_scalar(rneg[:, t:t + 1], top8[:, 0:1], -1.0, None, ALU.mult).then_inc(router_max, 1)
                link(dve.match_replace(rsel[:, t], rtop[:, t], rlog[:, t], UNSEEN))
                link(dve.tensor_tensor(rsel[:, t], rsel[:, t], rlog[:, t], ALU.not_equal))
                dve.wait_ge(router_exp, t + 1)
                link(dve.tensor_tensor(rgate[:, t], rexp[:, t], rsel[:, t, 0:NE], ALU.mult))
                link(dve.tensor_reduce(rsum[:, t:t + 1], rgate[:, t], AX.X, ALU.add))
                link(dve.reciprocal(rsum[:, t:t + 1], rsum[:, t:t + 1]))
                link(dve.tensor_scalar(rgate[:, t], rgate[:, t], rsum[:, t:t + 1], None, ALU.mult))
            with dve.Fori(0, NE) as e:
                ffn(MOE_CHUNKS, U_MOE, e, len(FFN_CHUNKS))
            dve.wait_ge(y_added, NE + 1)
            norm(4, 6)

        @block.tensor
        def _(pe):
            used = [0]

            def take(n, e=None):
                pe.wait_ge(lo_ready, at(n + 1, e, PER))

            def three(out, s_hi, s_lo, m_hi, m_lo, start, stop):
                pe.matmul(out, s_hi, m_hi, start=start, stop=False, skip_group_check=True)
                pe.matmul(out, s_hi, m_lo, start=False, stop=False, skip_group_check=True)
                return pe.matmul(out, s_lo, m_hi, start=False, stop=stop, skip_group_check=True)

            def project_T(first, blocks, bank, extra=None):
                for q in range(2):
                    n = first + q
                    take(n)
                    wh, wl = unit3(hi, n), unit3(lo, n)
                    for i in range(blocks):
                        out = ps[:, bank + i // 2, SEQ * (i % 2):SEQ * (i % 2) + SEQ]
                        cols = slice(P * i, P * i + P)
                        for k in range(4):
                            ins = three(out, wh[:, k, cols], wl[:, k, cols], xT_hi[:, 4 * q + k, :],
                                        xT_lo[:, 4 * q + k, :], q == 0 and k == 0 and i % 2 == 0, q == 1 and k == 3)
                    if extra:
                        c0, cn = extra
                        for t in range(T):
                            out = ps[:, bank + (blocks - 1) // 2, SEQ + cn * t:SEQ + cn * t + cn]
                            for k in range(4):
                                ts = slice(P * t, P * t + P)
                                ins = three(out, xT_hi[:, 4 * q + k, ts], xT_lo[:, 4 * q + k, ts],
                                            wh[:, k, c0:c0 + cn], wl[:, k, c0:c0 + cn], False, q == 1 and k == 3)
                    ins.then_inc(units_used, 1)

            def project(first, banks):
                for q in range(2):
                    n = first + q
                    take(n)
                    wh, wl = unit3(hi, n), unit3(lo, n)
                    for t in range(T):
                        ts = slice(P * t, P * t + P)
                        for k in range(4):
                            ins = three(ps[:, banks[t], :], xT_hi[:, 4 * q + k, ts], xT_lo[:, 4 * q + k, ts],
                                        wh[:, k, :], wl[:, k, :], q == 0 and k == 0, q == 1 and k == 3)
                    ins.then_inc(units_used, 1)

            def transpose_x(i):
                pe.wait_ge(xs_ready, 2 * i + 2)
                for b in range(4):
                    for k in range(2):
                        for t in range(T):
                            o = k * SEQ + t * P
                            ins = pe.transpose(ps[:, b, o:o + P], work[:, t, 2 * b + k::KD], ident[:])
                    ins.then_inc(xT_done, 1)
                pe.wait_ge(xT_ready, 4 * i + 4)

            pe.wait_ge(small_loaded, 16 * 8)
            pe.matmul(ps[0:CH, 7, 0:SEQ + P], rel_sb[:], bucket_sb[:], start=True, stop=True).then_inc(diag_done, 1)
            pe.wait_ge(ident_ready, 2)
            transpose_x(0)
            project_T(0, 3, 0, (384, 16))
            project_T(2, 4, 2)
            pe.wait_ge(hankel_loaded, 16)
            pe.wait_ge(flip_ready, 2)
            pe.wait_ge(diag_copied, 1)
            for a in range(4):
                for h in range(2):
                    ins = pe.matmul(ps[:, 4 + a, SEQ * h:SEQ * h + SEQ], flip[:], hankel[:, 2 * a + h, :],
                                    start=True, stop=True)
                ins.then_inc(bias_flipped, 1)
            pe.wait_ge(bias_copied, 4)
            project(4, (4, 5))
            pe.wait_ge(proj_copied, 2)
            for i, t in enumerate((1, 0)):
                n = P * (t + 1)
                if i:
                    pe.wait_ge(idx_relu, i)
                for h in range(4):
                    p0 = IDX_DIM * (h % 2)
                    ins = pe.matmul(score_psum(6, n)[:, 2 * (h % 2) + h // 2, :],
                                    iqT[p0:p0 + IDX_DIM, h // 2, P * t:P * t + P], ikT[p0:p0 + IDX_DIM, 0:n],
                                    start=True, stop=True)
                ins.then_inc(idx_done, 1)
            pe.wait_ge(proj_copied, 3)
            project_T(6, 4, 2)
            pe.wait_ge(small_copied, 1)
            project_T(8, 4, 0)
            pe.wait_ge(lat_ready, 2)
            for k in range(2):
                for t in range(T):
                    ins = pe.transpose(ps[:, 4, k * SEQ + t * P:k * SEQ + t * P + P], tok[:, t, k:RANK:2], ident[:])
            ins.then_inc(latT_done, 1)
            pe.wait_ge(latT_copied, 1)
            for k in range(2):
                pe.matmul(ps[:, 5, 0:SEQ], wuk[:, k, :], latT[:, k, :], start=(k == 0), stop=(k == 1))
            for t in range(T):
                for k in range(2):
                    ins = pe.matmul(ps[:, 5, SEQ + HD * t:SEQ + HD * t + HD], latT[:, k, P * t:P * t + P], wuv[:, k, :],
                                    start=(k == 0), stop=(k == 1))
            ins.then_inc(akv_done, 1)
            pe.wait_ge(idx_relu, 2)
            for j in range(2):
                ins = pe.transpose(ps[:, 7, CMP_LEN * j:CMP_LEN * j + CMP_LEN], pos_sb[:, j, :],
                                   ident[0:CMP_LEN, 0:CMP_LEN])
            ins.then_inc(pos_done, 1)
            for j in range(2):
                pe.wait_ge(blk_ready, j + 1)
                for q in range(2):
                    n = U_CMP + 2 * j + q
                    take(n)
                    wh, wl = unit3(hi, n), unit3(lo, n)
                    for l in range(16):
                        ins = three(ps[:, 7, 64 + NCP * j:64 + NCP * j + NCP], wh[:, l, :], wl[:, l, :],
                                    blk_hi[:, j, 16 * q + l, :], blk_lo[:, j, 16 * q + l, :],
                                    q == 0 and l == 0 and j == 0, q == 1 and l == 15)
                    ins.then_inc(units_used, 1)
            pe.wait_ge(hid_ready, 1)
            pe.wait_ge(akv_copied, 2)
            pe.matmul(ps[:, 4, 0:NCMP], w2[:, 0, :], hid[:, 0, 0:NCMP], start=True, stop=True)
            pe.matmul(ps[0:NCMP, 5, 0:HD], hid[:, 1, 0:NCMP], w2[:, 1, :], start=True, stop=True)\
                .then_inc(ckv_done, 1)
            pe.wait_ge(ckv_copied, 2)
            pe.wait_ge(proj_copied, 7)

            def scores(b):
                kind, t = BATCH[b]
                n = keys(b)
                if b >= 2:
                    pe.wait_ge(logits_ready, b - 1)
                kT = {"dsa": akT, "sel": skT, "win": wkT, "cmp": ckT}[kind]
                out = score_psum(2 * (b % 2), n)
                for h in range(4):
                    hq = h if kind == "dsa" else AH + h
                    ins = pe.matmul(out[:, h, :], qT[:, hq, P * t:P * t + P], kT[:, 0:n], start=True, stop=True)
                ins.then_inc(scores_done, 1)

            def transpose_probs(b, b_tile, n, bank):
                for c in range(max(n // P, 1)):
                    m = min(n, P)
                    for h in range(4):
                        ins = pe.transpose(ps[0:m, bank + c, P * h:P * h + P], prob_tile(b_tile, n)[:, h, P * c:P * c + m],
                                           ident[:])
                ins.then_inc(probT_done, 1)

            scores(0)
            for b in range(NBATCH):
                kind, t = BATCH[b]
                n, g = keys(b), GROUP[b]
                if b + 1 < NBATCH:
                    scores(b + 1)
                pe.wait_ge(probs_ready, b + 1)
                transpose_probs(b, b, n, 4)
                first = b == 0 or GROUP[b - 1] != g
                if first and g >= 2:
                    pe.wait_ge(oT_ready, g - 1)
                pe.wait_ge(probT_copied, b + 1)
                for h in range(4):
                    for c in range(max(n // P, 1)):
                        m = min(n, P)
                        val = {"dsa": av[:, c, :], "sel": tok[:, c, RANK:RANK + HD],
                               "win": tok[:, c, RANK + HD:W], "cmp": cv[0:min(m, NCMP), :]}[kind]
                        ins = pe.matmul(ps[:, 6 + g % 2, P * h:P * h + P], val, probT[0:m, c, h, :],
                                        start=(first and h == 0 and c == 0), stop=(h == 3), skip_group_check=True)
                ins.then_inc(pv_done, 1)

            def project_out(layer):
                pe.wait_ge(oT_ready, 4 * layer + 4)
                for n in range(2):
                    project(U_WO[layer] + 2 * n, (2 * n, 2 * n + 1))

            project_out(0)
            transpose_x(1)

            def ffn(chunks, first, e=None, cbase=0):
                ends = bounds(chunks)
                cu = chunk_units(chunks)
                per_c = T * len(chunks)

                def bank_free(c, i):
                    gi = 4 * c + i - 3
                    if gi < 0:
                        return
                    pc, pi = gi // 4, gi % 4
                    pe.wait_ge(silu_done if pi < 2 else h_done, at(T * (cbase + pc) + pi % 2 + 1, e, per_c))

                def gate_or_up(c, base, i0, start_n):
                    w = chunks[c][1]
                    nk = UNIT // w
                    for q in range(cu[c][0]):
                        n = first + start_n + q
                        take(n, e)
                        wh, wl = unit3(hi, n), unit3(lo, n)
                        for t in range(T):
                            if q == 0:
                                bank_free(c, i0 + t)
                            out = ps[:, 4 + (4 * c + i0 + t) % 3, 0:w]
                            ts = slice(P * t, P * t + P)
                            for kk in range(nk):
                                k = nk * q + kk
                                ins = three(out, xT_hi[:, k, ts], xT_lo[:, k, ts], wh[:, kk, :], wl[:, kk, :],
                                            k == 0, k == KD - 1)
                        ins.then_inc(units_used, 1)

                def transpose_h(c, t):
                    w = chunks[c][1]
                    nj = w // P
                    i = T * (cbase + c) + t
                    pe.wait_ge(h_done, at(i + 1, e, per_c))
                    if i or e is not None:
                        pe.wait_ge(hT_ready, at(i, e, per_c))
                    for j in range(nj):
                        ins = pe.transpose(ps[:, 7, P * j:P * j + P], work[:, 1, W * t + j:W * t + w:nj], ident[:])
                    ins.then_inc(hT_done, 1)

                def down(c, start_n):
                    w = chunks[c][1]
                    pe.wait_ge(hT_ready, at(T * (cbase + c) + T, e, per_c))
                    for q in range(cu[c][1]):
                        n = first + start_n + q
                        take(n, e)
                        wh, wl = unit3(hi, n), unit3(lo, n)
                        for jj in range(2):
                            j = 2 * q + jj
                            for t in range(T):
                                ts = slice(P * t, P * t + P)
                                for m in range(2):
                                    cols = slice(W * m, W * m + W)
                                    ins = three(ps[:, 2 * t + m, :], hT_hi[:, j, ts], hT_lo[:, j, ts],
                                                wh[:, jj, cols], wl[:, jj, cols], c == 0 and j == 0,
                                                c == len(chunks) - 1 and j == w // P - 1)
                        ins.then_inc(units_used, 1)

                for c, (g_end, u_end, d_end) in enumerate(ends):
                    gate_or_up(c, 0, 0, g_end - cu[c][0])
                    if c:
                        transpose_h(c - 1, 1)
                    gate_or_up(c, 0, 2, g_end)
                    if c:
                        if c == 1 and e is not None:
                            pe.wait_ge(y_added, at(1, e, 1))
                        down(c - 1, u_end)
                    transpose_h(c, 0)
                transpose_h(len(chunks) - 1, 1)
                down(len(chunks) - 1, ends[-1][2])

            ffn(FFN_CHUNKS, U_FFN)
            transpose_x(2)
            for g in range(4):
                project_T(U_QKV + 2 * g, 4, 2 * g)
            pe.wait_ge(proj_copied, 9)
            project(U_QKV + 8, (0, 1))
            project(U_QKV + 10, (2, 3))

            def stick_scores(b):
                t, g = STICK[b]
                n = P * (t + 1)
                if b == 0:
                    pe.wait_ge(proj_copied, 11)
                if b >= 2:
                    pe.wait_ge(stick_arg, b - 1)
                out = score_psum(4 + 2 * (b % 2), n)
                for h in range(4):
                    hd = 4 * g + h
                    ins = pe.matmul(out[:, h, :], qT[:, hd, P * t:P * t + P], bias_kT[:, hd, 0:n], start=True, stop=True)
                ins.then_inc(z_done, 1)

            stick_scores(0)
            for b in range(NSTICK):
                t, g = STICK[b]
                n = P * (t + 1)
                if b + 1 < NSTICK:
                    stick_scores(b + 1)
                if b == 0:
                    pe.wait_ge(proj_copied, 13)
                pe.wait_ge(stick_masked, b + 1)
                for c in range(n // P):
                    for h in range(4):
                        ins = pe.transpose(ps[:, c, P * h:P * h + P], prob_tile(b, n)[:, h, P * c:P * c + P], ident[:])
                ins.then_inc(probT_done, 1)
                if b >= 2:
                    pe.wait_ge(oT_ready, 4 + b - 1)
                pe.wait_ge(probT_copied, NBATCH + b + 1)
                for h in range(4):
                    hd = 4 * g + h
                    for c in range(n // P):
                        ins = pe.matmul(ps[:, 2 + b % 2, P * h:P * h + P], v1[:, c, HD * hd:HD * hd + HD],
                                        probT[:, c, h, :], start=(h == 0 and c == 0), stop=(h == 3),
                                        skip_group_check=True)
                ins.then_inc(pv_done, 1)
            project_out(1)
            transpose_x(3)
            pe.wait_ge(wr_ready, 1)
            for t in range(T):
                ts = slice(P * t, P * t + P)
                for k in range(KD):
                    ins = three(ps[:, 4, NE * t:NE * t + NE], xT_hi[:, k, ts], xT_lo[:, k, ts], wr_hi[:, k, :],
                                wr_lo[:, k, :], k == 0 and t == 0, k == KD - 1)
            ins.then_inc(logit_done, 1)
            pe.wait_ge(router_max, 2)
            with pe.Fori(0, NE) as e:
                ffn(MOE_CHUNKS, U_MOE, e, len(FFN_CHUNKS))


_INS = ['x', 'rel_bias', 'ev_norm_mix', 'ev_w_in', 'ev_kv_norm', 'ev_w_uk', 'ev_w_uv', 'ev_cmp_pos', 'ev_cmp_w1',
        'ev_cmp_w2', 'ev_w_out', 'ev_norm_ffn', 'ev_w_gate', 'ev_w_up', 'ev_w_down', 'od_norm_mix', 'od_w_qkv',
        'od_w_out', 'od_norm_ffn', 'od_w_router', 'od_w_gate', 'od_w_up', 'od_w_down', 'final_norm']


def kernel(**inputs):
    import numpy as _np
    import concourse.bacc as _bacc
    from concourse import mybir as _mybir
    from concourse.bass_utils import run_bass_kernel_spmd as _run

    nc = _bacc.Bacc("TRN2", target_bir_lowering=False, num_devices=1)
    arrays, args = {}, []
    for name in _INS:
        a = _np.ascontiguousarray(inputs[name])
        arrays[f"in_{name}_dram"] = a
        args.append(nc.dram_tensor(f"in_{name}_dram", a.shape, _mybir.dt.from_np(a.dtype), kind="ExternalInput").ap())
    out = nc.dram_tensor("out_0_dram", (1, SEQ, D), _mybir.dt.from_np(_np.dtype("float32")), kind="ExternalOutput").ap()
    build(nc, *args, out)
    r = _run(nc, [arrays], core_ids=[0])
    return r.results[0]["out_0_dram"]
```

```python
from contextlib import ExitStack

import numpy as np

import concourse.bass as bass
from concourse import mybir

F32 = mybir.dt.float32
F32R = mybir.dt.float32r
ALU = mybir.AluOpType
ACT = mybir.ActivationFunctionType
AX = mybir.AxisListType

P = 128
SEQ = 256
D = 1024
KD = D // P
T = SEQ // P
HD = 128
AH = BH = 4
CH = 8
RANK = 256
IDX_DIM = 64
NB = 32
MAX_DIST = 128
CMP_LEN, CMP_STRIDE = 32, 16
NCMP = (SEQ - CMP_LEN) // CMP_STRIDE + 1
NCP = NCMP + 1
TOPK = min(256, SEQ // 4)
FF = 2816
EFF = 3584
NE = 8
EPS = 1e-6
NEG = -1e30
UNSEEN = -1e38
TAKEN = -3e38
SCALE = HD ** -0.5
W = 512

O_AQ = 0
O_LAT = O_AQ + AH * HD
O_IQ = O_LAT + RANK
O_IK = O_IQ + 4 * IDX_DIM
O_IW = O_IK + IDX_DIM
O_BQ = O_IW + 4
O_KV = O_BQ + BH * HD
O_BG = O_KV + 6 * HD

UNIT = 2048
R = 6
H = 3

FFN_CHUNKS = [(f, min(W, FF - f)) for f in range(0, FF, W)]
MOE_CHUNKS = [(f, min(W, EFF - f)) for f in range(0, EFF, W)]


def bucket_rows():
    dist = np.arange(SEQ)
    half = NB // 2
    large = half + (np.log(np.maximum(dist, 1).astype(np.float32) / half)
                    / np.float32(np.log(MAX_DIST / half)) * (NB - half)).astype(np.int32)
    bucket = np.where(dist < half, dist, np.minimum(large, NB - 1))
    rows = np.zeros((NB, SEQ + P), np.float32)
    rows[bucket[::-1], np.arange(SEQ)] = 1.0
    return rows


def chunk_units(chunks):
    return [(2, 2) if w == W else (1, 1) for _, w in chunks]


def ffn_order(chunks):
    order = []
    cu = chunk_units(chunks)
    for c in range(len(chunks) + 1):
        if c < len(chunks):
            order += [("gate", c, q) for q in range(cu[c][0])] + [("up", c, q) for q in range(cu[c][0])]
        if c:
            order += [("down", c - 1, q) for q in range(cu[c - 1][1])]
    return order


def bounds(chunks):
    cu, n, out = chunk_units(chunks), 0, []
    for c in range(len(chunks)):
        g = n + cu[c][0]
        u = g + cu[c][0]
        n = u + (cu[c - 1][1] if c else 0)
        out.append((g, u, n))
    return out


def at(const, e=None, per=0):
    return const if e is None else e * per + const


def build(nc, x_d, rel_bias, ev_norm_mix, ev_w_in, ev_kv_norm, ev_w_uk, ev_w_uv, ev_cmp_pos, ev_cmp_w1,
          ev_cmp_w2, ev_w_out, ev_norm_ffn, ev_w_gate, ev_w_up, ev_w_down, od_norm_mix, od_w_qkv, od_w_out,
          od_norm_ffn, od_w_router, od_w_gate, od_w_up, od_w_down, final_norm, out_d):
    win = ev_w_in[0].rearrange("(p k) n -> p k n", k=KD)

    def k_units(view, parts, width):
        return [([(view[:, 4 * q:4 * q + 4, s:s + n], d, n) for s, d, n in parts], 4, width) for q in range(2)]

    units = []
    units += k_units(win, [(O_IQ, 0, 320), (O_IK, 320, 64), (O_IW, 384, 4), (O_BG, 388, 12)], 400)
    units += k_units(win, [(O_AQ, 0, W)], W)
    units += k_units(win, [(O_LAT, 0, RANK), (O_KV + 3 * HD, 256, HD), (O_KV + 5 * HD, 384, HD)], W)
    units += k_units(win, [(O_BQ, 0, W)], W)
    units += k_units(win, [(O_KV, 0, 3 * HD), (O_KV + 4 * HD, 3 * HD, HD)], W)
    U_CMP = len(units)
    for j in range(2):
        w1 = ev_cmp_w1[0, j].rearrange("(l p) n -> p l n", p=P)
        units += [([(w1[:, 16 * q:16 * q + 16], 0, HD)], 16, HD) for q in range(2)]
    U_WO = [0, 0]
    U_WO[0] = len(units)

    def out_units(w):
        v = w.rearrange("(h p) n -> p h n", p=P)
        return [u for n in range(2) for u in k_units(v, [(W * n, 0, W)], W)]

    units += out_units(ev_w_out[0])
    U_FFN = len(units)
    gate_v, up_v = (w[0].rearrange("(p k) f -> p k f", k=KD) for w in (ev_w_gate, ev_w_up))
    for kind, c, q in ffn_order(FFN_CHUNKS):
        f, w = FFN_CHUNKS[c]
        if kind == "down":
            v = ev_w_down[0, f:f + w].rearrange("(p j) n -> p j n", j=w // P)
            units.append(([(v[:, 2 * q:2 * q + 2], 0, D)], 2, D))
        else:
            v = gate_v if kind == "gate" else up_v
            ks = slice(4 * q, 4 * q + 4) if w == W else slice(0, KD)
            units.append(([(v[:, ks, f:f + w], 0, w)], UNIT // w, w))
    U_QKV = len(units)
    qkv_v = od_w_qkv[0].rearrange("(p k) n -> p k n", k=KD)
    for g in range(3 * D // W):
        units += k_units(qkv_v, [(W * g, 0, W)], W)
    U_WO[1] = len(units)
    units += out_units(od_w_out[0])
    U_MOE = len(units)
    moe_order = ffn_order(MOE_CHUNKS)
    PER = len(moe_order)
    assert PER % R == 0 and PER % H == 0
    moe_gate, moe_up = (w.rearrange("o e (p k) f -> (o e) p k f", k=KD) for w in (od_w_gate, od_w_up))
    moe_down = od_w_down.rearrange("o e (c p j) n -> (o e) c p j n", p=P, j=W // P)

    landed_at = []
    slot_total = [0] * R
    for n, (pieces, _, _) in enumerate(units):
        slot_total[n % R] += 16 * len(pieces)
        landed_at.append(slot_total[n % R])

    def landed(n):
        if n < U_MOE:
            return landed_at[n]
        return slot_total[n % R] + 16 * len([m for m in range(U_MOE, n + 1) if m % R == n % R])

    def shape_of(n):
        if n < U_MOE:
            return units[n][1:]
        return (2, D) if moe_order[(n - U_MOE) % PER][0] == "down" else (4, W)

    buckets_d = nc.inline_tensor(bucket_rows(), "bucket_rows").ap()
    diag_d = nc.dram_tensor("bias_by_distance", [CH, SEQ + P], F32).ap()

    with ExitStack() as ctx:
        def sb(name, shape, dt=F32):
            return ctx.enter_context(nc.sbuf_tensor(name, shape, dt))

        def sem(name):
            return ctx.enter_context(nc.semaphore(name))

        raw = sb("raw", [P, R, UNIT])
        hi = sb("hi", [P, H, UNIT], F32R)
        lo = sb("lo", [P, H, UNIT], F32R)
        x = sb("x", [P, T, D])
        work = sb("work", [P, 4, D])
        probT = sb("probT", [P, T, 4, P])
        xT_hi = sb("xT_hi", [P, KD, SEQ], F32R)
        xT_lo = sb("xT_lo", [P, KD, SEQ], F32R)
        gain = sb("gain", [P, 2, D])
        arena_at = nc.sbuf_base
        sb("arena", [P, 2 * KD * SEQ])
        qT = nc.alloc_sbuf_tensor_at("qT", [P, 8, SEQ], F32, offset=arena_at)
        bias_kT = nc.alloc_sbuf_tensor_at("bias_kT", [P, 8, SEQ], F32, offset=arena_at + 4 * KD * SEQ)
        xs_hi = nc.alloc_sbuf_tensor_at("xs_hi", [P, T, D], F32R, offset=arena_at)
        xs_lo = nc.alloc_sbuf_tensor_at("xs_lo", [P, T, D], F32R, offset=arena_at + 4 * KD * SEQ)
        kv = sb("kv", [P, 9 * SEQ])
        tok = sb("tok", [P, T, W])
        latT = sb("latT", [P, T, SEQ])
        hT_hi = sb("hT_hi", [P, 4, SEQ], F32R)
        hT_lo = sb("hT_lo", [P, 4, SEQ], F32R)
        iscore = sb("iscore", [P, T, SEQ])
        ident = sb("ident", [P, P])
        flip = sb("flip", [P, P])
        bucket_sb = sb("bucket_sb", [NB, SEQ + P])
        rel_sb = sb("rel_sb", [NB, CH])
        diag_sb = sb("diag_sb", [CH, SEQ + P])
        wuk = sb("wuk", [P, 2, HD])
        wuv = sb("wuv", [P, 2, HD])
        w2 = sb("w2", [P, 2, HD])
        pos_sb = sb("pos_sb", [CMP_LEN, 2, HD])
        posT = sb("posT", [P, 2, CMP_LEN])
        kv_gain = sb("kv_gain", [P, RANK])
        wr = sb("wr", [P, KD, NE])
        wr_hi = sb("wr_hi", [P, KD, NE], F32R)
        wr_lo = sb("wr_lo", [P, KD, NE], F32R)
        small = sb("small", [P, T, 16])
        gates = sb("gates", [P, T, 12])
        stat = sb("stat", [P, 8])
        hid = sb("hid", [P, 2, NCP])
        hid2 = sb("hid2", [P, 2, NCP])
        hid3 = sb("hid3", [P, 2, NCP])
        ckT = sb("ckT", [P, NCP])
        cv = sb("cv", [NCP, HD])
        negmax = sb("negmax", [P, 2, 4])
        expsum = sb("expsum", [P, 2, 4])
        inv = sb("inv", [P, 2, 4])
        top8 = sb("top8", [P, 8])
        rlog = sb("rlog", [P, T, 16])
        rsel = sb("rsel", [P, T, 16])
        rexp = sb("rexp", [P, T, NE])
        rtop = sb("rtop", [P, T, 8])
        rneg = sb("rneg", [P, T])
        rsum = sb("rsum", [P, T])
        rgate = sb("rgate", [P, T, 16])
        rpick = sb("rpick", [P, T, 16])
        rplace = sb("rplace", [P, T, 16])
        rcount = sb("rcount", [P, NE])
        most = sb("most", [1, 1])
        most_i = sb("most_i", [1, 1], mybir.dt.int32)
        iota = sb("iota", [P, P])
        before = sb("before", [P, P])
        place = sb("place", [P, T, P], F32R)
        placeT = sb("placeT", [P, SEQ], F32R)
        gate_col = sb("gate_col", [P, T])
        ones = sb("ones", [P, SEQ])
        root = sb("root", [P, 1])
        ps = ctx.enter_context(nc.psum_tensor("ps", [P, 8, W], F32))

        iqT = kv[:, 0:2 * SEQ].rearrange("p (b s) -> p b s", b=2)
        ikT = kv[:, 2 * SEQ:3 * SEQ]
        akT = kv[:, 3 * SEQ:4 * SEQ]
        skT = kv[:, 4 * SEQ:5 * SEQ]
        wkT = kv[:, 5 * SEQ:6 * SEQ]
        av = kv[:, 6 * SEQ:7 * SEQ].rearrange("p (t d) -> p t d", t=T)
        rawT = kv[:, 7 * SEQ:9 * SEQ].rearrange("p (j s) -> p j s", j=2)
        v1 = kv[:, 0:T * D].rearrange("p (t d) -> p t d", t=T)
        blk_hi, blk_lo = (h[:].rearrange("p j s -> p (j s)").rearrange("p (j l n) -> p j l n", j=2, n=NCP)
                          for h in (hT_hi, hT_lo))
        xg_hi, xg_lo = (h[:, 0:4, :].rearrange("p a (b s) -> p (a b) s", s=P) for h in (xT_hi, xT_lo))
        y_hi, y_lo = (h[:, 4:8, :].rearrange("p a s -> p (a s)") for h in (xT_hi, xT_lo))
        topw = work[:, 3, 0:SEQ]
        hankel = work[:, 2:4, :].rearrange("p a (b s) -> p (a b) s", s=SEQ)

        raw_landed = [sem(f"raw_landed{i}") for i in range(R)]
        hi_ready = sem("hi_ready")
        lo_ready = sem("lo_ready")
        units_used = sem("units_used")
        x_loaded = sem("x_loaded")
        gain_loaded = [sem(f"gain_loaded{i}") for i in range(5)]
        buckets_loaded = sem("buckets_loaded")
        small_loaded = sem("small_loaded")
        ident_ready = sem("ident_ready")
        flip_ready = sem("flip_ready")
        var_ready = sem("var_ready")
        std_ready = sem("std_ready")
        xs_ready = sem("xs_ready")
        xT_done = sem("xT_done")
        xT_hi_ready = sem("xT_hi_ready")
        xT_ready = sem("xT_ready")
        diag_done = sem("diag_done")
        diag_copied = sem("diag_copied")
        diag_stored = sem("diag_stored")
        hankel_loaded = sem("hankel_loaded")
        bias_flipped = sem("bias_flipped")
        bias_copied = sem("bias_copied")
        bias_masked = sem("bias_masked")
        proj_copied = sem("proj_copied")
        small_copied = sem("small_copied")
        gates_ready = sem("gates_ready")
        gates_masked = sem("gates_masked")
        lat_ready = sem("lat_ready")
        latT_done = sem("latT_done")
        latT_copied = sem("latT_copied")
        akv_done = sem("akv_done")
        akv_copied = sem("akv_copied")
        idx_done = sem("idx_done")
        idx_relu = sem("idx_relu")
        idx_summed = sem("idx_summed")
        idx_masked = sem("idx_masked")
        pos_done = sem("pos_done")
        blk_made = sem("blk_made")
        blk_hi_ready = sem("blk_hi_ready")
        blk_ready = sem("blk_ready")
        gelu_arg = sem("gelu_arg")
        gelu_exp = sem("gelu_exp")
        hid_ready = sem("hid_ready")
        ckv_done = sem("ckv_done")
        ckv_copied = sem("ckv_copied")
        scores_done = sem("scores_done")
        logits_ready = sem("logits_ready")
        exps_done = sem("exps_done")
        probs_ready = sem("probs_ready")
        probT_done = sem("probT_done")
        probT_copied = sem("probT_copied")
        pv_done = sem("pv_done")
        oT_hi_ready = sem("oT_hi_ready")
        oT_ready = sem("oT_ready")
        x_added = sem("x_added")
        silu_done = sem("silu_done")
        h_done = sem("h_done")
        hT_done = sem("hT_done")
        hT_hi_ready = sem("hT_hi_ready")
        hT_ready = sem("hT_ready")
        z_done = sem("z_done")
        rest_ready = sem("rest_ready")
        beta_ready = sem("beta_ready")
        rest_masked = sem("rest_masked")
        sticks_done = sem("sticks_done")
        stick_masked = sem("stick_masked")
        wr_hi_ready = sem("wr_hi_ready")
        wr_ready = sem("wr_ready")
        logit_done = sem("logit_done")
        router_max = sem("router_max")
        router_exp = sem("router_exp")
        y_added = sem("y_added")
        iota_ready = sem("iota_ready")
        ones_ready = sem("ones_ready")
        xs_hi_ready = sem("xs_hi_ready")
        xs_lo_ready = sem("xs_lo_ready")
        picks_ready = sem("picks_ready")
        places_done = sem("places_done")
        count_ready = sem("count_ready")
        place_ready = sem("place_ready")
        gathered = sem("gathered")
        xg_hi_ready = sem("xg_hi_ready")
        xg_ready = sem("xg_ready")
        placeT_done = sem("placeT_done")
        placeT_ready = sem("placeT_ready")
        y_hi_ready = sem("y_hi_ready")
        y_ready = sem("y_ready")
        gate_ready = sem("gate_ready")
        scattered = sem("scattered")
        scatter_added = sem("scatter_added")
        g_silu_done = sem("g_silu_done")
        g_h_done = sem("g_h_done")
        g_hT_done = sem("g_hT_done")
        g_hT_hi_ready = sem("g_hT_hi_ready")
        g_hT_ready = sem("g_hT_ready")
        dve_chain = sem("dve_chain")
        act_chain = sem("act_chain")
        out_ready = sem("out_ready")
        out_stored = sem("out_stored")

        block = ctx.enter_context(nc.Block())

        BATCH = [("dsa", 0), ("dsa", 1), ("sel", 0), ("win", 0), ("cmp", 0), ("sel", 1), ("win", 1), ("cmp", 1)]
        GROUP = [0, 1, 2, 2, 2, 3, 3, 3]
        NBATCH = len(BATCH)

        def keys(b):
            kind, t = BATCH[b]
            return P * (t + 1) if kind != "cmp" else (NCMP - CMP_STRIDE // 2 if t == 0 else NCMP)

        def key_bias(b):
            kind, t = BATCH[b]
            heads = slice(0, AH) if kind == "dsa" else slice(AH, AH + BH)
            if kind == "cmp":
                first = P * (1 - t) + CMP_LEN - 1
                return bias_kT[:, heads, first:first + CMP_STRIDE * (keys(b) - 1) + 1:CMP_STRIDE]
            return bias_kT[:, heads, P * (1 - t):P * (1 - t) + keys(b)]

        def logit_tile(b, n):
            return work[:, b % 2, :].rearrange("p (h s) -> p h s", h=4)[:, :, 0:n]

        def prob_tile(b, n):
            return work[:, 2 + b % 2, :].rearrange("p (h s) -> p h s", h=4)[:, :, 0:n]

        def score_psum(first, n):
            return ps[:, first:first + 2, :].rearrange("p a (h s) -> p (a h) s", s=SEQ)[:, :, 0:n]

        STICK = [(1, 0), (1, 1), (0, 0), (0, 1)]
        NSTICK = len(STICK)

        def unit(ring, n):
            a, b = shape_of(n)
            return ring[:, n % (R if ring is raw else H), 0:a * b]

        def unit3(ring, n):
            a, b = shape_of(n)
            return unit(ring, n).rearrange("p (a b) -> p a b", a=a)

        GB = bounds(MOE_CHUNKS)
        NC = len(MOE_CHUNKS)

        def few(eng):
            eng.wait_ge(count_ready, 1)
            return eng.value_load(most_i[0:1, 0:1], min_val=0, max_val=SEQ) <= P

        @block.sync
        def _(sp):
            for n, (pieces, a, b) in enumerate(units):
                if n >= R:
                    sp.wait_ge(lo_ready, n - R + 1)
                for src, d, cnt in pieces:
                    sp.dma_start(unit3(raw, n)[:, :, d:d + cnt], src).then_inc(raw_landed[n % R], 16)
            with sp.Fori(0, NE) as e:
                for i, (kind, c, q) in enumerate(moe_order):
                    n = U_MOE + i
                    sp.wait_ge(lo_ready, at(n - R + 1, e, PER))
                    if kind == "down":
                        src = moe_down[bass.ds(e, 1), c, :, 2 * q:2 * q + 2, :].rearrange("e p j n -> (e p) j n")
                    else:
                        view = moe_gate if kind == "gate" else moe_up
                        src = view[bass.ds(e, 1), :, 4 * q:4 * q + 4, W * c:W * c + W].rearrange(
                            "e p k f -> (e p) k f")
                    sp.dma_start(unit3(raw, n), src).then_inc(raw_landed[n % R], 16)
            sp.wait_ge(out_ready, T)
            sp.dma_start(out_d[0].rearrange("(t p) d -> p t d", p=P), work[:, 0:T, :]).then_inc(out_stored, 16)
            sp.wait_ge(out_stored, 16)

        gains = [ev_norm_mix[0], ev_norm_ffn[0], od_norm_mix[0], od_norm_ffn[0], final_norm]

        def row_to_all(row):
            return bass.AP(tensor=row.tensor, offset=row.offset, ap=[[0, P], [1, row.shape[0]]])

        @block.gpsimd
        def _(pool):
            pool.memset(ident[:], 0.0).then_inc(ident_ready, 1)
            pool.memset(flip[:], 0.0).then_inc(flip_ready, 1)
            pool.wait_ge(ident_ready, 1)
            pool.affine_select(out=ident[:], in_=ident[:], compare_op=ALU.not_equal, fill=1.0, base=0,
                               pattern=[[-1, P]], channel_multiplier=1).then_inc(ident_ready, 1)
            pool.wait_ge(flip_ready, 1)
            pool.affine_select(out=flip[:], in_=flip[:], compare_op=ALU.not_equal, fill=1.0, base=-(P - 1),
                               pattern=[[1, P]], channel_multiplier=1).then_inc(flip_ready, 1)
            pool.iota(iota[:], [[1, P]], base=0, channel_multiplier=0, allow_small_or_imprecise_dtypes=True)\
                .then_inc(iota_ready, 1)
            pool.memset(before[:], 1.0).then_inc(iota_ready, 1)
            pool.wait_ge(iota_ready, 2)
            pool.affine_select(out=before[:], in_=before[:], compare_op=ALU.is_gt, fill=0.0, base=0,
                               pattern=[[1, P]], channel_multiplier=-1).then_inc(iota_ready, 1)
            pool.wait_ge(diag_copied, 1)
            pool.dma_start(diag_d, diag_sb[:]).then_inc(diag_stored, 16)
            pool.wait_ge(diag_stored, 16)
            pool.dma_start(hankel, bass.AP(tensor=diag_d.tensor, offset=diag_d.offset,
                                           ap=[[1, P], [SEQ + P, CH], [1, SEQ]])).then_inc(hankel_loaded, 16)
            pool.wait_ge(bias_copied, 4)
            pool.affine_select(out=bias_kT[:], in_=bias_kT[:], compare_op=ALU.is_ge, fill=NEG, base=P,
                               pattern=[[0, 8], [-1, SEQ]], channel_multiplier=1).then_inc(bias_masked, 1)
            pool.wait_ge(gates_ready, 1)
            pool.affine_select(out=gates[:, 0, 0:BH], in_=gates[:, 0, 0:BH], compare_op=ALU.is_ge, fill=0.0,
                               base=-(CMP_LEN - 1), pattern=[[0, BH]], channel_multiplier=1)\
                .then_inc(gates_masked, 1)
            for i, t in enumerate((1, 0)):
                pool.wait_ge(idx_summed, i + 1)
                n = P * (t + 1)
                pool.affine_select(out=iscore[:, t, 0:n], in_=iscore[:, t, 0:n], compare_op=ALU.is_ge, fill=UNSEEN,
                                   base=P * t, pattern=[[-1, n]], channel_multiplier=1).then_inc(idx_masked, 1)
            pool.wait_ge(xs_ready, 2)
            pool.dma_start(gain[:, 0, :], row_to_all(gains[2])).then_inc(gain_loaded[2], 16)
            pool.wait_ge(xs_ready, 4)
            pool.dma_start(gain[:, 1, :], row_to_all(gains[3])).then_inc(gain_loaded[3], 16)
            pool.wait_ge(xs_ready, 6)
            pool.dma_start(gain[:, 0, :], row_to_all(gains[4])).then_inc(gain_loaded[4], 16)
            for b in range(NSTICK + 1):
                if b < NSTICK:
                    n = P * (STICK[b][0] + 1)
                    pool.wait_ge(rest_ready, b + 1)
                    lt = logit_tile(b, n)[:, :, n - P:n]
                    pool.affine_select(out=lt, in_=lt, compare_op=ALU.is_gt, fill=1.0, base=0,
                                       pattern=[[0, 4], [-1, P]], channel_multiplier=1).then_inc(rest_masked, 1)
                if b:
                    n = P * (STICK[b - 1][0] + 1)
                    pool.wait_ge(sticks_done, b)
                    pt = prob_tile(b - 1, n)[:, :, n - P:n]
                    pool.affine_select(out=pt, in_=pt, compare_op=ALU.is_gt, fill=0.0, base=0,
                                       pattern=[[0, 4], [-1, P]], channel_multiplier=1).then_inc(stick_masked, 1)

        @block.scalar
        def _(act):
            chain = [0]

            def link(ins):
                chain[0] += 1
                ins.then_inc(act_chain, 1)
                act.wait_ge(act_chain, chain[0])

            act.dma_start(x[:], x_d[0].rearrange("(t p) d -> p t d", p=P)).then_inc(x_loaded, 16)
            act.dma_start(gain[:, 0, :], row_to_all(gains[0])).then_inc(gain_loaded[0], 16)
            act.dma_start(rel_sb[:], rel_bias).then_inc(buckets_loaded, 16)
            act.dma_start(bucket_sb[:], buckets_d).then_inc(buckets_loaded, 16)
            act.dma_start(pos_sb[:], ev_cmp_pos[0].rearrange("j l d -> l j d")).then_inc(small_loaded, 16)
            act.dma_start(wuk[:], ev_w_uk[0].rearrange("(p k) d -> p k d", k=2)).then_inc(small_loaded, 16)
            act.dma_start(wuv[:], ev_w_uv[0].rearrange("(p k) d -> p k d", k=2)).then_inc(small_loaded, 16)
            act.dma_start(w2[:], ev_cmp_w2[0].rearrange("j p d -> p j d")).then_inc(small_loaded, 16)
            act.dma_start(kv_gain[:], row_to_all(ev_kv_norm[0])).then_inc(small_loaded, 16)
            act.dma_start(wr[:], od_w_router[0].rearrange("(p k) e -> p k e", k=KD)).then_inc(small_loaded, 16)
            act.dma_start(gain[:, 1, :], row_to_all(gains[1])).then_inc(gain_loaded[1], 16)

            done = [0]

            def split(n, e=None):
                act.wait_ge(raw_landed[n % R], at(landed(n), e, 16 * PER // R))
                if n >= H:
                    act.wait_ge(units_used, at(n - H + 1, e, PER))
                act.activation(unit(hi, n), unit(raw, n), ACT.Copy).then_inc(hi_ready, 1)

            def splits_to(n):
                while done[0] < n:
                    split(done[0])
                    done[0] += 1

            def norm_std(count, col=0):
                act.activation(root[:], root[:], ACT.Sqrt)
                act.wait_ge(var_ready, count)
                act.activation(stat[:, col + 2:col + 4], stat[:, col:col + 2], ACT.Sqrt).then_inc(std_ready, 1)

            def xT_high(i):
                for b in range(4):
                    act.wait_ge(xT_done, 4 * i + b + 1)
                    act.activation(xT_hi[:, 2 * b:2 * b + 2, :],
                                   ps[:, b, :].rearrange("p (k s) -> p k s", k=2), ACT.Copy)\
                        .then_inc(xT_hi_ready, 1)

            act.wait_ge(ones_ready, 1)
            splits_to(1)
            norm_std(1)
            act.wait_ge(diag_done, 1)
            act.activation(diag_sb[:], ps[0:CH, 7, 0:SEQ + P], ACT.Copy).then_inc(diag_copied, 1)
            splits_to(H)
            xT_high(0)

            def projected(g, n):
                splits_to(n + 2)
                act.wait_ge(units_used, n)

            projected(0, 2)
            act.activation(iqT, score_psum(0, SEQ)[:, 0:2, :], ACT.Copy).then_inc(proj_copied, 1)
            act.activation(ikT, ps[:, 1, 0:SEQ], ACT.Copy).then_inc(proj_copied, 1)
            projected(1, 4)
            act.activation(qT[:, 0:4, :], score_psum(2, SEQ), ACT.Copy).then_inc(proj_copied, 1)
            for a in range(4):
                act.wait_ge(bias_flipped, a + 1)
                act.activation(bias_kT[:, 2 * a:2 * a + 2, :], ps[:, 4 + a, :].rearrange("p (h s) -> p h s", h=2),
                               ACT.Copy).then_inc(bias_copied, 1)
            projected(2, 6)
            act.activation(tok[:], ps[:, 4:6, :], ACT.Copy).then_inc(proj_copied, 1)
            for i, t in enumerate((1, 0)):
                n = P * (t + 1)
                act.wait_ge(idx_done, i + 1)
                if i:
                    act.wait_ge(idx_summed, i)
                act.activation(logit_tile(0, n), score_psum(6, n), ACT.Relu, scale=IDX_DIM ** -0.5)\
                    .then_inc(idx_relu, 1)
            act.wait_ge(small_copied, 1)
            act.activation(gates[:], small[:, :, 4:16], ACT.Sigmoid).then_inc(gates_ready, 1)
            norm_std(2, 4)
            projected(3, 8)
            act.activation(qT[:, 4:8, :], score_psum(2, SEQ), ACT.Copy).then_inc(proj_copied, 1)
            act.wait_ge(latT_done, 1)
            act.activation(latT[:], ps[:, 4, :].rearrange("p (k s) -> p k s", k=2), ACT.Copy)\
                .then_inc(latT_copied, 1)
            projected(4, 10)
            act.activation(rawT, score_psum(0, SEQ)[:, 0:2, :], ACT.Copy).then_inc(proj_copied, 1)
            act.activation(kv[:, 4 * SEQ:6 * SEQ].rearrange("p (b s) -> p b s", b=2),
                           score_psum(0, SEQ)[:, 2:4, :], ACT.Copy).then_inc(proj_copied, 1)
            act.wait_ge(akv_done, 1)
            act.activation(akT, ps[:, 5, 0:SEQ], ACT.Copy).then_inc(akv_copied, 1)
            act.activation(av, ps[:, 5, SEQ:W].rearrange("p (t d) -> p t d", t=T), ACT.Copy).then_inc(akv_copied, 1)
            for j in range(2):
                act.wait_ge(blk_made, j + 1)
                act.activation(blk_hi[:, j], work[:, 1, W * j:W * j + W].rearrange("p (l n) -> p l n", n=NCP),
                               ACT.Copy).then_inc(blk_hi_ready, 1)
            splits_to(U_WO[0])
            act.wait_ge(gelu_arg, 1)
            act.activation(hid3[:], hid2[:], ACT.Exp, scale=-2.0 * (2.0 / np.pi) ** 0.5).then_inc(gelu_exp, 1)
            act.wait_ge(ckv_done, 1)
            act.activation(ckT[:, 0:NCMP], ps[:, 4, 0:NCMP], ACT.Copy).then_inc(ckv_copied, 1)
            act.activation(cv[0:NCMP, :], ps[0:NCMP, 5, 0:HD], ACT.Copy).then_inc(ckv_copied, 1)
            splits_to(U_WO[0] + H)

            def exps(b):
                act.wait_ge(logits_ready, b + 1)
                n = keys(b)
                for h in range(4):
                    ins = act.activation(prob_tile(b, n)[:, h, :], logit_tile(b, n)[:, h, :], ACT.Exp,
                                         bias=negmax[:, b % 2, h:h + 1], accum_out=expsum[:, b % 2, h:h + 1])
                ins.then_inc(exps_done, 1)

            def copy_probT(b, n, bank):
                act.wait_ge(probT_done, b + 1)
                if n < P:
                    act.activation(probT[0:n, 0], ps[0:n, bank, :].rearrange("p (h q) -> p h q", h=4),
                                   ACT.Copy).then_inc(probT_copied, 1)
                else:
                    act.activation(probT[:, 0:n // P], ps[:, bank:bank + n // P, :].rearrange("p t (h q) -> p t h q", h=4),
                                   ACT.Copy).then_inc(probT_copied, 1)

            def heads_hi(g, heads, t, bank):
                act.activation(xT_hi[:, heads, P * t:P * t + P], ps[:, bank, :].rearrange("p (h q) -> p h q", h=4),
                               ACT.Copy).then_inc(oT_hi_ready, 1)

            exps(0)
            exps(1)
            for b in range(NBATCH):
                copy_probT(b, keys(b), 4)
                g = GROUP[b]
                if b + 1 == NBATCH or GROUP[b + 1] != g:
                    act.wait_ge(pv_done, b + 1)
                    heads_hi(g, slice(4 * (g // 2), 4 * (g // 2) + 4), g % 2, 6 + g % 2)
                if b + 2 < NBATCH:
                    exps(b + 2)
            splits_to(U_FFN + H - 1)
            def ffn(chunks, first, e=None, cbase=0):
                pos, ends = [0], bounds(chunks)
                total = len(ffn_order(chunks))
                per_c = T * len(chunks)

                def to(n):
                    n = min(n, total)
                    if e is None:
                        splits_to(first + n)
                        return
                    while pos[0] < n:
                        split(first + pos[0], e)
                        pos[0] += 1

                def hT_high(c, t):
                    w = chunks[c][1]
                    act.wait_ge(hT_done, at(T * (cbase + c) + t + 1, e, per_c))
                    act.activation(hT_hi[:, 0:w // P, P * t:P * t + P],
                                   ps[:, 7, 0:w].rearrange("p (j q) -> p j q", q=P), ACT.Copy)\
                        .then_inc(hT_hi_ready, 1)

                for c, (g_end, u_end, d_end) in enumerate(ends):
                    w = chunks[c][1]
                    to(g_end + 2)
                    act.wait_ge(units_used, at(first + g_end, e, PER))
                    for t in range(T):
                        i = T * (cbase + c) + t
                        if i >= T or e is not None:
                            act.wait_ge(h_done, at(i - T + 1, e, per_c))
                        act.activation(work[:, 0, W * t:W * t + w], ps[:, 4 + (4 * c + t) % 3, 0:w], ACT.Silu)\
                            .then_inc(silu_done, 1)
                    if c:
                        hT_high(c - 1, 1)
                    to(d_end + 2)
                    hT_high(c, 0)
                hT_high(len(chunks) - 1, 1)
                to(total)

            norm_std(3)

            xT_high(1)
            ffn(FFN_CHUNKS, U_FFN)

            splits_to(U_QKV + H)
            norm_std(4)
            xT_high(2)
            act.activation(root[:], root[:], ACT.Sigmoid)
            for g in range(6):
                splits_to(U_QKV + 2 * g + 4)
                act.wait_ge(units_used, U_QKV + 2 * g + 2)
                if g < 2:
                    act.activation(qT[:, 4 * g:4 * g + 4, :], score_psum(2 * g, SEQ), ACT.Copy, scale=SCALE)\
                        .then_inc(proj_copied, 1)
                elif g < 4:
                    act.activation(bias_kT[:, 4 * g - 8:4 * g - 4, :], score_psum(2 * g, SEQ), ACT.Copy)\
                        .then_inc(proj_copied, 1)
                else:
                    act.activation(v1[:, :, W * (g - 4):W * (g - 4) + W], ps[:, 2 * g - 8:2 * g - 6, :], ACT.Copy)\
                        .then_inc(proj_copied, 1)
            splits_to(U_WO[1] + H)

            def sigmoids(b):
                n = P * (STICK[b][0] + 1)
                act.wait_ge(z_done, b + 1)
                if b >= 2:
                    act.wait_ge(sticks_done, b - 1)
                zt = score_psum(4 + 2 * (b % 2), n)
                act.activation(logit_tile(b, n), zt, ACT.Sigmoid, scale=-1.0).then_inc(rest_ready, 1)
                act.activation(zt, zt, ACT.Sigmoid).then_inc(beta_ready, 1)

            sigmoids(0)
            sigmoids(1)
            for b in range(NSTICK):
                t, g = STICK[b]
                copy_probT(NBATCH + b, P * (t + 1), 0)
                if b + 2 < NSTICK:
                    sigmoids(b + 2)
                act.wait_ge(pv_done, NBATCH + b + 1)
                heads_hi(4 + b, slice(4 * g, 4 * g + 4), t, 2 + b % 2)
            splits_to(U_MOE)
            norm_std(5)
            act.activation(wr_hi[:], wr[:], ACT.Copy).then_inc(wr_hi_ready, 1)
            xT_high(3)
            act.activation(xs_hi[:], work[:, 0:T, :], ACT.Copy).then_inc(xs_hi_ready, 1)
            for t in range(T):
                act.wait_ge(router_max, t + 1)
                act.activation(rexp[:, t], rlog[:, t, 0:NE], ACT.Exp, bias=rneg[:, t:t + 1]).then_inc(router_exp, 1)

            def gathered_high(e=None):
                for b in range(2):
                    act.wait_ge(gathered, at(b + 1 if e is None else b + 3, e, 2))
                    act.activation(xg_hi[:, 4 * b:4 * b + 4, :], ps[:, 2 + b, :].rearrange("p (k s) -> p k s", k=4),
                                   ACT.Copy).then_inc(xg_hi_ready, 1)

            def y_high(e=None):
                act.wait_ge(units_used, at(U_MOE if e is not None else U_MOE + NE * PER, e, PER))
                act.activation(y_hi, ps[:, 0:2, :].rearrange("p a n -> p (a n)"), ACT.Copy).then_inc(y_hi_ready, 1)

            fits = few(act)
            with act.If(fits):
                gathered_high()
                with act.Fori(0, NE) as e:
                    pos = [0]

                    def to(n):
                        while pos[0] < min(n, PER):
                            split(U_MOE + pos[0], e)
                            pos[0] += 1

                    to(2)
                    y_high(e)
                    for c, (g_end, u_end, d_end) in enumerate(GB):
                        to(g_end + 2)
                        act.wait_ge(units_used, at(U_MOE + g_end, e, PER))
                        if c:
                            act.wait_ge(g_h_done, at(c, e, NC))
                        act.activation(work[:, 0, 0:W], ps[:, 4 + 2 * c % 3, :], ACT.Silu).then_inc(g_silu_done, 1)
                        to(u_end + 2)
                        if c == 2:
                            act.wait_ge(placeT_done, at(1, e, 1))
                            act.activation(placeT[:], ps[:, 2, 0:SEQ], ACT.Copy).then_inc(placeT_ready, 1)
                        to(d_end + 2)
                        act.wait_ge(g_hT_done, at(c + 1, e, NC))
                        act.activation(hT_hi[:, :, 0:P], ps[:, 7, :].rearrange("p (j q) -> p j q", q=P), ACT.Copy)\
                            .then_inc(g_hT_hi_ready, 1)
                    to(PER)
                    gathered_high(e)
                y_high()
            with act.Else():
                with act.Fori(0, NE) as e:
                    ffn(MOE_CHUNKS, U_MOE, e, len(FFN_CHUNKS))
            norm_std(6)

        @block.vector
        def _(dve):
            chain = [0]

            def link(ins):
                chain[0] += 1
                ins.then_inc(dve_chain, 1)
                dve.wait_ge(dve_chain, chain[0])

            done = [0]

            def split(n, e=None):
                dve.wait_ge(hi_ready, at(n + 1, e, PER))
                dve.tensor_tensor(unit(lo, n), unit(raw, n), unit(hi, n).bitcast(F32), ALU.subtract)\
                    .then_inc(lo_ready, 1)

            def splits_to(n):
                while done[0] < n:
                    split(done[0])
                    done[0] += 1

            def rms(i, src, width, col, vcount):
                for t in range(T):
                    junk = work[:, t, 0:width]
                    link(dve.tensor_tensor_reduce(junk, src(t), src(t), 1.0, 0.0, ALU.mult, ALU.add,
                                                  stat[:, col + t:col + t + 1]))
                dve.tensor_scalar(stat[:, col:col + 2], stat[:, col:col + 2], 1.0 / width, EPS, ALU.mult, ALU.add)\
                    .then_inc(var_ready, 1)
                dve.wait_ge(std_ready, vcount)
                link(dve.reciprocal(stat[:, col + 2:col + 4], stat[:, col + 2:col + 4]))

            def norm(i, vcount):
                rms(i, lambda t: x[:, t, :], D, 0, vcount)
                dve.wait_ge(gain_loaded[i], 16)
                for t in range(T):
                    dve.scalar_tensor_tensor(out=work[:, t, :], in0=x[:, t, :], scalar=stat[:, 2 + t:3 + t],
                                             in1=gain[:, i % 2, :], op0=ALU.mult, op1=ALU.mult)\
                        .then_inc(xs_ready if i < 4 else out_ready, 1)

            def xT_low(i):
                for b in range(4):
                    dve.wait_ge(xT_hi_ready, 4 * i + b + 1)
                    dst = xT_lo[:, 2 * b:2 * b + 2, :]
                    dve.tensor_tensor(dst, ps[:, b, :].rearrange("p (k s) -> p k s", k=2),
                                      xT_hi[:, 2 * b:2 * b + 2, :].bitcast(F32), ALU.subtract).then_inc(xT_ready, 1)

            dve.memset(root[:], 1.0)
            dve.memset(ones[:], 1.0).then_inc(ones_ready, 1)
            dve.wait_ge(x_loaded, 16)
            norm(0, 1)
            splits_to(2)
            xT_low(0)
            splits_to(4)
            dve.wait_ge(proj_copied, 2)
            link(dve.tensor_copy(small[:], ps[:, 1, SEQ:SEQ + 32].rearrange("p (t n) -> p t n", t=T)))
            dve.tensor_scalar(small[:, :, 0:4], small[:, :, 0:4], 0.5, None, ALU.mult).then_inc(small_copied, 1)
            splits_to(8)
            dve.wait_ge(proj_copied, 4)
            dve.wait_ge(xT_done, 4)
            for t in range(T):
                link(dve.tensor_tensor_reduce(work[:, 1, RANK * t:RANK * t + RANK], tok[:, t, 0:RANK],
                                              tok[:, t, 0:RANK], 1.0, 0.0, ALU.mult, ALU.add, stat[:, 4 + t:5 + t]))
            dve.tensor_scalar(stat[:, 4:6], stat[:, 4:6], 1.0 / RANK, EPS, ALU.mult, ALU.add).then_inc(var_ready, 1)

            def index_sum(i, t):
                n = P * (t + 1)
                dve.wait_ge(idx_relu, i + 1)
                dve.wait_ge(small_copied, 1)
                sc, dst = logit_tile(0, n), iscore[:, t, 0:n]
                link(dve.tensor_scalar(dst, sc[:, 0, :], small[:, t, 0:1], None, ALU.mult))
                for h in range(1, 4):
                    ins = dve.scalar_tensor_tensor(out=dst, in0=sc[:, 2 * (h % 2) + h // 2, :],
                                                   scalar=small[:, t, h:h + 1], in1=dst, op0=ALU.mult, op1=ALU.add)
                    if h < 3:
                        link(ins)
                ins.then_inc(idx_summed, 1)

            def top_keys(i, t):
                n = P * (t + 1)
                dve.wait_ge(idx_masked, i + 1)
                src = iscore[:, t, 0:n]
                for r in range(TOPK // 8):
                    link(dve.max(top8[:], src))
                    link(dve.match_replace(topw[:, 0:n], top8[:], src, TAKEN))
                    src = topw[:, 0:n]
                link(dve.tensor_tensor(iscore[:, t, 0:n], topw[:, 0:n], iscore[:, t, 0:n], ALU.is_equal))

            index_sum(0, 1)
            index_sum(1, 0)
            dve.wait_ge(std_ready, 2)
            link(dve.reciprocal(stat[:, 6:8], stat[:, 6:8]))
            dve.wait_ge(small_loaded, 16 * 6)
            for t in range(T):
                dve.scalar_tensor_tensor(out=tok[:, t, 0:RANK], in0=tok[:, t, 0:RANK], scalar=stat[:, 6 + t:7 + t],
                                         in1=kv_gain[:], op0=ALU.mult, op1=ALU.mult).then_inc(lat_ready, 1)
            splits_to(10)
            dve.wait_ge(bias_flipped, 4)
            top_keys(0, 1)
            splits_to(12)
            top_keys(1, 0)
            dve.wait_ge(pos_done, 1)
            link(dve.tensor_copy(posT[:], ps[:, 7, 0:2 * CMP_LEN].rearrange("p (j l) -> p j l", j=2)))
            dve.wait_ge(proj_copied, 7)
            half = CMP_STRIDE
            for j in range(2):
                blk = work[:, 1, W * j:W * j + W].rearrange("p (l n) -> p l n", n=NCP)
                src = rawT[:, j, :].rearrange("p (n l) -> p l n", l=half)
                dve.memset(blk[:, :, NCMP:NCP], 0.0)
                for a in range(2):
                    ins = dve.tensor_tensor(blk[:, half * a:half * a + half, 0:NCMP], src[:, :, a:a + NCMP],
                                            posT[:, j, half * a:half * a + half].unsqueeze(2)
                                            .broadcast_to([P, half, NCMP]), ALU.add)
                ins.then_inc(blk_made, 1)
            for j in range(2):
                dve.wait_ge(blk_hi_ready, j + 1)
                dve.tensor_tensor(blk_lo[:, j], work[:, 1, W * j:W * j + W].rearrange("p (l n) -> p l n", n=NCP),
                                  blk_hi[:, j].bitcast(F32), ALU.subtract).then_inc(blk_ready, 1)
            splits_to(U_WO[0])
            dve.wait_ge(units_used, U_WO[0])
            link(dve.tensor_copy(hid[:], ps[:, 7, 64:64 + 2 * NCP].rearrange("p (j n) -> p j n", j=2)))
            link(dve.tensor_tensor(hid2[:], hid[:], hid[:], ALU.mult))
            link(dve.tensor_scalar(hid2[:], hid2[:], 0.044715, 1.0, ALU.mult, ALU.add))
            dve.tensor_tensor(hid2[:], hid2[:], hid[:], ALU.mult).then_inc(gelu_arg, 1)
            dve.wait_ge(gelu_exp, 1)
            link(dve.tensor_scalar(hid3[:], hid3[:], 1.0, None, ALU.add))
            link(dve.reciprocal(hid3[:], hid3[:]))
            dve.tensor_tensor(hid[:], hid[:], hid3[:], ALU.mult).then_inc(hid_ready, 1)
            splits_to(U_WO[0] + H)

            def logits(b):
                kind, t = BATCH[b]
                n = keys(b)
                dve.wait_ge(scores_done, b + 1)
                lt = logit_tile(b, n)
                link(dve.scalar_tensor_tensor(out=lt, in0=score_psum(2 * (b % 2), n), scalar=SCALE, in1=key_bias(b),
                                              op0=ALU.mult, op1=ALU.add))
                if kind == "dsa":
                    out_of = iscore[:, t, 0:n].unsqueeze(1).broadcast_to([P, 4, n])
                    link(dve.scalar_tensor_tensor(out=lt, in0=out_of, scalar=NEG, in1=lt, op0=ALU.mult, op1=ALU.add))
                dve.tensor_reduce(negmax[:, b % 2, :], lt, AX.X, ALU.max, negate=True).then_inc(logits_ready, 1)

            def normalise(b):
                kind, t = BATCH[b]
                n = keys(b)
                dve.wait_ge(exps_done, b + 1)
                iv = inv[:, b % 2, :]
                link(dve.reciprocal(iv, expsum[:, b % 2, :]))
                if kind != "dsa":
                    br = ("cmp", "sel", "win").index(kind)
                    link(dve.tensor_tensor(iv, iv, gates[:, t, 4 * br:4 * br + 4], ALU.mult))
                pt = prob_tile(b, n)
                dve.tensor_tensor(pt, pt, iv.unsqueeze(2).broadcast_to([P, 4, n]), ALU.mult)\
                    .then_inc(probs_ready, 1)

            def heads_lo(i, heads, t, bank):
                dve.wait_ge(oT_hi_ready, i + 1)
                dve.tensor_tensor(xT_lo[:, heads, P * t:P * t + P], ps[:, bank, :].rearrange("p (h q) -> p h q", h=4),
                                  xT_hi[:, heads, P * t:P * t + P].bitcast(F32), ALU.subtract).then_inc(oT_ready, 1)

            dve.wait_ge(bias_masked, 1)
            dve.wait_ge(gates_masked, 1)
            logits(0)
            logits(1)
            normalise(0)
            for b in range(NBATCH):
                if b + 1 < NBATCH:
                    normalise(b + 1)
                if b + 2 < NBATCH:
                    logits(b + 2)
                g = GROUP[b]
                if b + 1 == NBATCH or GROUP[b + 1] != g:
                    heads_lo(g, slice(4 * (g // 2), 4 * (g // 2) + 4), g % 2, 6 + g % 2)

            def add_out(layer):
                for n in range(2):
                    splits_to(min(U_WO[layer] + 2 * n + 4, U_MOE))
                    dve.wait_ge(units_used, U_WO[layer] + 2 * n + 2)
                    for t in range(T):
                        xs = x[:, t, W * n:W * n + W]
                        link(dve.tensor_tensor(xs, xs, ps[:, 2 * n + t, :], ALU.add))

            add_out(0)
            splits_to(U_FFN + H - 1)
            norm(1, 3)
            xT_low(1)

            def ffn(chunks, first, e=None, cbase=0):
                pos, ends = [0], bounds(chunks)
                total = len(ffn_order(chunks))
                per_c = T * len(chunks)

                def to(n):
                    n = min(n, total)
                    if e is None:
                        splits_to(first + n)
                        return
                    while pos[0] < n:
                        split(first + pos[0], e)
                        pos[0] += 1

                def hT_low(c, t):
                    w = chunks[c][1]
                    dve.wait_ge(hT_hi_ready, at(T * (cbase + c) + t + 1, e, per_c))
                    dve.tensor_tensor(hT_lo[:, 0:w // P, P * t:P * t + P],
                                      ps[:, 7, 0:w].rearrange("p (j q) -> p j q", q=P),
                                      hT_hi[:, 0:w // P, P * t:P * t + P].bitcast(F32), ALU.subtract)\
                        .then_inc(hT_ready, 1)

                for c, (g_end, u_end, d_end) in enumerate(ends):
                    w = chunks[c][1]
                    to(g_end + 2)
                    if c:
                        hT_low(c - 1, 1)
                    to(u_end + 1)
                    dve.wait_ge(units_used, at(first + u_end, e, PER))
                    for t in range(T):
                        i = T * (cbase + c) + t
                        dve.wait_ge(silu_done, at(i + 1, e, per_c))
                        if i >= T or e is not None:
                            dve.wait_ge(hT_done, at(i - T + 1, e, per_c))
                        dve.tensor_tensor(work[:, 1, W * t:W * t + w], work[:, 0, W * t:W * t + w],
                                          ps[:, 4 + (4 * c + 2 + t) % 3, 0:w], ALU.mult).then_inc(h_done, 1)
                    to(d_end + 2)
                    hT_low(c, 0)
                hT_low(len(chunks) - 1, 1)
                to(total)
                dve.wait_ge(units_used, at(first + total, e, PER))
                if e is not None:
                    dve.wait_ge(y_added, at(1, e, 1))
                for t in range(T):
                    for n in range(2):
                        xs = x[:, t, W * n:W * n + W]
                        if e is None:
                            ins = dve.tensor_tensor(xs, xs, ps[:, 2 * t + n, :], ALU.add)
                        else:
                            ins = dve.scalar_tensor_tensor(out=xs, in0=ps[:, 2 * t + n, :],
                                                           scalar=rgate[:, t, bass.ds(e, 1)], in1=xs,
                                                           op0=ALU.mult, op1=ALU.add)
                ins.then_inc(y_added, 1)

            ffn(FFN_CHUNKS, U_FFN)
            dve.wait_ge(y_added, 1)

            splits_to(U_QKV + H - 1)
            norm(2, 4)
            xT_low(2)
            splits_to(U_WO[1] + H)

            def sticks(b):
                t, g = STICK[b]
                n = P * (t + 1)
                if b >= 2:
                    dve.wait_ge(probT_done, NBATCH + b - 1)
                lt, pt, beta = logit_tile(b, n), prob_tile(b, n), score_psum(4 + 2 * (b % 2), n)
                dve.memset(pt[:, :, n - 1:n], 1.0)
                dve.wait_ge(rest_masked, b + 1)
                for h in range(4):
                    ins = dve.tensor_tensor_scan(pt[:, h, 0:n - 1][:, ::-1], lt[:, h, 1:n][:, ::-1],
                                                 ones[:, 0:n - 1], 1.0, ALU.mult, ALU.mult)
                link(ins)
                dve.wait_ge(beta_ready, b + 1)
                dve.tensor_tensor(pt, beta, pt, ALU.mult).then_inc(sticks_done, 1)

            sticks(0)
            for b in range(NSTICK):
                if b + 1 < NSTICK:
                    sticks(b + 1)
                t, g = STICK[b]
                heads_lo(4 + b, slice(4 * g, 4 * g + 4), t, 2 + b % 2)
            add_out(1)
            norm(3, 5)
            dve.wait_ge(wr_hi_ready, 1)
            dve.tensor_tensor(wr_lo[:], wr[:], wr_hi[:].bitcast(F32), ALU.subtract).then_inc(wr_ready, 1)
            xT_low(3)
            dve.wait_ge(xs_hi_ready, 1)
            dve.tensor_tensor(xs_lo[:], work[:, 0:T, :], xs_hi[:].bitcast(F32), ALU.subtract).then_inc(xs_lo_ready, 1)
            link(dve.memset(rlog[:], TAKEN))
            link(dve.memset(rtop[:], TAKEN))
            link(dve.memset(rgate[:], 0.0))
            link(dve.memset(rpick[:], 0.0))
            dve.wait_ge(logit_done, 1)
            for t in range(T):
                link(dve.tensor_copy(rlog[:, t, 0:NE], ps[:, 4, NE * t:NE * t + NE]))
                link(dve.max(top8[:], rlog[:, t]))
                link(dve.tensor_copy(rtop[:, t, 0:2], top8[:, 0:2]))
                dve.tensor_scalar(rneg[:, t:t + 1], top8[:, 0:1], -1.0, None, ALU.mult).then_inc(router_max, 1)
                link(dve.match_replace(rsel[:, t], rtop[:, t], rlog[:, t], UNSEEN))
                link(dve.tensor_tensor(rpick[:, t, 0:NE], rsel[:, t, 0:NE], rlog[:, t, 0:NE], ALU.not_equal))
                dve.wait_ge(router_exp, t + 1)
                gt = rgate[:, t, 0:NE]
                link(dve.tensor_tensor(gt, rexp[:, t], rpick[:, t, 0:NE], ALU.mult))
                link(dve.tensor_reduce(rsum[:, t:t + 1], gt, AX.X, ALU.add))
                link(dve.reciprocal(rsum[:, t:t + 1], rsum[:, t:t + 1]))
                dve.tensor_scalar(gt, gt, rsum[:, t:t + 1], None, ALU.mult).then_inc(picks_ready, 1)
            dve.wait_ge(places_done, 1)
            link(dve.memset(rplace[:], 0.0))
            link(dve.tensor_copy(rplace[:, :, 0:NE], ps[:, 4, 16:32].rearrange("p (t e) -> p t e", t=T)))
            link(dve.tensor_copy(rcount[:], ps[:, 4, 32:40]))
            link(dve.tensor_reduce(most[:], rcount[0:1, :], AX.X, ALU.max))
            dve.tensor_copy(most_i[:], most[:]).then_inc(count_ready, 1)

            def make_place(e=None):
                col = slice(0, 1) if e is None else bass.ds(e + 1, 1)
                for t in range(T):
                    ins = dve.tensor_scalar(place[:, t, :], iota[:], rplace[:, t, col], rpick[:, t, col],
                                            ALU.is_equal, ALU.mult)
                ins.then_inc(place_ready, 1)

            def gathered_low(e=None):
                for b in range(2):
                    dve.wait_ge(xg_hi_ready, at(b + 1 if e is None else b + 3, e, 2))
                    dst = slice(4 * b, 4 * b + 4)
                    dve.tensor_tensor(xg_lo[:, dst, :], ps[:, 2 + b, :].rearrange("p (k s) -> p k s", k=4),
                                      xg_hi[:, dst, :].bitcast(F32), ALU.subtract).then_inc(xg_ready, 1)

            def y_low(e=None):
                dve.wait_ge(y_hi_ready, at(1 if e is not None else NE + 1, e, 1))
                dve.tensor_tensor(y_lo, ps[:, 0:2, :].rearrange("p a n -> p (a n)"), y_hi.bitcast(F32), ALU.subtract)\
                    .then_inc(y_ready, 1)

            def add_scattered(i, e=None):
                first = 0 if e is not None else 4 * NE
                if i == 0:
                    dve.wait_ge(gate_ready, at(1 if e is not None else NE + 1, e, 1))
                    if e is None:
                        dve.wait_ge(scatter_added, first)
                dve.wait_ge(scattered, at(first + i + 1, e, 4))
                xs = x[:, i // 2, W * (i % 2):W * (i % 2) + W]
                dve.scalar_tensor_tensor(out=xs, in0=ps[:, 2 + i % 2, :], scalar=gate_col[:, i // 2:i // 2 + 1],
                                         in1=xs, op0=ALU.mult, op1=ALU.add).then_inc(scatter_added, 1)

            fits = few(dve)
            dve.wait_ge(iota_ready, 3)
            link(dve.memset(placeT[:].bitcast(F32), 0.0))
            dve.memset(gate_col[:], 0.0).then_inc(gate_ready, 1)
            with dve.If(fits):
                make_place()
                gathered_low()
                with dve.Fori(0, NE) as e:
                    pos = [0]

                    def to(n):
                        while pos[0] < min(n, PER):
                            split(U_MOE + pos[0], e)
                            pos[0] += 1

                    to(2)
                    y_low(e)
                    for c, (g_end, u_end, d_end) in enumerate(GB):
                        to(u_end + 1)
                        dve.wait_ge(units_used, at(U_MOE + u_end, e, PER))
                        dve.wait_ge(g_silu_done, at(c + 1, e, NC))
                        if c:
                            dve.wait_ge(g_hT_done, at(c, e, NC))
                        dve.tensor_tensor(work[:, 1, 0:W], work[:, 0, 0:W], ps[:, 4 + (2 * c + 1) % 3, :], ALU.mult)\
                            .then_inc(g_h_done, 1)
                        if c < 2:
                            add_scattered(2 * c, e)
                            add_scattered(2 * c + 1, e)
                        if c == 3:
                            dve.wait_ge(scatter_added, at(4, e, 4))
                            dve.tensor_copy(gate_col[:], rgate[:, :, bass.ds(e, 1)].rearrange("p t o -> p (t o)"))\
                                .then_inc(gate_ready, 1)
                        if c == 4:
                            dve.wait_ge(placeT_done, at(1, e, 1))
                            make_place(e)
                        to(d_end + 2)
                        dve.wait_ge(g_hT_hi_ready, at(c + 1, e, NC))
                        dve.tensor_tensor(hT_lo[:, :, 0:P], ps[:, 7, :].rearrange("p (j q) -> p j q", q=P),
                                          hT_hi[:, :, 0:P].bitcast(F32), ALU.subtract).then_inc(g_hT_ready, 1)
                    to(PER)
                    gathered_low(e)
                y_low()
                for i in range(4):
                    add_scattered(i)
                dve.wait_ge(scatter_added, 4 * NE + 4)
            with dve.Else():
                with dve.Fori(0, NE) as e:
                    ffn(MOE_CHUNKS, U_MOE, e, len(FFN_CHUNKS))
                dve.wait_ge(y_added, NE + 1)
            norm(4, 6)

        @block.tensor
        def _(pe):
            used = [0]

            def take(n, e=None):
                pe.wait_ge(lo_ready, at(n + 1, e, PER))

            def three(out, s_hi, s_lo, m_hi, m_lo, start, stop):
                pe.matmul(out, s_hi, m_hi, start=start, stop=False, skip_group_check=True)
                pe.matmul(out, s_hi, m_lo, start=False, stop=False, skip_group_check=True)
                return pe.matmul(out, s_lo, m_hi, start=False, stop=stop, skip_group_check=True)

            def project_T(first, blocks, bank, extra=None):
                for q in range(2):
                    n = first + q
                    take(n)
                    wh, wl = unit3(hi, n), unit3(lo, n)
                    for i in range(blocks):
                        out = ps[:, bank + i // 2, SEQ * (i % 2):SEQ * (i % 2) + SEQ]
                        cols = slice(P * i, P * i + P)
                        for k in range(4):
                            ins = three(out, wh[:, k, cols], wl[:, k, cols], xT_hi[:, 4 * q + k, :],
                                        xT_lo[:, 4 * q + k, :], q == 0 and k == 0 and i % 2 == 0, q == 1 and k == 3)
                    if extra:
                        c0, cn = extra
                        for t in range(T):
                            out = ps[:, bank + (blocks - 1) // 2, SEQ + cn * t:SEQ + cn * t + cn]
                            for k in range(4):
                                ts = slice(P * t, P * t + P)
                                ins = three(out, xT_hi[:, 4 * q + k, ts], xT_lo[:, 4 * q + k, ts],
                                            wh[:, k, c0:c0 + cn], wl[:, k, c0:c0 + cn], False, q == 1 and k == 3)
                    ins.then_inc(units_used, 1)

            def project(first, banks):
                for q in range(2):
                    n = first + q
                    take(n)
                    wh, wl = unit3(hi, n), unit3(lo, n)
                    for t in range(T):
                        ts = slice(P * t, P * t + P)
                        for k in range(4):
                            ins = three(ps[:, banks[t], :], xT_hi[:, 4 * q + k, ts], xT_lo[:, 4 * q + k, ts],
                                        wh[:, k, :], wl[:, k, :], q == 0 and k == 0, q == 1 and k == 3)
                    ins.then_inc(units_used, 1)

            def transpose_x(i):
                pe.wait_ge(xs_ready, 2 * i + 2)
                for b in range(4):
                    for k in range(2):
                        for t in range(T):
                            o = k * SEQ + t * P
                            ins = pe.transpose(ps[:, b, o:o + P], work[:, t, 2 * b + k::KD], ident[:])
                    ins.then_inc(xT_done, 1)
                pe.wait_ge(xT_ready, 4 * i + 4)

            pe.wait_ge(buckets_loaded, 32)
            pe.matmul(ps[0:CH, 7, 0:SEQ + P], rel_sb[:], bucket_sb[:], start=True, stop=True).then_inc(diag_done, 1)
            pe.wait_ge(ident_ready, 2)
            transpose_x(0)
            project_T(0, 3, 0, (384, 16))
            project_T(2, 4, 2)
            pe.wait_ge(hankel_loaded, 16)
            pe.wait_ge(flip_ready, 2)
            pe.wait_ge(diag_copied, 1)
            for a in range(4):
                for h in range(2):
                    ins = pe.matmul(ps[:, 4 + a, SEQ * h:SEQ * h + SEQ], flip[:], hankel[:, 2 * a + h, :],
                                    start=True, stop=True)
                ins.then_inc(bias_flipped, 1)
            pe.wait_ge(bias_copied, 4)
            project(4, (4, 5))
            pe.wait_ge(proj_copied, 2)
            for i, t in enumerate((1, 0)):
                n = P * (t + 1)
                if i:
                    pe.wait_ge(idx_relu, i)
                for h in range(4):
                    p0 = IDX_DIM * (h % 2)
                    ins = pe.matmul(score_psum(6, n)[:, 2 * (h % 2) + h // 2, :],
                                    iqT[p0:p0 + IDX_DIM, h // 2, P * t:P * t + P], ikT[p0:p0 + IDX_DIM, 0:n],
                                    start=True, stop=True)
                ins.then_inc(idx_done, 1)
            pe.wait_ge(proj_copied, 3)
            project_T(6, 4, 2)
            pe.wait_ge(small_copied, 1)
            project_T(8, 4, 0)
            pe.wait_ge(lat_ready, 2)
            for k in range(2):
                for t in range(T):
                    ins = pe.transpose(ps[:, 4, k * SEQ + t * P:k * SEQ + t * P + P], tok[:, t, k:RANK:2], ident[:])
            ins.then_inc(latT_done, 1)
            pe.wait_ge(latT_copied, 1)
            pe.wait_ge(small_loaded, 16 * 6)
            for k in range(2):
                pe.matmul(ps[:, 5, 0:SEQ], wuk[:, k, :], latT[:, k, :], start=(k == 0), stop=(k == 1))
            for t in range(T):
                for k in range(2):
                    ins = pe.matmul(ps[:, 5, SEQ + HD * t:SEQ + HD * t + HD], latT[:, k, P * t:P * t + P], wuv[:, k, :],
                                    start=(k == 0), stop=(k == 1))
            ins.then_inc(akv_done, 1)
            pe.wait_ge(small_loaded, 16 * 6)
            pe.wait_ge(idx_relu, 2)
            for j in range(2):
                ins = pe.transpose(ps[:, 7, CMP_LEN * j:CMP_LEN * j + CMP_LEN], pos_sb[:, j, :],
                                   ident[0:CMP_LEN, 0:CMP_LEN])
            ins.then_inc(pos_done, 1)
            for j in range(2):
                pe.wait_ge(blk_ready, j + 1)
                for q in range(2):
                    n = U_CMP + 2 * j + q
                    take(n)
                    wh, wl = unit3(hi, n), unit3(lo, n)
                    for l in range(16):
                        ins = three(ps[:, 7, 64 + NCP * j:64 + NCP * j + NCP], wh[:, l, :], wl[:, l, :],
                                    blk_hi[:, j, 16 * q + l, :], blk_lo[:, j, 16 * q + l, :],
                                    q == 0 and l == 0 and j == 0, q == 1 and l == 15)
                    ins.then_inc(units_used, 1)
            pe.wait_ge(hid_ready, 1)
            pe.wait_ge(akv_copied, 2)
            pe.matmul(ps[:, 4, 0:NCMP], w2[:, 0, :], hid[:, 0, 0:NCMP], start=True, stop=True)
            pe.matmul(ps[0:NCMP, 5, 0:HD], hid[:, 1, 0:NCMP], w2[:, 1, :], start=True, stop=True)\
                .then_inc(ckv_done, 1)
            pe.wait_ge(ckv_copied, 2)
            pe.wait_ge(proj_copied, 7)

            def scores(b):
                kind, t = BATCH[b]
                n = keys(b)
                if b >= 2:
                    pe.wait_ge(logits_ready, b - 1)
                kT = {"dsa": akT, "sel": skT, "win": wkT, "cmp": ckT}[kind]
                out = score_psum(2 * (b % 2), n)
                for h in range(4):
                    hq = h if kind == "dsa" else AH + h
                    ins = pe.matmul(out[:, h, :], qT[:, hq, P * t:P * t + P], kT[:, 0:n], start=True, stop=True)
                ins.then_inc(scores_done, 1)

            def transpose_probs(b, b_tile, n, bank):
                for c in range(max(n // P, 1)):
                    m = min(n, P)
                    for h in range(4):
                        ins = pe.transpose(ps[0:m, bank + c, P * h:P * h + P], prob_tile(b_tile, n)[:, h, P * c:P * c + m],
                                           ident[:])
                ins.then_inc(probT_done, 1)

            scores(0)
            scores(1)
            for b in range(NBATCH):
                kind, t = BATCH[b]
                n, g = keys(b), GROUP[b]
                pe.wait_ge(probs_ready, b + 1)
                transpose_probs(b, b, n, 4)
                if b + 2 < NBATCH:
                    scores(b + 2)
                first = b == 0 or GROUP[b - 1] != g
                if first and g >= 2:
                    pe.wait_ge(oT_ready, g - 1)
                pe.wait_ge(probT_copied, b + 1)
                for c in range(max(n // P, 1)):
                    m = min(n, P)
                    val = {"dsa": av[:, c, :], "sel": tok[:, c, RANK:RANK + HD],
                           "win": tok[:, c, RANK + HD:W], "cmp": cv[0:min(m, NCMP), :]}[kind]
                    ins = pe.matmul(ps[:, 6 + g % 2, :], val, probT[0:m, c].rearrange("p h q -> p (h q)"),
                                    start=(first and c == 0), stop=(b + 1 == NBATCH or GROUP[b + 1] != g),
                                    skip_group_check=True)
                ins.then_inc(pv_done, 1)

            def project_out(layer):
                pe.wait_ge(oT_ready, 4 * layer + 4)
                for n in range(2):
                    project(U_WO[layer] + 2 * n, (2 * n, 2 * n + 1))

            project_out(0)
            transpose_x(1)

            def ffn(chunks, first, e=None, cbase=0):
                ends = bounds(chunks)
                cu = chunk_units(chunks)
                per_c = T * len(chunks)

                def bank_free(c, i):
                    gi = 4 * c + i - 3
                    if gi < 0:
                        return
                    pc, pi = gi // 4, gi % 4
                    pe.wait_ge(silu_done if pi < 2 else h_done, at(T * (cbase + pc) + pi % 2 + 1, e, per_c))

                def gate_or_up(c, base, i0, start_n):
                    w = chunks[c][1]
                    nk = UNIT // w
                    for q in range(cu[c][0]):
                        n = first + start_n + q
                        take(n, e)
                        wh, wl = unit3(hi, n), unit3(lo, n)
                        for t in range(T):
                            if q == 0:
                                bank_free(c, i0 + t)
                            out = ps[:, 4 + (4 * c + i0 + t) % 3, 0:w]
                            ts = slice(P * t, P * t + P)
                            for kk in range(nk):
                                k = nk * q + kk
                                ins = three(out, xT_hi[:, k, ts], xT_lo[:, k, ts], wh[:, kk, :], wl[:, kk, :],
                                            k == 0, k == KD - 1)
                        ins.then_inc(units_used, 1)

                def transpose_h(c, t):
                    w = chunks[c][1]
                    nj = w // P
                    i = T * (cbase + c) + t
                    pe.wait_ge(h_done, at(i + 1, e, per_c))
                    if i or e is not None:
                        pe.wait_ge(hT_ready, at(i, e, per_c))
                    for j in range(nj):
                        ins = pe.transpose(ps[:, 7, P * j:P * j + P], work[:, 1, W * t + j:W * t + w:nj], ident[:])
                    ins.then_inc(hT_done, 1)

                def down(c, start_n):
                    w = chunks[c][1]
                    pe.wait_ge(hT_ready, at(T * (cbase + c) + T, e, per_c))
                    for q in range(cu[c][1]):
                        n = first + start_n + q
                        take(n, e)
                        wh, wl = unit3(hi, n), unit3(lo, n)
                        for jj in range(2):
                            j = 2 * q + jj
                            for t in range(T):
                                ts = slice(P * t, P * t + P)
                                for m in range(2):
                                    cols = slice(W * m, W * m + W)
                                    ins = three(ps[:, 2 * t + m, :], hT_hi[:, j, ts], hT_lo[:, j, ts],
                                                wh[:, jj, cols], wl[:, jj, cols], c == 0 and j == 0,
                                                c == len(chunks) - 1 and j == w // P - 1)
                        ins.then_inc(units_used, 1)

                for c, (g_end, u_end, d_end) in enumerate(ends):
                    gate_or_up(c, 0, 0, g_end - cu[c][0])
                    if c:
                        transpose_h(c - 1, 1)
                    gate_or_up(c, 0, 2, g_end)
                    if c:
                        if c == 1 and e is not None:
                            pe.wait_ge(y_added, at(1, e, 1))
                        down(c - 1, u_end)
                    transpose_h(c, 0)
                transpose_h(len(chunks) - 1, 1)
                down(len(chunks) - 1, ends[-1][2])

            ffn(FFN_CHUNKS, U_FFN)
            transpose_x(2)
            for g in range(4):
                project_T(U_QKV + 2 * g, 4, 2 * g)
            pe.wait_ge(proj_copied, 9)
            project(U_QKV + 8, (0, 1))
            project(U_QKV + 10, (2, 3))

            def stick_scores(b):
                t, g = STICK[b]
                n = P * (t + 1)
                if b == 0:
                    pe.wait_ge(proj_copied, 11)
                if b >= 2:
                    pe.wait_ge(sticks_done, b - 1)
                out = score_psum(4 + 2 * (b % 2), n)
                for h in range(4):
                    hd = 4 * g + h
                    ins = pe.matmul(out[:, h, :], qT[:, hd, P * t:P * t + P], bias_kT[:, hd, 0:n], start=True, stop=True)
                ins.then_inc(z_done, 1)

            stick_scores(0)
            stick_scores(1)
            for b in range(NSTICK):
                t, g = STICK[b]
                n = P * (t + 1)
                if b == 0:
                    pe.wait_ge(proj_copied, 13)
                pe.wait_ge(stick_masked, b + 1)
                for c in range(n // P):
                    for h in range(4):
                        ins = pe.transpose(ps[:, c, P * h:P * h + P], prob_tile(b, n)[:, h, P * c:P * c + P], ident[:])
                ins.then_inc(probT_done, 1)
                if b + 2 < NSTICK:
                    stick_scores(b + 2)
                if b >= 2:
                    pe.wait_ge(oT_ready, 4 + b - 1)
                pe.wait_ge(probT_copied, NBATCH + b + 1)
                for h in range(4):
                    hd = 4 * g + h
                    for c in range(n // P):
                        ins = pe.matmul(ps[:, 2 + b % 2, P * h:P * h + P], v1[:, c, HD * hd:HD * hd + HD],
                                        probT[:, c, h, :], start=(h == 0 and c == 0), stop=(h == 3),
                                        skip_group_check=True)
                ins.then_inc(pv_done, 1)
            project_out(1)
            transpose_x(3)
            pe.wait_ge(wr_ready, 1)
            for t in range(T):
                ts = slice(P * t, P * t + P)
                for k in range(KD):
                    ins = three(ps[:, 4, NE * t:NE * t + NE], xT_hi[:, k, ts], xT_lo[:, k, ts], wr_hi[:, k, :],
                                wr_lo[:, k, :], k == 0 and t == 0, k == KD - 1)
            ins.then_inc(logit_done, 1)
            pe.wait_ge(picks_ready, 2)
            pe.wait_ge(iota_ready, 3)
            pk = [rpick[:, t, 0:NE] for t in range(T)]
            pe.matmul(ps[:, 4, 16:24], before[:], pk[0], start=True, stop=True)
            pe.matmul(ps[:, 4, 24:32], before[:], pk[1], start=True, stop=False)
            pe.matmul(ps[:, 4, 24:32], ones[:, 0:P], pk[0], start=False, stop=True)
            pe.matmul(ps[:, 4, 32:40], ones[:, 0:P], pk[0], start=True, stop=False)
            pe.matmul(ps[:, 4, 32:40], ones[:, 0:P], pk[1], start=False, stop=True).then_inc(places_done, 1)

            def gather(e=None):
                pe.wait_ge(place_ready, at(1 if e is None else 2, e, 1))
                if e is None:
                    pe.wait_ge(xs_lo_ready, 1)
                else:
                    pe.wait_ge(placeT_ready, at(1, e, 1))
                for k in range(KD):
                    out = ps[:, 2 + k // 4, P * (k % 4):P * (k % 4) + P]
                    for t in range(T):
                        for part in (xs_hi, xs_lo):
                            ins = pe.matmul(out, part[:, t, k::KD], place[:, t, :], start=(t == 0 and part is xs_hi),
                                            stop=(t == T - 1 and part is xs_lo))
                    if k % 4 == 3:
                        ins.then_inc(gathered, 1)

            def scatter(i, e=None):
                first = 0 if e is not None else 4 * NE
                if i == 0:
                    pe.wait_ge(y_ready, at(1 if e is not None else NE + 1, e, 1))
                    pe.wait_ge(gate_ready, at(1 if e is not None else NE + 1, e, 1))
                if i >= 2:
                    pe.wait_ge(scatter_added, at(first + i - 1, e, 4))
                cols = slice(W * (i % 2), W * (i % 2) + W)
                to_tok = placeT[:, P * (i // 2):P * (i // 2) + P]
                pe.matmul(ps[:, 2 + i % 2, :], to_tok, y_hi[:, cols], start=True, stop=False)
                pe.matmul(ps[:, 2 + i % 2, :], to_tok, y_lo[:, cols], start=False, stop=True).then_inc(scattered, 1)

            fits = few(pe)
            with pe.If(fits):
                gather()
                with pe.Fori(0, NE) as e:
                    def columns(c, base, which):
                        gi = 2 * c + which
                        if gi >= 3:
                            pc, pw = (gi - 3) // 2, (gi - 3) % 2
                            pe.wait_ge(g_h_done if pw else g_silu_done, at(pc + 1, e, NC))
                        for q in range(2):
                            n = U_MOE + base + q
                            take(n, e)
                            wh, wl = unit3(hi, n), unit3(lo, n)
                            for kk in range(4):
                                k = 4 * q + kk
                                ins = three(ps[:, 4 + gi % 3, :], xg_hi[:, k, :], xg_lo[:, k, :], wh[:, kk, :],
                                            wl[:, kk, :], k == 0, k == KD - 1)
                            ins.then_inc(units_used, 1)

                    def rows(c, base):
                        pe.wait_ge(g_hT_ready, at(c + 1, e, NC))
                        for q in range(2):
                            n = U_MOE + base + q
                            take(n, e)
                            wh, wl = unit3(hi, n), unit3(lo, n)
                            for jj in range(2):
                                j = 2 * q + jj
                                for m in range(2):
                                    cols = slice(W * m, W * m + W)
                                    ins = three(ps[:, m, :], hT_hi[:, j, 0:P], hT_lo[:, j, 0:P], wh[:, jj, cols],
                                                wl[:, jj, cols], c == 0 and j == 0, c == NC - 1 and j == 3)
                            ins.then_inc(units_used, 1)

                    pe.wait_ge(xg_ready, at(2, e, 2))
                    for c, (g_end, u_end, d_end) in enumerate(GB):
                        columns(c, g_end - 2, 0)
                        columns(c, g_end, 1)
                        if c < 2:
                            scatter(2 * c, e)
                            scatter(2 * c + 1, e)
                        if c == 2:
                            pe.wait_ge(scatter_added, at(3, e, 4))
                            for t in range(T):
                                ins = pe.transpose(ps[:, 2, P * t:P * t + P], place[:, t, :].bitcast(F32), ident[:])
                            ins.then_inc(placeT_done, 1)
                        if c:
                            rows(c - 1, u_end)
                        pe.wait_ge(g_h_done, at(c + 1, e, NC))
                        for j in range(4):
                            ins = pe.transpose(ps[:, 7, P * j:P * j + P], work[:, 1, j:W:4], ident[:])
                        ins.then_inc(g_hT_done, 1)
                    gather(e)
                    rows(NC - 1, GB[-1][2])
                for i in range(4):
                    scatter(i)
            with pe.Else():
                with pe.Fori(0, NE) as e:
                    ffn(MOE_CHUNKS, U_MOE, e, len(FFN_CHUNKS))


_INS = ['x', 'rel_bias', 'ev_norm_mix', 'ev_w_in', 'ev_kv_norm', 'ev_w_uk', 'ev_w_uv', 'ev_cmp_pos', 'ev_cmp_w1',
        'ev_cmp_w2', 'ev_w_out', 'ev_norm_ffn', 'ev_w_gate', 'ev_w_up', 'ev_w_down', 'od_norm_mix', 'od_w_qkv',
        'od_w_out', 'od_norm_ffn', 'od_w_router', 'od_w_gate', 'od_w_up', 'od_w_down', 'final_norm']


def kernel(**inputs):
    import numpy as _np
    import concourse.bacc as _bacc
    from concourse import mybir as _mybir
    from concourse.bass_utils import run_bass_kernel_spmd as _run

    nc = _bacc.Bacc("TRN2", target_bir_lowering=False, num_devices=1)
    arrays, args = {}, []
    for name in _INS:
        a = _np.ascontiguousarray(inputs[name])
        arrays[f"in_{name}_dram"] = a
        args.append(nc.dram_tensor(f"in_{name}_dram", a.shape, _mybir.dt.from_np(a.dtype), kind="ExternalInput").ap())
    out = nc.dram_tensor("out_0_dram", (1, SEQ, D), _mybir.dt.from_np(_np.dtype("float32")), kind="ExternalOutput").ap()
    build(nc, *args, out)
    r = _run(nc, [arrays], core_ids=[0])
    return r.results[0]["out_0_dram"]
```

```python
from contextlib import ExitStack

import numpy as np

import concourse.bass as bass
from concourse import mybir

F32 = mybir.dt.float32
F32R = mybir.dt.float32r
ALU = mybir.AluOpType
ACT = mybir.ActivationFunctionType
AX = mybir.AxisListType

P = 128
SEQ = 256
D = 1024
KD = D // P
T = SEQ // P
HD = 128
AH = BH = 4
CH = 8
RANK = 256
IDX_DIM = 64
NB = 32
MAX_DIST = 128
CMP_LEN, CMP_STRIDE = 32, 16
NCMP = (SEQ - CMP_LEN) // CMP_STRIDE + 1
NCP = NCMP + 1
TOPK = min(256, SEQ // 4)
FF = 2816
EFF = 3584
NE = 8
EPS = 1e-6
NEG = -1e30
UNSEEN = -1e38
TAKEN = -3e38
SCALE = HD ** -0.5
W = 512

O_AQ = 0
O_LAT = O_AQ + AH * HD
O_IQ = O_LAT + RANK
O_IK = O_IQ + 4 * IDX_DIM
O_IW = O_IK + IDX_DIM
O_BQ = O_IW + 4
O_KV = O_BQ + BH * HD
O_BG = O_KV + 6 * HD

UNIT = 2048
R = 6
H = 3

FFN_CHUNKS = [(f, min(W, FF - f)) for f in range(0, FF, W)]
MOE_CHUNKS = [(f, min(W, EFF - f)) for f in range(0, EFF, W)]


def bucket_rows():
    dist = np.arange(SEQ)
    half = NB // 2
    large = half + (np.log(np.maximum(dist, 1).astype(np.float32) / half)
                    / np.float32(np.log(MAX_DIST / half)) * (NB - half)).astype(np.int32)
    bucket = np.where(dist < half, dist, np.minimum(large, NB - 1))
    rows = np.zeros((NB, SEQ + P), np.float32)
    rows[bucket[::-1], np.arange(SEQ)] = 1.0
    return rows


def chunk_units(chunks):
    return [(2, 2) if w == W else (1, 1) for _, w in chunks]


def ffn_order(chunks):
    order = []
    cu = chunk_units(chunks)
    for c in range(len(chunks) + 1):
        if c < len(chunks):
            order += [("gate", c, q) for q in range(cu[c][0])] + [("up", c, q) for q in range(cu[c][0])]
        if c:
            order += [("down", c - 1, q) for q in range(cu[c - 1][1])]
    return order


def bounds(chunks):
    cu, n, out = chunk_units(chunks), 0, []
    for c in range(len(chunks)):
        g = n + cu[c][0]
        u = g + cu[c][0]
        n = u + (cu[c - 1][1] if c else 0)
        out.append((g, u, n))
    return out


def at(const, e=None, per=0):
    return const if e is None else e * per + const


def build(nc, x_d, rel_bias, ev_norm_mix, ev_w_in, ev_kv_norm, ev_w_uk, ev_w_uv, ev_cmp_pos, ev_cmp_w1,
          ev_cmp_w2, ev_w_out, ev_norm_ffn, ev_w_gate, ev_w_up, ev_w_down, od_norm_mix, od_w_qkv, od_w_out,
          od_norm_ffn, od_w_router, od_w_gate, od_w_up, od_w_down, final_norm, out_d):
    win = ev_w_in[0].rearrange("(p k) n -> p k n", k=KD)

    def k_units(view, parts, width):
        return [([(view[:, 4 * q:4 * q + 4, s:s + n], d, n) for s, d, n in parts], 4, width) for q in range(2)]

    units = []
    units += k_units(win, [(O_IQ, 0, 320), (O_IK, 320, 64), (O_IW, 384, 4), (O_BG, 388, 12)], 400)
    units += k_units(win, [(O_AQ, 0, W)], W)
    units += k_units(win, [(O_LAT, 0, RANK), (O_KV + 3 * HD, 256, HD), (O_KV + 5 * HD, 384, HD)], W)
    units += k_units(win, [(O_BQ, 0, W)], W)
    units += k_units(win, [(O_KV, 0, 3 * HD), (O_KV + 4 * HD, 3 * HD, HD)], W)
    U_CMP = len(units)
    for j in range(2):
        w1 = ev_cmp_w1[0, j].rearrange("(l p) n -> p l n", p=P)
        units += [([(w1[:, 16 * q:16 * q + 16], 0, HD)], 16, HD) for q in range(2)]
    U_WO = [0, 0]
    U_WO[0] = len(units)

    def out_units(w):
        v = w.rearrange("(h p) n -> p h n", p=P)
        return [u for n in range(2) for u in k_units(v, [(W * n, 0, W)], W)]

    units += out_units(ev_w_out[0])
    U_FFN = len(units)
    gate_v, up_v = (w[0].rearrange("(p k) f -> p k f", k=KD) for w in (ev_w_gate, ev_w_up))
    for kind, c, q in ffn_order(FFN_CHUNKS):
        f, w = FFN_CHUNKS[c]
        if kind == "down":
            v = ev_w_down[0, f:f + w].rearrange("(p j) n -> p j n", j=w // P)
            units.append(([(v[:, 2 * q:2 * q + 2], 0, D)], 2, D))
        else:
            v = gate_v if kind == "gate" else up_v
            ks = slice(4 * q, 4 * q + 4) if w == W else slice(0, KD)
            units.append(([(v[:, ks, f:f + w], 0, w)], UNIT // w, w))
    U_QKV = len(units)
    qkv_v = od_w_qkv[0].rearrange("(p k) n -> p k n", k=KD)
    for g in range(3 * D // W):
        units += k_units(qkv_v, [(W * g, 0, W)], W)
    U_WO[1] = len(units)
    units += out_units(od_w_out[0])
    U_MOE = len(units)
    moe_order = ffn_order(MOE_CHUNKS)
    PER = len(moe_order)
    assert PER % R == 0 and PER % H == 0
    moe_gate, moe_up = (w.rearrange("o e (p k) f -> (o e) p k f", k=KD) for w in (od_w_gate, od_w_up))
    moe_down = od_w_down.rearrange("o e (c p j) n -> (o e) c p j n", p=P, j=W // P)

    landed_at = []
    slot_total = [0] * R
    for n, (pieces, _, _) in enumerate(units):
        slot_total[n % R] += 16 * len(pieces)
        landed_at.append(slot_total[n % R])

    def landed(n):
        if n < U_MOE:
            return landed_at[n]
        return slot_total[n % R] + 16 * len([m for m in range(U_MOE, n + 1) if m % R == n % R])

    def shape_of(n):
        if n < U_MOE:
            return units[n][1:]
        return (2, D) if moe_order[(n - U_MOE) % PER][0] == "down" else (4, W)

    buckets_d = nc.inline_tensor(bucket_rows(), "bucket_rows").ap()
    diag_d = nc.dram_tensor("bias_by_distance", [CH, SEQ + P], F32).ap()

    with ExitStack() as ctx:
        def sb(name, shape, dt=F32):
            return ctx.enter_context(nc.sbuf_tensor(name, shape, dt))

        def sem(name):
            return ctx.enter_context(nc.semaphore(name))

        raw = sb("raw", [P, R, UNIT])
        hi = sb("hi", [P, H, UNIT], F32R)
        lo = sb("lo", [P, H, UNIT], F32R)
        x = sb("x", [P, T, D])
        work = sb("work", [P, 4, D])
        probT_at = nc.sbuf_base
        probT = sb("probT", [P, T, 4, P])
        bucket_sb = nc.alloc_sbuf_tensor_at("bucket_sb", [NB, SEQ + P], F32, offset=probT_at)
        diag_sb = nc.alloc_sbuf_tensor_at("diag_sb", [CH, SEQ + P], F32, offset=probT_at + 4 * (SEQ + P))
        xT_hi = sb("xT_hi", [P, KD, SEQ], F32R)
        xT_lo = sb("xT_lo", [P, KD, SEQ], F32R)
        gain = sb("gain", [P, 2, D])
        arena_at = nc.sbuf_base
        sb("arena", [P, 2 * KD * SEQ])
        qT = nc.alloc_sbuf_tensor_at("qT", [P, 8, SEQ], F32, offset=arena_at)
        bias_kT = nc.alloc_sbuf_tensor_at("bias_kT", [P, 8, SEQ], F32, offset=arena_at + 4 * KD * SEQ)
        xs_hi = nc.alloc_sbuf_tensor_at("xs_hi", [P, T, D], F32R, offset=arena_at)
        xs_lo = nc.alloc_sbuf_tensor_at("xs_lo", [P, T, D], F32R, offset=arena_at + 4 * KD * SEQ)
        kv = sb("kv", [P, 9 * SEQ])
        tok = sb("tok", [P, T, W])
        latT = sb("latT", [P, T, SEQ])
        hT_at = nc.sbuf_base
        hT_hi = sb("hT_hi", [P, 4, SEQ], F32R)
        hT_lo = sb("hT_lo", [P, 4, SEQ], F32R)
        sb("blk_tail", [P, P])
        blk = nc.alloc_sbuf_tensor_at("blk", [P, 4 * CMP_LEN * NCP + P], F32R, offset=hT_at)
        iscore = sb("iscore", [P, T, SEQ])
        ident = sb("ident", [P, P])
        flip = sb("flip", [P, P])
        rel_sb = sb("rel_sb", [NB, CH])
        wuk = sb("wuk", [P, 2, HD])
        wuv = sb("wuv", [P, 2, HD])
        w2 = sb("w2", [P, 2, HD])
        pos_sb = sb("pos_sb", [CMP_LEN, 2, HD])
        posT = sb("posT", [P, 2, CMP_LEN])
        kv_gain = sb("kv_gain", [P, RANK])
        wr = sb("wr", [P, KD, NE])
        wr_hi = sb("wr_hi", [P, KD * NE + P], F32R)
        wr_lo = sb("wr_lo", [P, KD * NE + P], F32R)
        small = sb("small", [P, T, 16])
        gates = sb("gates", [P, T, 12])
        stat = sb("stat", [P, 8])
        hid = sb("hid", [NCP, 2 * HD])
        hidT = sb("hidT", [P, 2, NCP])
        ckT = sb("ckT", [P, NCP])
        cv = sb("cv", [NCP, HD])
        negmax = sb("negmax", [P, 2, 4])
        expsum = sb("expsum", [P, 2, 4])
        inv = sb("inv", [P, 2, 4])
        top8 = sb("top8", [P, 8])
        rlog = sb("rlog", [P, T, 16])
        rsel = sb("rsel", [P, T, 16])
        rexp = sb("rexp", [P, T, NE])
        rtop = sb("rtop", [P, T, 8])
        rneg = sb("rneg", [P, T])
        rsum = sb("rsum", [P, T])
        rgate = sb("rgate", [P, T, 16])
        rpick = sb("rpick", [P, T, 16])
        rplace = sb("rplace", [P, T, 16])
        rcount = sb("rcount", [P, NE])
        most = sb("most", [1, 1])
        most_i = sb("most_i", [1, 1], mybir.dt.int32)
        iota = sb("iota", [P, P])
        before = sb("before", [P, P])
        place = sb("place", [P, T, P], F32R)
        placeT = sb("placeT", [P, SEQ], F32R)
        gate_col = sb("gate_col", [P, T])
        ones = sb("ones", [P, SEQ])
        root = sb("root", [P, 1])
        ps = ctx.enter_context(nc.psum_tensor("ps", [P, 8, W], F32))

        iqT = kv[:, 0:2 * SEQ].rearrange("p (b s) -> p b s", b=2)
        ikT = kv[:, 2 * SEQ:3 * SEQ]
        akT = kv[:, 3 * SEQ:4 * SEQ]
        skT = kv[:, 4 * SEQ:5 * SEQ]
        wkT = kv[:, 5 * SEQ:6 * SEQ]
        av = kv[:, 6 * SEQ:7 * SEQ].rearrange("p (t d) -> p t d", t=T)
        rawT = kv[:, 7 * SEQ:9 * SEQ].rearrange("p (j s) -> p j s", j=2)
        v1 = kv[:, 0:T * D].rearrange("p (t d) -> p t d", t=T)
        hid2, hid3 = latT[0:NCP, 0, :], latT[0:NCP, 1, :]

        rlogT = latT[0:NE, 0, :]

        def blk_part(part, j):
            first = (2 * part + j) * CMP_LEN * NCP
            return blk[:, first:first + CMP_LEN * NCP]

        def blk_window(part, j, place):
            first = ((2 * part + j) * CMP_LEN + place) * NCP
            return blk[:, first:first + P]

        xg_hi, xg_lo = (h[:, 0:4, :].rearrange("p a (b s) -> p (a b) s", s=P) for h in (xT_hi, xT_lo))
        y_hi, y_lo = (h[:, 4:8, :].rearrange("p a s -> p (a s)") for h in (xT_hi, xT_lo))
        topw = kv[:, 0:SEQ]
        hankel = work[:, 2:4, :].rearrange("p a (b s) -> p (a b) s", s=SEQ)

        raw_landed = [sem(f"raw_landed{i}") for i in range(R)]
        hi_ready = sem("hi_ready")
        lo_ready = sem("lo_ready")
        units_used = sem("units_used")
        x_loaded = sem("x_loaded")
        gain_loaded = [sem(f"gain_loaded{i}") for i in range(5)]
        buckets_loaded = sem("buckets_loaded")
        small_loaded = sem("small_loaded")
        ident_ready = sem("ident_ready")
        flip_ready = sem("flip_ready")
        var_ready = sem("var_ready")
        std_ready = sem("std_ready")
        xs_ready = sem("xs_ready")
        xT_done = sem("xT_done")
        xT_hi_ready = sem("xT_hi_ready")
        xT_ready = sem("xT_ready")
        diag_done = sem("diag_done")
        diag_copied = sem("diag_copied")
        diag_stored = sem("diag_stored")
        hankel_loaded = sem("hankel_loaded")
        bias_flipped = sem("bias_flipped")
        bias_copied = sem("bias_copied")
        bias_masked = sem("bias_masked")
        proj_copied = sem("proj_copied")
        small_copied = sem("small_copied")
        gates_ready = sem("gates_ready")
        gates_masked = sem("gates_masked")
        lat_ready = sem("lat_ready")
        latT_done = sem("latT_done")
        latT_copied = sem("latT_copied")
        akv_done = sem("akv_done")
        akv_copied = sem("akv_copied")
        idx_done = sem("idx_done")
        idx_relu = sem("idx_relu")
        idx_summed = sem("idx_summed")
        idx_masked = sem("idx_masked")
        pos_done = sem("pos_done")
        pos_copied = sem("pos_copied")
        blk_made = sem("blk_made")
        blk_hi_ready = sem("blk_hi_ready")
        blk_ready = sem("blk_ready")
        gelu_arg = sem("gelu_arg")
        gelu_exp = sem("gelu_exp")
        hid_ready = sem("hid_ready")
        hidT_done = sem("hidT_done")
        hidT_copied = sem("hidT_copied")
        ckv_done = sem("ckv_done")
        ckv_copied = sem("ckv_copied")
        scores_done = sem("scores_done")
        logits_ready = sem("logits_ready")
        exps_done = sem("exps_done")
        probs_ready = sem("probs_ready")
        probT_done = sem("probT_done")
        probT_copied = sem("probT_copied")
        pv_done = sem("pv_done")
        oT_hi_ready = sem("oT_hi_ready")
        oT_ready = sem("oT_ready")
        x_added = sem("x_added")
        squares_done = sem("squares_done")
        silu_done = sem("silu_done")
        h_done = sem("h_done")
        hT_done = sem("hT_done")
        hT_hi_ready = sem("hT_hi_ready")
        hT_ready = sem("hT_ready")
        z_done = sem("z_done")
        rest_ready = sem("rest_ready")
        beta_ready = sem("beta_ready")
        rest_masked = sem("rest_masked")
        sticks_done = sem("sticks_done")
        stick_masked = sem("stick_masked")
        wr_hi_ready = sem("wr_hi_ready")
        wr_ready = sem("wr_ready")
        logitT_done = sem("logitT_done")
        logitT_copied = sem("logitT_copied")
        logit_done = sem("logit_done")
        router_max = sem("router_max")
        router_exp = sem("router_exp")
        y_added = sem("y_added")
        iota_ready = sem("iota_ready")
        ones_ready = sem("ones_ready")
        xs_hi_ready = sem("xs_hi_ready")
        xs_lo_ready = sem("xs_lo_ready")
        picks_ready = sem("picks_ready")
        places_done = sem("places_done")
        count_ready = sem("count_ready")
        place_ready = sem("place_ready")
        gathered = sem("gathered")
        xg_hi_ready = sem("xg_hi_ready")
        xg_ready = sem("xg_ready")
        placeT_done = sem("placeT_done")
        placeT_ready = sem("placeT_ready")
        y_hi_ready = sem("y_hi_ready")
        y_ready = sem("y_ready")
        gate_ready = sem("gate_ready")
        scattered = sem("scattered")
        scatter_added = sem("scatter_added")
        g_silu_done = sem("g_silu_done")
        g_h_done = sem("g_h_done")
        g_hT_done = sem("g_hT_done")
        g_hT_hi_ready = sem("g_hT_hi_ready")
        g_hT_ready = sem("g_hT_ready")
        dve_chain = sem("dve_chain")
        out_ready = sem("out_ready")
        out_stored = sem("out_stored")

        block = ctx.enter_context(nc.Block())

        BATCH = [("dsa", 0), ("sel", 0), ("win", 0), ("dsa", 1), ("sel", 1), ("win", 1), ("cmp", 0), ("cmp", 1)]
        GROUP = [0, 2, 2, 1, 3, 3, 2, 3]
        NBATCH = len(BATCH)

        def opens(b):
            return GROUP[b] not in GROUP[:b]

        def closes(b):
            return GROUP[b] not in GROUP[b + 1:]

        def keys(b):
            kind, t = BATCH[b]
            return P * (t + 1) if kind != "cmp" else (NCMP - CMP_STRIDE // 2 if t == 0 else NCMP)

        def key_bias(b):
            kind, t = BATCH[b]
            heads = slice(0, AH) if kind == "dsa" else slice(AH, AH + BH)
            if kind == "cmp":
                first = P * (1 - t) + CMP_LEN - 1
                return bias_kT[:, heads, first:first + CMP_STRIDE * (keys(b) - 1) + 1:CMP_STRIDE]
            return bias_kT[:, heads, P * (1 - t):P * (1 - t) + keys(b)]

        def logit_tile(b, n):
            return work[:, b % 2, :].rearrange("p (h s) -> p h s", h=4)[:, :, 0:n]

        def prob_tile(b, n):
            return work[:, 2 + b % 2, :].rearrange("p (h s) -> p h s", h=4)[:, :, 0:n]

        def out_bank(layer, t, n):
            return 2 * t + n if layer == 0 else 6 - 2 * t + n

        def score_psum(first, n):
            return ps[:, first:first + 2, :].rearrange("p a (h s) -> p (a h) s", s=SEQ)[:, :, 0:n]

        STICK = [(1, 0), (1, 1), (0, 0), (0, 1)]
        NSTICK = len(STICK)

        def unit(ring, n):
            a, b = shape_of(n)
            return ring[:, n % (R if ring is raw else H), 0:a * b]

        def unit3(ring, n):
            a, b = shape_of(n)
            return unit(ring, n).rearrange("p (a b) -> p a b", a=a)

        GB = bounds(MOE_CHUNKS)
        NC = len(MOE_CHUNKS)

        def scatter_tile(i, e):
            return i // 2 if e is not None else 1 - i // 2

        def few(eng):
            eng.wait_ge(count_ready, 1)
            return eng.value_load(most_i[0:1, 0:1], min_val=0, max_val=SEQ) <= P

        @block.sync
        def _(sp):
            sp.dma_start(x[:], x_d[0].rearrange("(t p) d -> p t d", p=P)).then_inc(x_loaded, 16)
            for n, (pieces, a, b) in enumerate(units):
                if n >= R:
                    sp.wait_ge(lo_ready, n - R + 1)
                for src, d, cnt in pieces:
                    sp.dma_start(unit3(raw, n)[:, :, d:d + cnt], src).then_inc(raw_landed[n % R], 16)
            with sp.Fori(0, NE) as e:
                for i, (kind, c, q) in enumerate(moe_order):
                    n = U_MOE + i
                    sp.wait_ge(lo_ready, at(n - R + 1, e, PER))
                    if kind == "down":
                        src = moe_down[bass.ds(e, 1), c, :, 2 * q:2 * q + 2, :].rearrange("e p j n -> (e p) j n")
                    else:
                        view = moe_gate if kind == "gate" else moe_up
                        src = view[bass.ds(e, 1), :, 4 * q:4 * q + 4, W * c:W * c + W].rearrange(
                            "e p k f -> (e p) k f")
                    sp.dma_start(unit3(raw, n), src).then_inc(raw_landed[n % R], 16)
            for t in range(T):
                sp.wait_ge(out_ready, t + 1)
                sp.dma_start(out_d[0, P * t:P * t + P, :], work[:, t, :]).then_inc(out_stored, 16)
            sp.wait_ge(out_stored, 16 * T)

        gains = [ev_norm_mix[0], ev_norm_ffn[0], od_norm_mix[0], od_norm_ffn[0], final_norm]

        def row_to_all(row):
            return bass.AP(tensor=row.tensor, offset=row.offset, ap=[[0, P], [1, row.shape[0]]])

        @block.gpsimd
        def _(pool):
            pool.memset(ident[:], 0.0).then_inc(ident_ready, 1)
            pool.memset(flip[:], 0.0).then_inc(flip_ready, 1)
            pool.wait_ge(ident_ready, 1)
            pool.affine_select(out=ident[:], in_=ident[:], compare_op=ALU.not_equal, fill=1.0, base=0,
                               pattern=[[-1, P]], channel_multiplier=1).then_inc(ident_ready, 1)
            pool.wait_ge(flip_ready, 1)
            pool.affine_select(out=flip[:], in_=flip[:], compare_op=ALU.not_equal, fill=1.0, base=-(P - 1),
                               pattern=[[1, P]], channel_multiplier=1).then_inc(flip_ready, 1)
            pool.iota(iota[:], [[1, P]], base=0, channel_multiplier=0, allow_small_or_imprecise_dtypes=True)\
                .then_inc(iota_ready, 1)
            pool.memset(before[:], 1.0).then_inc(iota_ready, 1)
            pool.wait_ge(iota_ready, 2)
            pool.affine_select(out=before[:], in_=before[:], compare_op=ALU.is_gt, fill=0.0, base=0,
                               pattern=[[1, P]], channel_multiplier=-1).then_inc(iota_ready, 1)
            pool.wait_ge(diag_copied, 1)
            pool.dma_start(diag_d, diag_sb[:]).then_inc(diag_stored, 16)
            pool.wait_ge(diag_stored, 16)
            pool.dma_start(hankel, bass.AP(tensor=diag_d.tensor, offset=diag_d.offset,
                                           ap=[[1, P], [SEQ + P, CH], [1, SEQ]])).then_inc(hankel_loaded, 16)
            pool.wait_ge(bias_copied, 4)
            pool.affine_select(out=bias_kT[:], in_=bias_kT[:], compare_op=ALU.is_ge, fill=NEG, base=P,
                               pattern=[[0, 8], [-1, SEQ]], channel_multiplier=1).then_inc(bias_masked, 1)
            pool.wait_ge(gates_ready, 1)
            pool.affine_select(out=gates[:, 0, 0:BH], in_=gates[:, 0, 0:BH], compare_op=ALU.is_ge, fill=0.0,
                               base=-(CMP_LEN - 1), pattern=[[0, BH]], channel_multiplier=1)\
                .then_inc(gates_masked, 1)
            for i, t in enumerate((1, 0)):
                pool.wait_ge(idx_summed, i + 1)
                n = P * (t + 1)
                pool.affine_select(out=iscore[:, t, 0:n], in_=iscore[:, t, 0:n], compare_op=ALU.is_ge, fill=UNSEEN,
                                   base=P * t, pattern=[[-1, n]], channel_multiplier=1).then_inc(idx_masked, 1)
            pool.wait_ge(xs_ready, 2)
            pool.dma_start(gain[:, 0, :], row_to_all(gains[2])).then_inc(gain_loaded[2], 16)
            pool.wait_ge(xs_ready, 4)
            pool.dma_start(gain[:, 1, :], row_to_all(gains[3])).then_inc(gain_loaded[3], 16)
            pool.wait_ge(xs_ready, 6)
            pool.dma_start(gain[:, 0, :], row_to_all(gains[4])).then_inc(gain_loaded[4], 16)
            for b in range(NSTICK + 1):
                if b < NSTICK:
                    n = P * (STICK[b][0] + 1)
                    pool.wait_ge(rest_ready, b + 1)
                    lt = logit_tile(b, n)[:, :, n - P:n]
                    pool.affine_select(out=lt, in_=lt, compare_op=ALU.is_gt, fill=1.0, base=0,
                                       pattern=[[0, 4], [-1, P]], channel_multiplier=1).then_inc(rest_masked, 1)
                if b:
                    n = P * (STICK[b - 1][0] + 1)
                    pool.wait_ge(sticks_done, b)
                    pt = prob_tile(b - 1, n)[:, :, n - P:n]
                    pool.affine_select(out=pt, in_=pt, compare_op=ALU.is_gt, fill=0.0, base=0,
                                       pattern=[[0, 4], [-1, P]], channel_multiplier=1).then_inc(stick_masked, 1)

        @block.scalar
        def _(act):
            act.dma_start(gain[:, 0, :], row_to_all(gains[0])).then_inc(gain_loaded[0], 16)
            act.dma_start(rel_sb[:], rel_bias).then_inc(buckets_loaded, 16)
            act.dma_start(bucket_sb[:], buckets_d).then_inc(buckets_loaded, 16)

            done = [0]

            def split(n, e=None):
                act.wait_ge(raw_landed[n % R], at(landed(n), e, 16 * PER // R))
                if n >= H:
                    act.wait_ge(units_used, at(n - H + 1, e, PER))
                act.activation(unit(hi, n), unit(raw, n), ACT.Copy).then_inc(hi_ready, 1)

            def splits_to(n):
                while done[0] < n:
                    split(done[0])
                    done[0] += 1

            def norm_std(count, col=0, tile1=None):
                act.activation(root[:], root[:], ACT.Sqrt)
                if tile1 is not None:
                    for signal, value in tile1:
                        act.wait_ge(signal, value)
                    act.activation(work[:, 1, :], x[:, 1, :], ACT.Square, accum_out=stat[:, 1:2])\
                        .then_inc(squares_done, 1)
                act.wait_ge(var_ready, count)
                act.activation(stat[:, col + 2:col + 4], stat[:, col:col + 2], ACT.Sqrt).then_inc(std_ready, 1)

            def xT_high(i):
                for b in range(4):
                    act.wait_ge(xT_done, 4 * i + b + 1)
                    act.activation(xT_hi[:, 2 * b:2 * b + 2, :],
                                   ps[:, b, :].rearrange("p (k s) -> p k s", k=2), ACT.Copy)\
                        .then_inc(xT_hi_ready, 1)

            act.wait_ge(ones_ready, 1)
            norm_std(1, tile1=[(x_loaded, 16)])
            splits_to(1)
            xT_high(0)
            act.dma_start(pos_sb[:], ev_cmp_pos[0].rearrange("j l d -> l j d")).then_inc(small_loaded, 16)
            act.dma_start(wuk[:], ev_w_uk[0].rearrange("(p k) d -> p k d", k=2)).then_inc(small_loaded, 16)
            act.dma_start(wuv[:], ev_w_uv[0].rearrange("(p k) d -> p k d", k=2)).then_inc(small_loaded, 16)
            act.dma_start(w2[:], ev_cmp_w2[0].rearrange("j p d -> p j d")).then_inc(small_loaded, 16)
            act.dma_start(kv_gain[:], row_to_all(ev_kv_norm[0])).then_inc(small_loaded, 16)
            act.dma_start(wr[:], od_w_router[0].rearrange("(p k) e -> p k e", k=KD)).then_inc(small_loaded, 16)
            act.dma_start(gain[:, 1, :], row_to_all(gains[1])).then_inc(gain_loaded[1], 16)

            splits_to(2)
            act.wait_ge(diag_done, 1)
            act.activation(diag_sb[:], ps[0:CH, 7, 0:SEQ + P], ACT.Copy).then_inc(diag_copied, 1)
            splits_to(H)

            def projected(n, ahead=2):
                splits_to(n + ahead)
                act.wait_ge(units_used, n)

            projected(2)
            act.activation(iqT, score_psum(0, SEQ)[:, 0:2, :], ACT.Copy).then_inc(proj_copied, 1)
            act.activation(ikT, ps[:, 1, 0:SEQ], ACT.Copy).then_inc(proj_copied, 1)
            projected(4)
            act.activation(qT[:, 0:4, :], score_psum(2, SEQ), ACT.Copy).then_inc(proj_copied, 1)
            for a in range(4):
                act.wait_ge(bias_flipped, a + 1)
                act.activation(bias_kT[:, 2 * a:2 * a + 2, :], ps[:, 4 + a, :].rearrange("p (h s) -> p h s", h=2),
                               ACT.Copy).then_inc(bias_copied, 1)
            projected(6)
            act.activation(tok[:], ps[:, 4:6, :], ACT.Copy).then_inc(proj_copied, 1)
            for i, t in enumerate((1, 0)):
                n = P * (t + 1)
                act.wait_ge(idx_done, i + 1)
                if i:
                    act.wait_ge(idx_summed, i)
                act.activation(logit_tile(0, n), score_psum(6, n), ACT.Relu, scale=IDX_DIM ** -0.5)\
                    .then_inc(idx_relu, 1)
            act.wait_ge(small_copied, 1)
            act.activation(gates[:], small[:, :, 4:16], ACT.Sigmoid).then_inc(gates_ready, 1)
            norm_std(2, 4)
            projected(8)
            act.activation(qT[:, 4:8, :], score_psum(2, SEQ), ACT.Copy).then_inc(proj_copied, 1)
            act.wait_ge(latT_done, 1)
            act.activation(latT[:], ps[:, 4, :].rearrange("p (k s) -> p k s", k=2), ACT.Copy)\
                .then_inc(latT_copied, 1)
            projected(10, 1)
            act.activation(rawT, score_psum(0, SEQ)[:, 0:2, :], ACT.Copy).then_inc(proj_copied, 1)
            act.activation(kv[:, 4 * SEQ:6 * SEQ].rearrange("p (b s) -> p b s", b=2),
                           score_psum(0, SEQ)[:, 2:4, :], ACT.Copy).then_inc(proj_copied, 1)
            act.wait_ge(akv_done, 1)
            act.activation(akT, ps[:, 5, 0:SEQ], ACT.Copy).then_inc(akv_copied, 1)
            act.activation(av, ps[:, 5, SEQ:W].rearrange("p (t d) -> p t d", t=T), ACT.Copy).then_inc(akv_copied, 1)
            for j in range(2):
                act.wait_ge(blk_made, j + 1)
                act.activation(blk_part(0, j), work[:, 1, W * j:W * j + W], ACT.Copy).then_inc(blk_hi_ready, 1)
            splits_to(U_CMP + 3)

            def exps(b):
                act.wait_ge(logits_ready, b + 1)
                n = keys(b)
                for h in range(4):
                    ins = act.activation(prob_tile(b, n)[:, h, :], logit_tile(b, n)[:, h, :], ACT.Exp,
                                         bias=negmax[:, b % 2, h:h + 1], accum_out=expsum[:, b % 2, h:h + 1])
                ins.then_inc(exps_done, 1)

            def copy_probT(b, n, bank):
                act.wait_ge(probT_done, b + 1)
                if n < P:
                    act.activation(probT[0:n, 0], ps[0:n, bank, :].rearrange("p (h q) -> p h q", h=4),
                                   ACT.Copy).then_inc(probT_copied, 1)
                else:
                    act.activation(probT[:, 0:n // P], ps[:, bank:bank + n // P, :].rearrange("p t (h q) -> p t h q", h=4),
                                   ACT.Copy).then_inc(probT_copied, 1)

            def heads_hi(g, heads, t, bank):
                act.activation(xT_hi[:, heads, P * t:P * t + P], ps[:, bank, :].rearrange("p (h q) -> p h q", h=4),
                               ACT.Copy).then_inc(oT_hi_ready, 1)

            exps(0)
            exps(1)
            splits_to(U_CMP + 4)
            for b in range(NBATCH):
                copy_probT(b, keys(b), 4)
                if b == 3:
                    act.wait_ge(ckv_done, 1)
                    act.activation(ckT[:, 0:NCMP], ps[:, 7, 0:NCMP], ACT.Copy).then_inc(ckv_copied, 1)
                    act.activation(cv[0:NCMP, :], ps[0:NCMP, 7, HD:2 * HD], ACT.Copy).then_inc(ckv_copied, 1)
                if closes(b):
                    g = GROUP[b]
                    act.wait_ge(pv_done, b + 1)
                    heads_hi(g, slice(4 * (g // 2), 4 * (g // 2) + 4), g % 2, 6 + g % 2)
                if b + 2 < NBATCH:
                    exps(b + 2)
                if b == 1:
                    act.wait_ge(gelu_arg, 1)
                    act.activation(hid3, hid2, ACT.Exp, scale=-2.0 * (2.0 / np.pi) ** 0.5).then_inc(gelu_exp, 1)
                if b < 3:
                    splits_to(U_CMP + 5 + b)
                if b == 2:
                    act.wait_ge(hidT_done, 1)
                    act.activation(hidT[:], ps[:, 7, 2 * HD:2 * HD + 2 * NCP].rearrange("p (j n) -> p j n", j=2),
                                   ACT.Copy).then_inc(hidT_copied, 1)
            splits_to(U_FFN + H - 1)

            def ffn(chunks, first, e=None, cbase=0):
                pos, ends = [0], bounds(chunks)
                total = len(ffn_order(chunks))
                per_c = T * len(chunks)

                def to(n):
                    n = min(n, total)
                    if e is None:
                        splits_to(first + n)
                        return
                    while pos[0] < n:
                        split(first + pos[0], e)
                        pos[0] += 1

                def hT_high(c, t):
                    w = chunks[c][1]
                    act.wait_ge(hT_done, at(T * (cbase + c) + t + 1, e, per_c))
                    act.activation(hT_hi[:, 0:w // P, P * t:P * t + P],
                                   ps[:, 7, 0:w].rearrange("p (j q) -> p j q", q=P), ACT.Copy)\
                        .then_inc(hT_hi_ready, 1)

                for c, (g_end, u_end, d_end) in enumerate(ends):
                    w = chunks[c][1]
                    to(g_end + 2)
                    act.wait_ge(units_used, at(first + g_end, e, PER))
                    for t in range(T):
                        i = T * (cbase + c) + t
                        if i >= T or e is not None:
                            act.wait_ge(h_done, at(i - T + 1, e, per_c))
                        act.activation(work[:, 0, W * t:W * t + w], ps[:, 4 + (4 * c + t) % 3, 0:w], ACT.Silu)\
                            .then_inc(silu_done, 1)
                    if c:
                        hT_high(c - 1, 1)
                    to(d_end + 2)
                    hT_high(c, 0)
                hT_high(len(chunks) - 1, 1)
                to(total)

            norm_std(3, tile1=[(x_added, 1)])

            xT_high(1)
            ffn(FFN_CHUNKS, U_FFN)

            splits_to(U_QKV + H)
            norm_std(4, tile1=[(x_added, 2)])
            xT_high(2)
            def sigmoids(b):
                n = P * (STICK[b][0] + 1)
                act.wait_ge(z_done, b + 1)
                if b >= 2:
                    act.wait_ge(sticks_done, b - 1)
                zt = score_psum(4 + 2 * (b % 2), n)
                act.activation(logit_tile(b, n), zt, ACT.Sigmoid, scale=-1.0).then_inc(rest_ready, 1)
                act.activation(zt, zt, ACT.Sigmoid).then_inc(beta_ready, 1)

            act.activation(root[:], root[:], ACT.Sigmoid)
            for g in range(6):
                if g >= 4:
                    sigmoids(g - 4)
                splits_to(U_QKV + 2 * g + 4)
                act.wait_ge(units_used, U_QKV + 2 * g + 2)
                if g < 2:
                    act.activation(qT[:, 4 * g:4 * g + 4, :], score_psum(2 * g, SEQ), ACT.Copy, scale=SCALE)\
                        .then_inc(proj_copied, 1)
                elif g < 4:
                    act.activation(bias_kT[:, 4 * g - 8:4 * g - 4, :], score_psum(2 * g, SEQ), ACT.Copy)\
                        .then_inc(proj_copied, 1)
                else:
                    act.activation(v1[:, :, W * (g - 4):W * (g - 4) + W], ps[:, 2 * g - 8:2 * g - 6, :], ACT.Copy)\
                        .then_inc(proj_copied, 1)
            splits_to(U_WO[1] + H)

            for b in range(NSTICK):
                t, g = STICK[b]
                copy_probT(NBATCH + b, P * (t + 1), 0)
                if b + 2 < NSTICK:
                    sigmoids(b + 2)
                act.wait_ge(pv_done, NBATCH + b + 1)
                heads_hi(4 + b, slice(4 * g, 4 * g + 4), t, 2 + b % 2)
            splits_to(U_MOE)
            norm_std(5, tile1=[(x_added, 3)])
            act.activation(wr_hi[:, 0:KD * NE], wr[:].rearrange("p k e -> p (k e)"), ACT.Copy).then_inc(wr_hi_ready, 1)
            xT_high(3)
            act.activation(root[:], root[:], ACT.Exp)
            act.wait_ge(logitT_done, 1)
            act.activation(rlogT, ps[0:NE, 4, 0:SEQ], ACT.Copy).then_inc(logitT_copied, 1)
            for t in range(T):
                act.wait_ge(router_max, t + 1)
                act.activation(rexp[:, t], rlog[:, t, 0:NE], ACT.Exp, bias=rneg[:, t:t + 1]).then_inc(router_exp, 1)
                act.activation(xs_hi[:, t], work[:, t, :], ACT.Copy).then_inc(xs_hi_ready, 1)

            def gathered_high(e=None):
                for b in range(2):
                    act.wait_ge(gathered, at(b + 1 if e is None else b + 3, e, 2))
                    act.activation(xg_hi[:, 4 * b:4 * b + 4, :], ps[:, 2 + b, :].rearrange("p (k s) -> p k s", k=4),
                                   ACT.Copy).then_inc(xg_hi_ready, 1)

            def y_high(e=None):
                act.wait_ge(units_used, at(U_MOE if e is not None else U_MOE + NE * PER, e, PER))
                act.activation(y_hi, ps[:, 0:2, :].rearrange("p a n -> p (a n)"), ACT.Copy).then_inc(y_hi_ready, 1)

            fits = few(act)
            with act.If(fits):
                gathered_high()
                with act.Fori(0, NE) as e:
                    pos = [0]

                    def to(n):
                        while pos[0] < min(n, PER):
                            split(U_MOE + pos[0], e)
                            pos[0] += 1

                    to(3)
                    y_high(e)
                    for c, (g_end, u_end, d_end) in enumerate(GB):
                        to(g_end + 2)
                        act.wait_ge(units_used, at(U_MOE + g_end, e, PER))
                        if c:
                            act.wait_ge(g_h_done, at(c, e, NC))
                        act.activation(work[:, 0, 0:W], ps[:, 4 + 2 * c % 3, :], ACT.Silu).then_inc(g_silu_done, 1)
                        to(u_end + 2)
                        if c == 2:
                            act.wait_ge(placeT_done, at(1, e, 1))
                            act.activation(placeT[:], ps[:, 2, 0:SEQ], ACT.Copy).then_inc(placeT_ready, 1)
                        to(d_end + 2)
                        act.wait_ge(g_hT_done, at(c + 1, e, NC))
                        act.activation(hT_hi[:, :, 0:P], ps[:, 7, :].rearrange("p (j q) -> p j q", q=P), ACT.Copy)\
                            .then_inc(g_hT_hi_ready, 1)
                    to(PER)
                    gathered_high(e)
                y_high()
                act.wait_ge(scatter_added, 4 * NE + 2)
            with act.Else():
                with act.Fori(0, NE) as e:
                    ffn(MOE_CHUNKS, U_MOE, e, len(FFN_CHUNKS))
                act.wait_ge(y_added, NE + 1)
            norm_std(6, tile1=[])

        @block.vector
        def _(dve):
            chain = [0]

            def link(ins):
                chain[0] += 1
                ins.then_inc(dve_chain, 1)
                dve.wait_ge(dve_chain, chain[0])

            done = [0]

            def split(n, e=None):
                dve.wait_ge(hi_ready, at(n + 1, e, PER))
                dve.tensor_tensor(unit(lo, n), unit(raw, n), unit(hi, n).bitcast(F32), ALU.subtract)\
                    .then_inc(lo_ready, 1)

            def splits_to(n):
                while done[0] < n:
                    split(done[0])
                    done[0] += 1

            def rms(i, src, width, col, vcount):
                link(dve.tensor_tensor_reduce(work[:, 0, 0:width], src, src, 1.0, 0.0, ALU.mult, ALU.add,
                                              stat[:, col:col + 1]))
                dve.wait_ge(squares_done, i + 1)
                dve.tensor_scalar(stat[:, col:col + 2], stat[:, col:col + 2], 1.0 / width, EPS, ALU.mult, ALU.add)\
                    .then_inc(var_ready, 1)
                dve.wait_ge(std_ready, vcount)
                link(dve.reciprocal(stat[:, col + 2:col + 4], stat[:, col + 2:col + 4]))

            def norm(i, vcount):
                rms(i, x[:, 0, :], D, 0, vcount)
                dve.wait_ge(gain_loaded[i], 16)
                for t in range(T):
                    dve.scalar_tensor_tensor(out=work[:, t, :], in0=x[:, t, :], scalar=stat[:, 2 + t:3 + t],
                                             in1=gain[:, i % 2, :], op0=ALU.mult, op1=ALU.mult)\
                        .then_inc(xs_ready if i < 4 else out_ready, 1)

            def xT_low(i):
                for b in range(4):
                    dve.wait_ge(xT_hi_ready, 4 * i + b + 1)
                    dst = xT_lo[:, 2 * b:2 * b + 2, :]
                    dve.tensor_tensor(dst, ps[:, b, :].rearrange("p (k s) -> p k s", k=2),
                                      xT_hi[:, 2 * b:2 * b + 2, :].bitcast(F32), ALU.subtract).then_inc(xT_ready, 1)

            dve.memset(root[:], 1.0)
            for part in (wr_hi, wr_lo):
                dve.memset(part[:, KD * NE:].bitcast(F32), 0.0)
            dve.memset(blk[:, 4 * CMP_LEN * NCP:].bitcast(F32), 0.0)
            dve.memset(ones[:], 1.0).then_inc(ones_ready, 1)
            dve.wait_ge(x_loaded, 16)
            norm(0, 1)
            splits_to(1)
            xT_low(0)
            splits_to(4)
            dve.wait_ge(proj_copied, 2)
            link(dve.tensor_copy(small[:], ps[:, 1, SEQ:SEQ + 32].rearrange("p (t n) -> p t n", t=T)))
            dve.tensor_scalar(small[:, :, 0:4], small[:, :, 0:4], 0.5, None, ALU.mult).then_inc(small_copied, 1)
            dve.wait_ge(pos_done, 1)
            dve.tensor_copy(posT[:], ps[:, 6, 0:2 * CMP_LEN].rearrange("p (j l) -> p j l", j=2)).then_inc(pos_copied, 1)
            splits_to(8)
            dve.wait_ge(proj_copied, 4)
            dve.wait_ge(xT_done, 4)
            for t in range(T):
                link(dve.tensor_tensor_reduce(work[:, 1, RANK * t:RANK * t + RANK], tok[:, t, 0:RANK],
                                              tok[:, t, 0:RANK], 1.0, 0.0, ALU.mult, ALU.add, stat[:, 4 + t:5 + t]))
            dve.tensor_scalar(stat[:, 4:6], stat[:, 4:6], 1.0 / RANK, EPS, ALU.mult, ALU.add).then_inc(var_ready, 1)

            def index_sum(i, t):
                n = P * (t + 1)
                dve.wait_ge(idx_relu, i + 1)
                dve.wait_ge(small_copied, 1)
                sc, dst = logit_tile(0, n), iscore[:, t, 0:n]
                link(dve.tensor_scalar(dst, sc[:, 0, :], small[:, t, 0:1], None, ALU.mult))
                for h in range(1, 4):
                    ins = dve.scalar_tensor_tensor(out=dst, in0=sc[:, 2 * (h % 2) + h // 2, :],
                                                   scalar=small[:, t, h:h + 1], in1=dst, op0=ALU.mult, op1=ALU.add)
                    if h < 3:
                        link(ins)
                ins.then_inc(idx_summed, 1)

            def top_keys(i, t):
                n = P * (t + 1)
                dve.wait_ge(idx_masked, i + 1)
                src = iscore[:, t, 0:n]
                for r in range(TOPK // 8):
                    link(dve.max(top8[:], src))
                    link(dve.match_replace(topw[:, 0:n], top8[:], src, TAKEN))
                    src = topw[:, 0:n]
                link(dve.tensor_tensor(iscore[:, t, 0:n], topw[:, 0:n], iscore[:, t, 0:n], ALU.is_equal))

            index_sum(0, 1)
            index_sum(1, 0)
            dve.wait_ge(std_ready, 2)
            link(dve.reciprocal(stat[:, 6:8], stat[:, 6:8]))
            dve.wait_ge(small_loaded, 16 * 6)
            for t in range(T):
                dve.scalar_tensor_tensor(out=tok[:, t, 0:RANK], in0=tok[:, t, 0:RANK], scalar=stat[:, 6 + t:7 + t],
                                         in1=kv_gain[:], op0=ALU.mult, op1=ALU.mult).then_inc(lat_ready, 1)
            splits_to(10)
            dve.wait_ge(idx_done, 2)
            top_keys(0, 1)
            top_keys(1, 0)
            dve.wait_ge(pos_copied, 1)
            dve.wait_ge(proj_copied, 6)
            half = CMP_STRIDE
            for j in range(2):
                both = work[:, 1, W * j:W * j + W].rearrange("p (l n) -> p l n", n=NCP)
                src = rawT[:, j, :].rearrange("p (n l) -> p l n", l=half)
                dve.memset(both[:, :, NCMP:NCP], 0.0)
                for a in range(2):
                    ins = dve.tensor_tensor(both[:, half * a:half * a + half, 0:NCMP], src[:, :, a:a + NCMP],
                                            posT[:, j, half * a:half * a + half].unsqueeze(2)
                                            .broadcast_to([P, half, NCMP]), ALU.add)
                ins.then_inc(blk_made, 1)
            for j in range(2):
                dve.wait_ge(blk_hi_ready, j + 1)
                dve.tensor_tensor(blk_part(1, j), work[:, 1, W * j:W * j + W], blk_part(0, j).bitcast(F32),
                                  ALU.subtract).then_inc(blk_ready, 1)
            splits_to(U_CMP + 3)

            def gelu():
                dve.wait_ge(units_used, U_CMP + 4)
                link(dve.tensor_copy(hid[:], ps[0:NCP, 7, 0:2 * HD]))
                link(dve.tensor_tensor(hid2, hid[:], hid[:], ALU.mult))
                link(dve.tensor_scalar(hid2, hid2, 0.044715, 1.0, ALU.mult, ALU.add))
                dve.tensor_tensor(hid2, hid2, hid[:], ALU.mult).then_inc(gelu_arg, 1)
                dve.wait_ge(gelu_exp, 1)
                link(dve.tensor_scalar(hid3, hid3, 1.0, None, ALU.add))
                link(dve.reciprocal(hid3, hid3))
                dve.tensor_tensor(hid[:], hid[:], hid3, ALU.mult).then_inc(hid_ready, 1)

            def logits(b):
                kind, t = BATCH[b]
                n = keys(b)
                dve.wait_ge(scores_done, b + 1)
                lt = logit_tile(b, n)
                link(dve.scalar_tensor_tensor(out=lt, in0=score_psum(2 * (b % 2), n), scalar=SCALE, in1=key_bias(b),
                                              op0=ALU.mult, op1=ALU.add))
                if kind == "dsa":
                    out_of = iscore[:, t, 0:n].unsqueeze(1).broadcast_to([P, 4, n])
                    link(dve.scalar_tensor_tensor(out=lt, in0=out_of, scalar=NEG, in1=lt, op0=ALU.mult, op1=ALU.add))
                dve.tensor_reduce(negmax[:, b % 2, :], lt, AX.X, ALU.max, negate=True).then_inc(logits_ready, 1)

            def normalise(b):
                kind, t = BATCH[b]
                n = keys(b)
                dve.wait_ge(exps_done, b + 1)
                iv = inv[:, b % 2, :]
                link(dve.reciprocal(iv, expsum[:, b % 2, :]))
                if kind != "dsa":
                    br = ("cmp", "sel", "win").index(kind)
                    link(dve.tensor_tensor(iv, iv, gates[:, t, 4 * br:4 * br + 4], ALU.mult))
                pt = prob_tile(b, n)
                dve.tensor_tensor(pt, pt, iv.unsqueeze(2).broadcast_to([P, 4, n]), ALU.mult)\
                    .then_inc(probs_ready, 1)

            def heads_lo(i, heads, t, bank):
                dve.wait_ge(oT_hi_ready, i + 1)
                dve.tensor_tensor(xT_lo[:, heads, P * t:P * t + P], ps[:, bank, :].rearrange("p (h q) -> p h q", h=4),
                                  xT_hi[:, heads, P * t:P * t + P].bitcast(F32), ALU.subtract).then_inc(oT_ready, 1)

            dve.wait_ge(bias_masked, 1)
            dve.wait_ge(gates_masked, 1)
            logits(0)
            logits(1)
            normalise(0)
            splits_to(U_CMP + 4)
            for b in range(NBATCH):
                if b + 1 < NBATCH:
                    normalise(b + 1)
                if b + 2 < NBATCH:
                    logits(b + 2)
                g = GROUP[b]
                if closes(b):
                    heads_lo(g, slice(4 * (g // 2), 4 * (g // 2) + 4), g % 2, 6 + g % 2)
                if b == 1:
                    gelu()
                if b < 3:
                    splits_to(U_CMP + 5 + b)

            def add_out(layer):
                for n in range(2):
                    splits_to(min(U_WO[layer] + 2 * n + 4, U_MOE))
                    dve.wait_ge(units_used, U_WO[layer] + 2 * n + 2)
                    for t in (1, 0):
                        xs = x[:, t, W * n:W * n + W]
                        ins = dve.tensor_tensor(xs, xs, ps[:, out_bank(layer, t, n), :], ALU.add)
                        if (t, n) == (1, 1):
                            ins.then_inc(x_added, 1)
                        else:
                            link(ins)

            add_out(0)
            splits_to(U_FFN + H - 1)
            norm(1, 3)
            xT_low(1)

            def ffn(chunks, first, e=None, cbase=0):
                pos, ends = [0], bounds(chunks)
                total = len(ffn_order(chunks))
                per_c = T * len(chunks)

                def to(n):
                    n = min(n, total)
                    if e is None:
                        splits_to(first + n)
                        return
                    while pos[0] < n:
                        split(first + pos[0], e)
                        pos[0] += 1

                def hT_low(c, t):
                    w = chunks[c][1]
                    dve.wait_ge(hT_hi_ready, at(T * (cbase + c) + t + 1, e, per_c))
                    dve.tensor_tensor(hT_lo[:, 0:w // P, P * t:P * t + P],
                                      ps[:, 7, 0:w].rearrange("p (j q) -> p j q", q=P),
                                      hT_hi[:, 0:w // P, P * t:P * t + P].bitcast(F32), ALU.subtract)\
                        .then_inc(hT_ready, 1)

                for c, (g_end, u_end, d_end) in enumerate(ends):
                    w = chunks[c][1]
                    to(g_end + 2)
                    if c:
                        hT_low(c - 1, 1)
                    to(u_end + 1)
                    dve.wait_ge(units_used, at(first + u_end, e, PER))
                    for t in range(T):
                        i = T * (cbase + c) + t
                        dve.wait_ge(silu_done, at(i + 1, e, per_c))
                        if i >= T or e is not None:
                            dve.wait_ge(hT_done, at(i - T + 1, e, per_c))
                        dve.tensor_tensor(work[:, 1, W * t:W * t + w], work[:, 0, W * t:W * t + w],
                                          ps[:, 4 + (4 * c + 2 + t) % 3, 0:w], ALU.mult).then_inc(h_done, 1)
                    to(d_end + 2)
                    hT_low(c, 0)
                hT_low(len(chunks) - 1, 1)
                to(total)
                dve.wait_ge(units_used, at(first + total, e, PER))
                if e is not None:
                    dve.wait_ge(y_added, at(1, e, 1))
                for t in (1, 0):
                    for n in range(2):
                        xs = x[:, t, W * n:W * n + W]
                        if e is None:
                            ins = dve.tensor_tensor(xs, xs, ps[:, 2 * t + n, :], ALU.add)
                            if (t, n) == (1, 1):
                                ins.then_inc(x_added, 1)
                        else:
                            ins = dve.scalar_tensor_tensor(out=xs, in0=ps[:, 2 * t + n, :],
                                                           scalar=rgate[:, t, bass.ds(e, 1)], in1=xs,
                                                           op0=ALU.mult, op1=ALU.add)
                ins.then_inc(y_added, 1)

            ffn(FFN_CHUNKS, U_FFN)
            dve.wait_ge(y_added, 1)

            splits_to(U_QKV + H - 1)
            norm(2, 4)
            xT_low(2)

            def sticks(b):
                t, g = STICK[b]
                n = P * (t + 1)
                if b >= 2:
                    dve.wait_ge(probT_done, NBATCH + b - 1)
                lt, pt, beta = logit_tile(b, n), prob_tile(b, n), score_psum(4 + 2 * (b % 2), n)
                dve.memset(pt[:, :, n - 1:n], 1.0)
                dve.wait_ge(rest_masked, b + 1)
                for h in range(4):
                    ins = dve.tensor_tensor_scan(pt[:, h, 0:n - 1][:, ::-1], lt[:, h, 1:n][:, ::-1],
                                                 ones[:, 0:n - 1], 1.0, ALU.mult, ALU.mult)
                link(ins)
                dve.wait_ge(beta_ready, b + 1)
                dve.tensor_tensor(pt, beta, pt, ALU.mult).then_inc(sticks_done, 1)

            splits_to(U_QKV + 10)
            sticks(0)
            splits_to(U_QKV + 12)
            sticks(1)
            splits_to(U_WO[1] + H)
            for b in range(NSTICK):
                if b and b + 1 < NSTICK:
                    sticks(b + 1)
                t, g = STICK[b]
                heads_lo(4 + b, slice(4 * g, 4 * g + 4), t, 2 + b % 2)
            add_out(1)
            norm(3, 5)
            dve.wait_ge(wr_hi_ready, 1)
            dve.tensor_tensor(wr_lo[:, 0:KD * NE], wr[:].rearrange("p k e -> p (k e)"),
                              wr_hi[:, 0:KD * NE].bitcast(F32), ALU.subtract).then_inc(wr_ready, 1)
            xT_low(3)
            link(dve.memset(rlog[:], TAKEN))
            link(dve.memset(placeT[:].bitcast(F32), 0.0))
            dve.memset(gate_col[:], 0.0).then_inc(gate_ready, 1)
            link(dve.memset(rtop[:], TAKEN))
            link(dve.memset(rgate[:], 0.0))
            link(dve.memset(rpick[:], 0.0))
            link(dve.memset(rplace[:], 0.0))
            dve.wait_ge(logit_done, 1)
            for t in range(T):
                link(dve.tensor_copy(rlog[:, t, 0:NE], ps[:, 4, SEQ + NE * t:SEQ + NE * t + NE]))
                link(dve.max(top8[:], rlog[:, t]))
                link(dve.tensor_copy(rtop[:, t, 0:2], top8[:, 0:2]))
                dve.tensor_scalar(rneg[:, t:t + 1], top8[:, 0:1], -1.0, None, ALU.mult).then_inc(router_max, 1)
                link(dve.match_replace(rsel[:, t], rtop[:, t], rlog[:, t], UNSEEN))
                link(dve.tensor_tensor(rpick[:, t, 0:NE], rsel[:, t, 0:NE], rlog[:, t, 0:NE], ALU.not_equal))
                dve.wait_ge(router_exp, t + 1)
                gt = rgate[:, t, 0:NE]
                link(dve.tensor_tensor(gt, rexp[:, t], rpick[:, t, 0:NE], ALU.mult))
                link(dve.tensor_reduce(rsum[:, t:t + 1], gt, AX.X, ALU.add))
                link(dve.reciprocal(rsum[:, t:t + 1], rsum[:, t:t + 1]))
                dve.tensor_scalar(gt, gt, rsum[:, t:t + 1], None, ALU.mult).then_inc(picks_ready, 1)
            dve.wait_ge(xs_hi_ready, T)
            dve.tensor_tensor(xs_lo[:], work[:, 0:T, :], xs_hi[:].bitcast(F32), ALU.subtract).then_inc(xs_lo_ready, 1)
            dve.wait_ge(places_done, 1)
            link(dve.tensor_copy(rplace[:, :, 0:NE], ps[:, 4, 16:32].rearrange("p (t e) -> p t e", t=T)))
            link(dve.tensor_copy(rcount[:], ps[:, 4, 32:40]))
            link(dve.tensor_reduce(most[:], rcount[0:1, :], AX.X, ALU.max))
            dve.tensor_copy(most_i[:], most[:]).then_inc(count_ready, 1)

            def make_place(e=None):
                col = slice(0, 1) if e is None else bass.ds(e + 1, 1)
                for t in range(T):
                    ins = dve.tensor_scalar(place[:, t, :], iota[:], rplace[:, t, col], rpick[:, t, col],
                                            ALU.is_equal, ALU.mult)
                ins.then_inc(place_ready, 1)

            def gathered_low(e=None):
                for b in range(2):
                    dve.wait_ge(xg_hi_ready, at(b + 1 if e is None else b + 3, e, 2))
                    dst = slice(4 * b, 4 * b + 4)
                    dve.tensor_tensor(xg_lo[:, dst, :], ps[:, 2 + b, :].rearrange("p (k s) -> p k s", k=4),
                                      xg_hi[:, dst, :].bitcast(F32), ALU.subtract).then_inc(xg_ready, 1)

            def y_low(e=None):
                dve.wait_ge(y_hi_ready, at(1 if e is not None else NE + 1, e, 1))
                dve.tensor_tensor(y_lo, ps[:, 0:2, :].rearrange("p a n -> p (a n)"), y_hi.bitcast(F32), ALU.subtract)\
                    .then_inc(y_ready, 1)

            def add_scattered(i, e=None):
                first = 0 if e is not None else 4 * NE
                if i == 0:
                    dve.wait_ge(gate_ready, at(1 if e is not None else NE + 1, e, 1))
                    if e is None:
                        dve.wait_ge(scatter_added, first)
                dve.wait_ge(scattered, at(first + i + 1, e, 4))
                t = scatter_tile(i, e)
                xs = x[:, t, W * (i % 2):W * (i % 2) + W]
                dve.scalar_tensor_tensor(out=xs, in0=ps[:, 2 + i % 2, :], scalar=gate_col[:, t:t + 1],
                                         in1=xs, op0=ALU.mult, op1=ALU.add).then_inc(scatter_added, 1)

            fits = few(dve)
            dve.wait_ge(iota_ready, 3)
            with dve.If(fits):
                make_place()
                gathered_low()
                with dve.Fori(0, NE) as e:
                    pos = [0]

                    def to(n):
                        while pos[0] < min(n, PER):
                            split(U_MOE + pos[0], e)
                            pos[0] += 1

                    to(4)
                    y_low(e)
                    for c, (g_end, u_end, d_end) in enumerate(GB):
                        to(u_end + 1)
                        dve.wait_ge(units_used, at(U_MOE + u_end, e, PER))
                        dve.wait_ge(g_silu_done, at(c + 1, e, NC))
                        if c:
                            dve.wait_ge(g_hT_done, at(c, e, NC))
                        dve.tensor_tensor(work[:, 1, 0:W], work[:, 0, 0:W], ps[:, 4 + (2 * c + 1) % 3, :], ALU.mult)\
                            .then_inc(g_h_done, 1)
                        if c < 2:
                            add_scattered(2 * c, e)
                            add_scattered(2 * c + 1, e)
                        if c == 3:
                            dve.wait_ge(scatter_added, at(4, e, 4))
                            dve.tensor_copy(gate_col[:], rgate[:, :, bass.ds(e, 1)].rearrange("p t o -> p (t o)"))\
                                .then_inc(gate_ready, 1)
                        if c == 4:
                            dve.wait_ge(placeT_done, at(1, e, 1))
                            make_place(e)
                        to(d_end + 2)
                        dve.wait_ge(g_hT_hi_ready, at(c + 1, e, NC))
                        dve.tensor_tensor(hT_lo[:, :, 0:P], ps[:, 7, :].rearrange("p (j q) -> p j q", q=P),
                                          hT_hi[:, :, 0:P].bitcast(F32), ALU.subtract).then_inc(g_hT_ready, 1)
                    to(PER)
                    gathered_low(e)
                y_low()
                for i in range(4):
                    add_scattered(i)
                dve.wait_ge(scatter_added, 4 * NE + 4)
            with dve.Else():
                with dve.Fori(0, NE) as e:
                    ffn(MOE_CHUNKS, U_MOE, e, len(FFN_CHUNKS))
                dve.wait_ge(y_added, NE + 1)
            norm(4, 6)

        @block.tensor
        def _(pe):
            def take(n, e=None):
                pe.wait_ge(lo_ready, at(n + 1, e, PER))

            def three(out, s_hi, s_lo, m_hi, m_lo, start, stop):
                pe.matmul(out, s_hi, m_hi, start=start, stop=False, skip_group_check=True)
                pe.matmul(out, s_hi, m_lo, start=False, stop=False, skip_group_check=True)
                return pe.matmul(out, s_lo, m_hi, start=False, stop=stop, skip_group_check=True)

            def project_T(first, blocks, bank, extra=None, norm=None):
                for q in range(2):
                    n = first + q
                    take(n)
                    if norm is not None:
                        features(norm, q)
                    wh, wl = unit3(hi, n), unit3(lo, n)
                    for i in range(blocks):
                        out = ps[:, bank + i // 2, SEQ * (i % 2):SEQ * (i % 2) + SEQ]
                        cols = slice(P * i, P * i + P)
                        for k in range(4):
                            ins = three(out, wh[:, k, cols], wl[:, k, cols], xT_hi[:, 4 * q + k, :],
                                        xT_lo[:, 4 * q + k, :], q == 0 and k == 0 and i % 2 == 0, q == 1 and k == 3)
                    if extra:
                        c0, cn = extra
                        for t in range(T):
                            out = ps[:, bank + (blocks - 1) // 2, SEQ + cn * t:SEQ + cn * t + cn]
                            for k in range(4):
                                ts = slice(P * t, P * t + P)
                                ins = three(out, xT_hi[:, 4 * q + k, ts], xT_lo[:, 4 * q + k, ts],
                                            wh[:, k, c0:c0 + cn], wl[:, k, c0:c0 + cn], False, q == 1 and k == 3)
                    ins.then_inc(units_used, 1)

            def project(first, banks):
                for q in range(2):
                    n = first + q
                    take(n)
                    wh, wl = unit3(hi, n), unit3(lo, n)
                    for t in range(T):
                        ts = slice(P * t, P * t + P)
                        for k in range(4):
                            ins = three(ps[:, banks[t], :], xT_hi[:, 4 * q + k, ts], xT_lo[:, 4 * q + k, ts],
                                        wh[:, k, :], wl[:, k, :], q == 0 and k == 0, q == 1 and k == 3)
                    ins.then_inc(units_used, 1)

            def transpose_x(i):
                for t in range(T):
                    pe.wait_ge(xs_ready, 2 * i + t + 1)
                    for b in range(4):
                        for k in range(2):
                            o = k * SEQ + t * P
                            ins = pe.transpose(ps[:, b, o:o + P], work[:, t, 2 * b + k::KD], ident[:])
                        if t == T - 1:
                            ins.then_inc(xT_done, 1)

            def features(i, q):
                pe.wait_ge(xT_ready, 4 * i + 2 * q + 2)

            pe.wait_ge(ident_ready, 2)
            transpose_x(0)
            pe.wait_ge(buckets_loaded, 32)
            pe.matmul(ps[0:CH, 7, 0:SEQ + P], rel_sb[:], bucket_sb[:], start=True, stop=True).then_inc(diag_done, 1)
            project_T(0, 3, 0, (384, 16), norm=0)
            pe.wait_ge(small_loaded, 16 * 6)
            for j in range(2):
                ins = pe.transpose(ps[:, 6, CMP_LEN * j:CMP_LEN * j + CMP_LEN], pos_sb[:, j, :],
                                   ident[0:CMP_LEN, 0:CMP_LEN])
            ins.then_inc(pos_done, 1)
            project_T(2, 4, 2)
            pe.wait_ge(hankel_loaded, 16)
            pe.wait_ge(flip_ready, 2)
            pe.wait_ge(diag_copied, 1)
            pe.wait_ge(pos_copied, 1)
            for a in range(4):
                for h in range(2):
                    ins = pe.matmul(ps[:, 4 + a, SEQ * h:SEQ * h + SEQ], flip[:], hankel[:, 2 * a + h, :],
                                    start=True, stop=True)
                ins.then_inc(bias_flipped, 1)
            pe.wait_ge(bias_copied, 4)
            project(4, (4, 5))
            pe.wait_ge(proj_copied, 2)
            for i, t in enumerate((1, 0)):
                n = P * (t + 1)
                if i:
                    pe.wait_ge(idx_relu, i)
                for h in range(4):
                    p0 = IDX_DIM * (h % 2)
                    ins = pe.matmul(score_psum(6, n)[:, 2 * (h % 2) + h // 2, :],
                                    iqT[p0:p0 + IDX_DIM, h // 2, P * t:P * t + P], ikT[p0:p0 + IDX_DIM, 0:n],
                                    start=True, stop=True)
                ins.then_inc(idx_done, 1)
            pe.wait_ge(proj_copied, 3)
            project_T(6, 4, 2)
            pe.wait_ge(lat_ready, 2)
            for k in range(2):
                for t in range(T):
                    ins = pe.transpose(ps[:, 4, k * SEQ + t * P:k * SEQ + t * P + P], tok[:, t, k:RANK:2], ident[:])
            ins.then_inc(latT_done, 1)
            pe.wait_ge(small_copied, 1)
            project_T(8, 4, 0)
            pe.wait_ge(latT_copied, 1)
            pe.wait_ge(small_loaded, 16 * 6)
            for k in range(2):
                pe.matmul(ps[:, 5, 0:SEQ], wuk[:, k, :], latT[:, k, :], start=(k == 0), stop=(k == 1))
            for t in range(T):
                for k in range(2):
                    ins = pe.matmul(ps[:, 5, SEQ + HD * t:SEQ + HD * t + HD], latT[:, k, P * t:P * t + P], wuv[:, k, :],
                                    start=(k == 0), stop=(k == 1))
            ins.then_inc(akv_done, 1)
            pe.wait_ge(akv_copied, 2)
            pe.wait_ge(proj_copied, 7)

            def compress(i):
                if i == 0:
                    pe.wait_ge(blk_ready, 2)
                    pe.wait_ge(idx_relu, 2)
                j, q = i // 2, i % 2
                take(U_CMP + i)
                wh, wl = unit3(hi, U_CMP + i), unit3(lo, U_CMP + i)
                for l in range(16):
                    place = 16 * q + l
                    ins = three(ps[:, 7, HD * j:HD * j + HD], blk_window(0, j, place), blk_window(1, j, place),
                                wh[:, l, :], wl[:, l, :], i == 0 and l == 0, q == 1 and l == 15)
                ins.then_inc(units_used, 1)

            def transpose_hidden():
                pe.wait_ge(hid_ready, 1)
                for j in range(2):
                    first = 2 * HD + NCP * j
                    ins = pe.transpose(ps[:, 7, first:first + NCP], hid[:, HD * j:HD * j + HD], ident[0:NCP, 0:NCP])
                ins.then_inc(hidT_done, 1)

            def compressed():
                pe.wait_ge(hidT_copied, 1)
                pe.matmul(ps[:, 7, 0:NCMP], w2[:, 0, :], hidT[:, 0, 0:NCMP], start=True, stop=True)
                pe.matmul(ps[0:NCMP, 7, HD:2 * HD], hidT[:, 1, 0:NCMP], w2[:, 1, :], start=True, stop=True)\
                    .then_inc(ckv_done, 1)
                pe.wait_ge(ckv_copied, 2)

            def project_out(layer, u, t):
                n, q = u // 2, u % 2
                last = t == (0 if layer else 1)
                if u == 0:
                    pe.wait_ge(oT_ready, 4 * layer + (4 if last else 2 + (layer == 0)))
                take(U_WO[layer] + u)
                wh, wl = unit3(hi, U_WO[layer] + u), unit3(lo, U_WO[layer] + u)
                ts = slice(P * t, P * t + P)
                for k in range(4):
                    ins = three(ps[:, out_bank(layer, t, n), :], xT_hi[:, 4 * q + k, ts], xT_lo[:, 4 * q + k, ts],
                                wh[:, k, :], wl[:, k, :], q == 0 and k == 0, q == 1 and k == 3)
                if last:
                    ins.then_inc(units_used, 1)

            def scores(b):
                kind, t = BATCH[b]
                n = keys(b)
                if b >= 2:
                    pe.wait_ge(logits_ready, b - 1)
                kT = {"dsa": akT, "sel": skT, "win": wkT, "cmp": ckT}[kind]
                out = score_psum(2 * (b % 2), n)
                for h in range(4):
                    hq = h if kind == "dsa" else AH + h
                    ins = pe.matmul(out[:, h, :], qT[:, hq, P * t:P * t + P], kT[:, 0:n], start=True, stop=True)
                ins.then_inc(scores_done, 1)

            def transpose_probs(b, b_tile, n, bank):
                for c in range(max(n // P, 1)):
                    m = min(n, P)
                    for h in range(4):
                        ins = pe.transpose(ps[0:m, bank + c, P * h:P * h + P], prob_tile(b_tile, n)[:, h, P * c:P * c + m],
                                           ident[:])
                ins.then_inc(probT_done, 1)

            scores(0)
            scores(1)
            compress(0)
            compress(1)
            for b in range(NBATCH):
                kind, t = BATCH[b]
                n, g = keys(b), GROUP[b]
                pe.wait_ge(probs_ready, b + 1)
                transpose_probs(b, b, n, 4)
                if b + 2 < NBATCH:
                    scores(b + 2)
                first = opens(b)
                if b == 3:
                    compressed()
                if first and g >= 2:
                    pe.wait_ge(oT_ready, g - 1)
                if b == NBATCH - 1:
                    project_out(0, 0, 0)
                pe.wait_ge(probT_copied, b + 1)
                for c in range(max(n // P, 1)):
                    m = min(n, P)
                    val = {"dsa": av[:, c, :], "sel": tok[:, c, RANK:RANK + HD],
                           "win": tok[:, c, RANK + HD:W], "cmp": cv[0:min(m, NCMP), :]}[kind]
                    ins = pe.matmul(ps[:, 6 + g % 2, :], val, probT[0:m, c].rearrange("p h q -> p (h q)"),
                                    start=(first and c == 0), stop=closes(b), skip_group_check=True)
                ins.then_inc(pv_done, 1)
                if b < 2:
                    compress(b + 2)
                if b == 2:
                    transpose_hidden()

            project_out(0, 1, 0)
            project_out(0, 2, 0)
            for u in range(3):
                project_out(0, u, 1)
            for t in (0, 1):
                project_out(0, 3, t)
            transpose_x(1)

            def ffn(chunks, first, e=None, cbase=0):
                ends = bounds(chunks)
                cu = chunk_units(chunks)
                per_c = T * len(chunks)

                def bank_free(c, i):
                    gi = 4 * c + i - 3
                    if gi < 0:
                        return
                    pc, pi = gi // 4, gi % 4
                    pe.wait_ge(silu_done if pi < 2 else h_done, at(T * (cbase + pc) + pi % 2 + 1, e, per_c))

                def gate_or_up(c, base, i0, start_n):
                    w = chunks[c][1]
                    nk = UNIT // w
                    for q in range(cu[c][0]):
                        n = first + start_n + q
                        take(n, e)
                        if e is None and c == 0:
                            features(1, q if nk == 4 else 1)
                        wh, wl = unit3(hi, n), unit3(lo, n)
                        for t in range(T):
                            if q == 0:
                                bank_free(c, i0 + t)
                            out = ps[:, 4 + (4 * c + i0 + t) % 3, 0:w]
                            ts = slice(P * t, P * t + P)
                            for kk in range(nk):
                                k = nk * q + kk
                                ins = three(out, xT_hi[:, k, ts], xT_lo[:, k, ts], wh[:, kk, :], wl[:, kk, :],
                                            k == 0, k == KD - 1)
                        ins.then_inc(units_used, 1)

                def transpose_h(c, t):
                    w = chunks[c][1]
                    nj = w // P
                    i = T * (cbase + c) + t
                    pe.wait_ge(h_done, at(i + 1, e, per_c))
                    if i or e is not None:
                        pe.wait_ge(hT_ready, at(i, e, per_c))
                    for j in range(nj):
                        ins = pe.transpose(ps[:, 7, P * j:P * j + P], work[:, 1, W * t + j:W * t + w:nj], ident[:])
                    ins.then_inc(hT_done, 1)

                def down(c, start_n):
                    w = chunks[c][1]
                    pe.wait_ge(hT_ready, at(T * (cbase + c) + T, e, per_c))
                    for q in range(cu[c][1]):
                        n = first + start_n + q
                        take(n, e)
                        wh, wl = unit3(hi, n), unit3(lo, n)
                        for jj in range(2):
                            j = 2 * q + jj
                            for t in range(T):
                                ts = slice(P * t, P * t + P)
                                for m in range(2):
                                    cols = slice(W * m, W * m + W)
                                    ins = three(ps[:, 2 * t + m, :], hT_hi[:, j, ts], hT_lo[:, j, ts],
                                                wh[:, jj, cols], wl[:, jj, cols], c == 0 and j == 0,
                                                c == len(chunks) - 1 and j == w // P - 1)
                        ins.then_inc(units_used, 1)

                for c, (g_end, u_end, d_end) in enumerate(ends):
                    gate_or_up(c, 0, 0, g_end - cu[c][0])
                    if c:
                        transpose_h(c - 1, 1)
                    gate_or_up(c, 0, 2, g_end)
                    if c:
                        if c == 1 and e is not None:
                            pe.wait_ge(y_added, at(1, e, 1))
                        down(c - 1, u_end)
                    transpose_h(c, 0)
                transpose_h(len(chunks) - 1, 1)
                down(len(chunks) - 1, ends[-1][2])

            ffn(FFN_CHUNKS, U_FFN)
            transpose_x(2)
            for g in range(4):
                project_T(U_QKV + 2 * g, 4, 2 * g, norm=2 if g == 0 else None)

            def stick_scores(b):
                t, g = STICK[b]
                n = P * (t + 1)
                if b == 0:
                    pe.wait_ge(proj_copied, 11)
                if b >= 2:
                    pe.wait_ge(sticks_done, b - 1)
                out = score_psum(4 + 2 * (b % 2), n)
                for h in range(4):
                    hd = 4 * g + h
                    ins = pe.matmul(out[:, h, :], qT[:, hd, P * t:P * t + P], bias_kT[:, hd, 0:n], start=True, stop=True)
                ins.then_inc(z_done, 1)

            stick_scores(0)
            stick_scores(1)
            project(U_QKV + 8, (0, 1))
            project(U_QKV + 10, (2, 3))
            for b in range(NSTICK):
                t, g = STICK[b]
                n = P * (t + 1)
                if b == 0:
                    pe.wait_ge(proj_copied, 13)
                pe.wait_ge(stick_masked, b + 1)
                for c in range(n // P):
                    for h in range(4):
                        ins = pe.transpose(ps[:, c, P * h:P * h + P], prob_tile(b, n)[:, h, P * c:P * c + P], ident[:])
                ins.then_inc(probT_done, 1)
                if b + 2 < NSTICK:
                    stick_scores(b + 2)
                if b >= 2:
                    pe.wait_ge(oT_ready, 4 + b - 1)
                if b == 2:
                    project_out(1, 0, 1)
                if b == 3:
                    project_out(1, 1, 1)
                pe.wait_ge(probT_copied, NBATCH + b + 1)
                for h in range(4):
                    hd = 4 * g + h
                    for c in range(n // P):
                        ins = pe.matmul(ps[:, 2 + b % 2, P * h:P * h + P], v1[:, c, HD * hd:HD * hd + HD],
                                        probT[:, c, h, :], start=(h == 0 and c == 0), stop=(h == 3),
                                        skip_group_check=True)
                ins.then_inc(pv_done, 1)
            project_out(1, 2, 1)
            for u in range(3):
                project_out(1, u, 0)
            for t in (1, 0):
                project_out(1, 3, t)
            transpose_x(3)
            pe.wait_ge(wr_ready, 1)
            for k in range(KD):
                if k % 4 == 0:
                    features(3, k // 4)
                window = slice(NE * k, NE * k + P)
                ins = three(ps[:, 4, 0:SEQ], wr_hi[:, window], wr_lo[:, window], xT_hi[:, k, :], xT_lo[:, k, :],
                            k == 0, k == KD - 1)
            ins.then_inc(logitT_done, 1)
            pe.wait_ge(logitT_copied, 1)
            for t in range(T):
                first = SEQ + NE * t
                ins = pe.transpose(ps[:, 4, first:first + NE], rlogT[:, P * t:P * t + P], ident[0:NE, 0:NE])
            ins.then_inc(logit_done, 1)
            pe.wait_ge(picks_ready, 2)
            pe.wait_ge(iota_ready, 3)
            pk = [rpick[:, t, 0:NE] for t in range(T)]
            pe.matmul(ps[:, 4, 16:24], before[:], pk[0], start=True, stop=True)
            pe.matmul(ps[:, 4, 24:32], before[:], pk[1], start=True, stop=False)
            pe.matmul(ps[:, 4, 24:32], ones[:, 0:P], pk[0], start=False, stop=True)
            pe.matmul(ps[:, 4, 32:40], ones[:, 0:P], pk[0], start=True, stop=False)
            pe.matmul(ps[:, 4, 32:40], ones[:, 0:P], pk[1], start=False, stop=True).then_inc(places_done, 1)

            def gather(e=None):
                pe.wait_ge(place_ready, at(1 if e is None else 2, e, 1))
                if e is None:
                    pe.wait_ge(xs_lo_ready, 1)
                else:
                    pe.wait_ge(placeT_ready, at(1, e, 1))
                for k in range(KD):
                    out = ps[:, 2 + k // 4, P * (k % 4):P * (k % 4) + P]
                    for t in range(T):
                        for part in (xs_hi, xs_lo):
                            ins = pe.matmul(out, part[:, t, k::KD], place[:, t, :], start=(t == 0 and part is xs_hi),
                                            stop=(t == T - 1 and part is xs_lo))
                    if k % 4 == 3:
                        ins.then_inc(gathered, 1)

            def scatter(i, e=None):
                first = 0 if e is not None else 4 * NE
                if i == 0:
                    pe.wait_ge(y_ready, at(1 if e is not None else NE + 1, e, 1))
                    pe.wait_ge(gate_ready, at(1 if e is not None else NE + 1, e, 1))
                if i >= 2:
                    pe.wait_ge(scatter_added, at(first + i - 1, e, 4))
                cols = slice(W * (i % 2), W * (i % 2) + W)
                t = scatter_tile(i, e)
                to_tok = placeT[:, P * t:P * t + P]
                pe.matmul(ps[:, 2 + i % 2, :], to_tok, y_hi[:, cols], start=True, stop=False)
                pe.matmul(ps[:, 2 + i % 2, :], to_tok, y_lo[:, cols], start=False, stop=True).then_inc(scattered, 1)

            fits = few(pe)
            with pe.If(fits):
                gather()
                with pe.Fori(0, NE) as e:
                    def columns(c, base, which):
                        gi = 2 * c + which
                        if gi >= 3:
                            pc, pw = (gi - 3) // 2, (gi - 3) % 2
                            pe.wait_ge(g_h_done if pw else g_silu_done, at(pc + 1, e, NC))
                        for q in range(2):
                            n = U_MOE + base + q
                            take(n, e)
                            wh, wl = unit3(hi, n), unit3(lo, n)
                            for kk in range(4):
                                k = 4 * q + kk
                                ins = three(ps[:, 4 + gi % 3, :], xg_hi[:, k, :], xg_lo[:, k, :], wh[:, kk, :],
                                            wl[:, kk, :], k == 0, k == KD - 1)
                            ins.then_inc(units_used, 1)

                    def rows(c, base):
                        pe.wait_ge(g_hT_ready, at(c + 1, e, NC))
                        for q in range(2):
                            n = U_MOE + base + q
                            take(n, e)
                            wh, wl = unit3(hi, n), unit3(lo, n)
                            for jj in range(2):
                                j = 2 * q + jj
                                for m in range(2):
                                    cols = slice(W * m, W * m + W)
                                    ins = three(ps[:, m, :], hT_hi[:, j, 0:P], hT_lo[:, j, 0:P], wh[:, jj, cols],
                                                wl[:, jj, cols], c == 0 and j == 0, c == NC - 1 and j == 3)
                            ins.then_inc(units_used, 1)

                    pe.wait_ge(xg_ready, at(2, e, 2))
                    for c, (g_end, u_end, d_end) in enumerate(GB):
                        columns(c, g_end - 2, 0)
                        columns(c, g_end, 1)
                        if c < 2:
                            scatter(2 * c, e)
                            scatter(2 * c + 1, e)
                        if c == 2:
                            pe.wait_ge(scatter_added, at(3, e, 4))
                            for t in range(T):
                                ins = pe.transpose(ps[:, 2, P * t:P * t + P], place[:, t, :].bitcast(F32), ident[:])
                            ins.then_inc(placeT_done, 1)
                        if c:
                            rows(c - 1, u_end)
                        pe.wait_ge(g_h_done, at(c + 1, e, NC))
                        for j in range(4):
                            ins = pe.transpose(ps[:, 7, P * j:P * j + P], work[:, 1, j:W:4], ident[:])
                        ins.then_inc(g_hT_done, 1)
                    gather(e)
                    rows(NC - 1, GB[-1][2])
                for i in range(4):
                    scatter(i)
            with pe.Else():
                with pe.Fori(0, NE) as e:
                    ffn(MOE_CHUNKS, U_MOE, e, len(FFN_CHUNKS))


_INS = ['x', 'rel_bias', 'ev_norm_mix', 'ev_w_in', 'ev_kv_norm', 'ev_w_uk', 'ev_w_uv', 'ev_cmp_pos', 'ev_cmp_w1',
        'ev_cmp_w2', 'ev_w_out', 'ev_norm_ffn', 'ev_w_gate', 'ev_w_up', 'ev_w_down', 'od_norm_mix', 'od_w_qkv',
        'od_w_out', 'od_norm_ffn', 'od_w_router', 'od_w_gate', 'od_w_up', 'od_w_down', 'final_norm']


def kernel(**inputs):
    import numpy as _np
    import concourse.bacc as _bacc
    from concourse import mybir as _mybir
    from concourse.bass_utils import run_bass_kernel_spmd as _run

    nc = _bacc.Bacc("TRN2", target_bir_lowering=False, num_devices=1)
    arrays, args = {}, []
    for name in _INS:
        a = _np.ascontiguousarray(inputs[name])
        arrays[f"in_{name}_dram"] = a
        args.append(nc.dram_tensor(f"in_{name}_dram", a.shape, _mybir.dt.from_np(a.dtype), kind="ExternalInput").ap())
    out = nc.dram_tensor("out_0_dram", (1, SEQ, D), _mybir.dt.from_np(_np.dtype("float32")), kind="ExternalOutput").ap()
    build(nc, *args, out)
    r = _run(nc, [arrays], core_ids=[0])
    return r.results[0]["out_0_dram"]
```
